# Optimizing a Trainium2 kernel written in Bass

```python
import math
import jax, jax.numpy as jnp
from jax import lax
import numpy as np

D_MODEL = 1024
BATCH = 1
SEQ = 256
DEPTH = 2

N_A_LAYERS = DEPTH // 2
N_B_LAYERS = DEPTH - N_A_LAYERS
CONV_WIDTH = 31
FOX_HEADS = 16
FOX_HEAD_DIM = D_MODEL // FOX_HEADS
MEM_LEN = 256
MEM_HEADS = 4
MEM_HEAD_DIM = D_MODEL // MEM_HEADS
D_FF = 4 * D_MODEL
Q_BLOCK = 128
RMS_EPS = 1e-6
LN_EPS = 1e-5


def rmsnorm(x, g):
    xf = x.astype(jnp.float32)
    y = xf * lax.rsqrt(jnp.mean(xf * xf, axis=-1, keepdims=True) + RMS_EPS)
    return (y * g.astype(jnp.float32)).astype(x.dtype)

def layernorm(x, g, b):
    xf = x.astype(jnp.float32)
    mu = jnp.mean(xf, axis=-1, keepdims=True)
    var = jnp.mean(jnp.square(xf - mu), axis=-1, keepdims=True)
    y = (xf - mu) * lax.rsqrt(var + LN_EPS)
    return (y * g.astype(jnp.float32) + b.astype(jnp.float32)).astype(x.dtype)

def conformer_conv(h, w_pw1, b_pw1, w_dw, b_dw, ln_g, ln_b, w_pw2, b_pw2):
    u = h @ w_pw1 + b_pw1
    a, gate = jnp.split(u, 2, axis=-1)
    u = a * jax.nn.sigmoid(gate)
    u = lax.conv_general_dilated(
        u, w_dw[:, None, :].astype(u.dtype),
        window_strides=(1,), padding=[(CONV_WIDTH - 1, 0)],
        dimension_numbers=("NWC", "WIO", "NWC"),
        feature_group_count=D_MODEL) + b_dw
    u = jax.nn.silu(layernorm(u, ln_g, ln_b))
    return u @ w_pw2 + b_pw2

def fox_attention(h, w_q, w_o, k, v, c_bhs):
    B, S, _ = h.shape
    nb = S // Q_BLOCK
    q = (h @ w_q).reshape(B, nb, Q_BLOCK, FOX_HEADS, FOX_HEAD_DIM).transpose(1, 0, 2, 3, 4)
    c_q = c_bhs.reshape(B, FOX_HEADS, nb, Q_BLOCK).transpose(2, 0, 1, 3)
    key_pos = jnp.arange(S)
    scale = 1.0 / math.sqrt(FOX_HEAD_DIM)

    def block(args):
        qi, ci, i = args
        s = jnp.einsum("bqhd,bkhd->bhqk", qi, k).astype(jnp.float32) * scale
        s = s + (ci[..., :, None] - c_bhs[:, :, None, :])
        q_pos = i * Q_BLOCK + jnp.arange(Q_BLOCK)
        mask = key_pos[None, :] <= q_pos[:, None]
        s = jnp.where(mask[None, None], s, -jnp.inf)
        p = jax.nn.softmax(s, axis=-1)
        return jnp.einsum("bhqk,bkhd->bqhd", p.astype(v.dtype), v)

    out = lax.map(block, (q, c_q, jnp.arange(nb)))
    out = out.transpose(1, 0, 2, 3, 4).reshape(B, S, D_MODEL)
    return out @ w_o

def memory_cross_attention(h, mem_n, w_q, w_k, w_v, w_o):
    B, S, _ = h.shape
    q = (h @ w_q).reshape(B, S, MEM_HEADS, MEM_HEAD_DIM)
    k = (mem_n @ w_k).reshape(B, MEM_LEN, MEM_HEADS, MEM_HEAD_DIM)
    v = (mem_n @ w_v).reshape(B, MEM_LEN, MEM_HEADS, MEM_HEAD_DIM)
    s = jnp.einsum("bshd,bmhd->bhsm", q, k).astype(jnp.float32) / math.sqrt(MEM_HEAD_DIM)
    p = jax.nn.softmax(s, axis=-1)
    o = jnp.einsum("bhsm,bmhd->bshd", p.astype(v.dtype), v).reshape(B, S, D_MODEL)
    return o @ w_o

def sqrelu_mlp(h, w1, w2):
    return jnp.square(jax.nn.relu(h @ w1)) @ w2

def first_inputs(seed: int = 0) -> dict:
    key = jax.random.key(seed)
    ks = iter(jax.random.split(key, 40))

    def nrm(shape, scale):
        return jax.random.normal(next(ks), shape, jnp.float32) * scale

    def gain(shape):
        return 1.0 + nrm(shape, 0.05)

    D = D_MODEL
    return {
        "x": nrm((BATCH, SEQ, D), 1.0),
        "mem": nrm((BATCH, MEM_LEN, D), 1.0),
        "norm_mix_g": gain((DEPTH, D)),
        "norm_mem_g": gain((DEPTH, D)),
        "norm_memsrc_g": gain((DEPTH, D)),
        "norm_ff_g": gain((DEPTH, D)),
        "mem_wq": nrm((DEPTH, D, D), D ** -0.5),
        "mem_wk": nrm((DEPTH, D, D), D ** -0.5),
        "mem_wv": nrm((DEPTH, D, D), D ** -0.5),
        "mem_wo": nrm((DEPTH, D, D), 0.5 * D ** -0.5),
        "ff_w1": nrm((DEPTH, D, D_FF), D ** -0.5),
        "ff_w2": nrm((DEPTH, D_FF, D), 0.5 * D_FF ** -0.5),
        "conv_pw1_w": nrm((N_A_LAYERS, D, 2 * D), D ** -0.5),
        "conv_pw1_b": nrm((N_A_LAYERS, 2 * D), 0.02),
        "conv_dw_w": nrm((N_A_LAYERS, CONV_WIDTH, D), CONV_WIDTH ** -0.5),
        "conv_dw_b": nrm((N_A_LAYERS, D), 0.02),
        "conv_ln_g": gain((N_A_LAYERS, D)),
        "conv_ln_b": nrm((N_A_LAYERS, D), 0.02),
        "conv_pw2_w": nrm((N_A_LAYERS, D, D), 0.5 * D ** -0.5),
        "conv_pw2_b": nrm((N_A_LAYERS, D), 0.02),
        "kv_norm_g": gain((D,)),
        "kvf_w": nrm((D, 2 * D + FOX_HEADS), D ** -0.5),
        "fgate_b": 3.0 + nrm((FOX_HEADS,), 0.5),
        "fox_wq": nrm((N_B_LAYERS, D, D), D ** -0.5),
        "fox_wo": nrm((N_B_LAYERS, D, D), 0.5 * D ** -0.5),
        "final_norm_g": gain((D,)),
    }

def first_block(x, mem, norm_mix_g, norm_mem_g, norm_memsrc_g, norm_ff_g,
              mem_wq, mem_wk, mem_wv, mem_wo, ff_w1, ff_w2,
              conv_pw1_w, conv_pw1_b, conv_dw_w, conv_dw_b, conv_ln_g, conv_ln_b,
              conv_pw2_w, conv_pw2_b,
              kv_norm_g, kvf_w, fgate_b, fox_wq, fox_wo, final_norm_g):
    B, S, D = x.shape
    k = v = c_bhs = None
    for l in range(DEPTH):
        if l == N_A_LAYERS:
            hk = rmsnorm(x, kv_norm_g)
            kvf = hk @ kvf_w
            k = kvf[..., :D].reshape(B, S, FOX_HEADS, FOX_HEAD_DIM)
            v = kvf[..., D:2 * D].reshape(B, S, FOX_HEADS, FOX_HEAD_DIM)
            log_f = jax.nn.log_sigmoid((kvf[..., 2 * D:] + fgate_b).astype(jnp.float32))
            c_bhs = jnp.cumsum(log_f, axis=1).transpose(0, 2, 1)
        h = rmsnorm(x, norm_mix_g[l])
        if l < N_A_LAYERS:
            a = l
            x = x + conformer_conv(h, conv_pw1_w[a], conv_pw1_b[a], conv_dw_w[a], conv_dw_b[a],
                                   conv_ln_g[a], conv_ln_b[a], conv_pw2_w[a], conv_pw2_b[a])
        else:
            bl = l - N_A_LAYERS
            x = x + fox_attention(h, fox_wq[bl], fox_wo[bl], k, v, c_bhs)
        h = rmsnorm(x, norm_mem_g[l])
        mem_n = rmsnorm(mem, norm_memsrc_g[l])
        x = x + memory_cross_attention(h, mem_n, mem_wq[l], mem_wk[l], mem_wv[l], mem_wo[l])
        h = rmsnorm(x, norm_ff_g[l])
        x = x + sqrelu_mlp(h, ff_w1[l], ff_w2[l])
    return rmsnorm(x, final_norm_g)


DEPTH_2 = 1

GLA_HEADS = 4
GLA_DK = D_MODEL // 16
GLA_DV = D_MODEL // 8
GLA_LOWRANK = 16
GLA_TAU = 16.0
GLA_CHUNK = 64
MOBA_HEADS = 4
MOBA_DH = 128
MOBA_BLOCK = 256
MOBA_TOPK = 3
MOBA_QCHUNK = 32
NUM_BUCKETS = 32
MAX_DISTANCE = 128
MAX_EXACT = NUM_BUCKETS // 2
D_FF_2 = 2816
FFN_RES = 0.5
EPS = 1e-6
N_MOD = 9
GLA_QK_W = GLA_HEADS * GLA_DK
GLA_V_W = GLA_HEADS * GLA_DV
MOBA_W = MOBA_HEADS * MOBA_DH
IN_SIZES = (GLA_QK_W, GLA_QK_W, GLA_V_W, GLA_LOWRANK, GLA_V_W, MOBA_W, MOBA_W, MOBA_W, D_MODEL, D_MODEL)
IN_WIDTH = sum(IN_SIZES)


def rmsnorm_2(x, g):
    xf = x.astype(jnp.float32)
    y = xf * lax.rsqrt(jnp.mean(xf * xf, axis=-1, keepdims=True) + EPS) * g.astype(jnp.float32)
    return y.astype(x.dtype)

def modulate(x, shift, scale):
    return x * (1.0 + scale[:, None, :]) + shift[:, None, :]

def swiglu(x, w_gate, w_up, w_down):
    return (jax.nn.silu(x @ w_gate) * (x @ w_up)) @ w_down

def rel_bucket(dist):
    n = jnp.maximum(dist, 0)
    nf = jnp.maximum(n, 1).astype(jnp.float32)
    large = MAX_EXACT + (jnp.log(nf / MAX_EXACT) / math.log(MAX_DISTANCE / MAX_EXACT)
                         * (NUM_BUCKETS - MAX_EXACT)).astype(jnp.int32)
    large = jnp.minimum(large, NUM_BUCKETS - 1)
    return jnp.where(n < MAX_EXACT, n, large)

def gla_chunked(q, k, v, log_a):
    B, H, S, dk = q.shape
    dv = v.shape[-1]
    nc = S // GLA_CHUNK

    def to_chunks(t):
        return jnp.moveaxis(t.astype(jnp.float32).reshape(B, H, nc, GLA_CHUNK, t.shape[-1]), 2, 0)

    causal = jnp.tril(jnp.ones((GLA_CHUNK, GLA_CHUNK), dtype=bool))

    def step(state, inp):
        qc, kc, vc, gc = inp
        b = jnp.cumsum(gc, axis=2)
        o_inter = jnp.einsum('bhcd,bhde->bhce', qc * jnp.exp(b), state)
        diff = b[:, :, :, None, :] - b[:, :, None, :, :]
        decay = jnp.exp(jnp.where(causal[:, :, None], diff, -jnp.inf))
        attn = jnp.einsum('bhid,bhijd,bhjd->bhij', qc, decay, kc)
        o = o_inter + jnp.einsum('bhij,bhje->bhie', attn, vc)
        b_last = b[:, :, -1:, :]
        state = (jnp.exp(b_last[:, :, 0, :])[..., None] * state
                 + jnp.einsum('bhcd,bhce->bhde', kc * jnp.exp(b_last - b), vc))
        return state, o

    state0 = jnp.zeros((B, H, dk, dv), jnp.float32)
    _, o = lax.scan(step, state0, (to_chunks(q), to_chunks(k), to_chunks(v), to_chunks(log_a)))
    return jnp.moveaxis(o, 0, 2).reshape(B, H, S, dv)

def moba_attention(q, k, v, rel_bias):
    B, H, S, dh = q.shape
    nb = -(-S // MOBA_BLOCK)
    s_pad = nb * MOBA_BLOCK
    pad = ((0, 0), (0, 0), (0, s_pad - S), (0, 0))
    q = q.astype(jnp.float32)
    k = jnp.pad(k.astype(jnp.float32), pad)
    v = jnp.pad(v.astype(jnp.float32), pad)
    k_blocks = k.reshape(B, H, nb, MOBA_BLOCK, dh)
    v_blocks = v.reshape(B, H, nb, MOBA_BLOCK, dh)
    k_mean = jnp.mean(k_blocks, axis=3)
    topk = min(MOBA_TOPK, nb)
    scale = dh ** -0.5
    head_ix = jnp.arange(H)[None, :, None, None, None]
    gather = jax.vmap(jax.vmap(lambda blocks, ix: blocks[ix]))

    def chunk(ci):
        start = ci * MOBA_QCHUNK
        q_c = lax.dynamic_slice_in_dim(q, start, MOBA_QCHUNK, axis=2)
        q_pos = start + jnp.arange(MOBA_QCHUNK)
        cur = start // MOBA_BLOCK
        gate = jnp.einsum('bhqd,bhnd->bhqn', q_c, k_mean)
        gate = jnp.where(jnp.arange(nb) < cur, gate, -jnp.inf)
        _, sel = lax.top_k(gate, topk)
        sel_valid = jnp.arange(topk) < cur
        k_sel = gather(k_blocks, sel)
        v_sel = gather(v_blocks, sel)
        sel_pos = sel[..., None] * MOBA_BLOCK + jnp.arange(MOBA_BLOCK)
        sel_bias = rel_bias[head_ix, rel_bucket(q_pos[:, None, None] - sel_pos)]
        s_sel = jnp.einsum('bhqd,bhqrkd->bhqrk', q_c, k_sel) * scale + sel_bias
        s_sel = jnp.where(sel_valid[:, None], s_sel, -jnp.inf)
        own_start = cur * MOBA_BLOCK
        k_own = lax.dynamic_slice_in_dim(k, own_start, MOBA_BLOCK, axis=2)
        v_own = lax.dynamic_slice_in_dim(v, own_start, MOBA_BLOCK, axis=2)
        rel = q_pos[:, None] - (own_start + jnp.arange(MOBA_BLOCK))[None, :]
        s_own = jnp.einsum('bhqd,bhkd->bhqk', q_c, k_own) * scale + rel_bias[:, rel_bucket(rel)]
        s_own = jnp.where(rel >= 0, s_own, -jnp.inf)
        n_sel = topk * MOBA_BLOCK
        logits = jnp.concatenate([s_sel.reshape(B, H, MOBA_QCHUNK, n_sel), s_own], axis=-1)
        p = jax.nn.softmax(logits, axis=-1)
        p_sel = p[..., :n_sel].reshape(B, H, MOBA_QCHUNK, topk, MOBA_BLOCK)
        p_own = p[..., n_sel:]
        return (jnp.einsum('bhqrk,bhqrkd->bhqd', p_sel, v_sel)
                + jnp.einsum('bhqk,bhkd->bhqd', p_own, v_own))

    out = lax.map(chunk, jnp.arange(S // MOBA_QCHUNK))
    return jnp.transpose(out, (1, 2, 0, 3, 4)).reshape(B, H, S, dh)

def token_mixing(u, w_in, w_gla_lr, b_gla_lr, gla_norm, rel_bias, w_br_gla, w_br_moba, w_out):
    B, S, _ = u.shape
    proj = u @ w_in
    offsets = np.cumsum(IN_SIZES)[:-1].tolist()
    gq, gk, gv, glr, gog, mq, mk, mv, ga, gb = jnp.split(proj, offsets, axis=-1)

    def heads(t, n):
        return t.reshape(B, S, n, -1).transpose(0, 2, 1, 3)

    log_a = jax.nn.log_sigmoid((glr @ w_gla_lr + b_gla_lr).astype(jnp.float32)) / GLA_TAU
    o_a = gla_chunked(heads(gq, GLA_HEADS) * (GLA_DK ** -0.5), heads(gk, GLA_HEADS),
                      heads(gv, GLA_HEADS), heads(log_a, GLA_HEADS))
    o_a = rmsnorm_2(o_a.transpose(0, 2, 1, 3), gla_norm)
    o_a = o_a * jax.nn.silu(gog.reshape(B, S, GLA_HEADS, GLA_DV).astype(jnp.float32))
    y_a = o_a.reshape(B, S, GLA_V_W).astype(u.dtype) @ w_br_gla

    o_b = moba_attention(heads(mq, MOBA_HEADS), heads(mk, MOBA_HEADS), heads(mv, MOBA_HEADS), rel_bias)
    y_b = o_b.transpose(0, 2, 1, 3).reshape(B, S, MOBA_W).astype(u.dtype) @ w_br_moba

    merged = jax.nn.sigmoid(ga) * y_a + jax.nn.sigmoid(gb) * y_b
    return merged @ w_out

def second_inputs(seed: int = 0) -> dict:
    key = jax.random.key(seed)
    ks = jax.random.split(key, 24)
    L, D, F = DEPTH_2, D_MODEL, D_FF_2
    nrm = lambda k, shape, fan_in: jax.random.normal(k, shape, jnp.float32) * (fan_in ** -0.5)
    gain = lambda k, shape: 1.0 + 0.05 * jax.random.normal(k, shape, jnp.float32)
    return {
        "x": jax.random.normal(ks[0], (BATCH, SEQ, D), jnp.float32),
        "c": jax.random.normal(ks[1], (BATCH, D), jnp.float32),
        "w_ada": nrm(ks[2], (L, D, N_MOD * D), D) * 0.5,
        "b_ada": 0.01 * jax.random.normal(ks[3], (L, N_MOD * D), jnp.float32),
        "norm_ff1": gain(ks[4], (L, D)),
        "w_ff1_gate": nrm(ks[5], (L, D, F), D),
        "w_ff1_up": nrm(ks[6], (L, D, F), D),
        "w_ff1_down": nrm(ks[7], (L, F, D), F),
        "norm_mix": gain(ks[8], (L, D)),
        "w_in": nrm(ks[9], (L, D, IN_WIDTH), D),
        "w_gla_lr": nrm(ks[10], (L, GLA_LOWRANK, GLA_QK_W), GLA_LOWRANK),
        "b_gla_lr": 0.1 * jax.random.normal(ks[11], (L, GLA_QK_W), jnp.float32),
        "gla_norm": gain(ks[12], (L, GLA_DV)),
        "rel_bias": 0.5 * jax.random.normal(ks[13], (MOBA_HEADS, NUM_BUCKETS), jnp.float32),
        "w_br_gla": nrm(ks[14], (L, GLA_V_W, D), GLA_V_W),
        "w_br_moba": nrm(ks[15], (L, MOBA_W, D), MOBA_W),
        "w_out": nrm(ks[16], (L, D, D), D),
        "norm_ff2": gain(ks[17], (L, D)),
        "w_ff2_gate": nrm(ks[18], (L, D, F), D),
        "w_ff2_up": nrm(ks[19], (L, D, F), D),
        "w_ff2_down": nrm(ks[20], (L, F, D), F),
        "norm_final": gain(ks[21], (D,)),
    }

def second_block(x, c, w_ada, b_ada, norm_ff1, w_ff1_gate, w_ff1_up, w_ff1_down, norm_mix, w_in,
              w_gla_lr, b_gla_lr, gla_norm, rel_bias, w_br_gla, w_br_moba, w_out, norm_ff2,
              w_ff2_gate, w_ff2_up, w_ff2_down, norm_final):
    h = x
    c_act = jax.nn.silu(c)
    for l in range(DEPTH_2):
        mod = c_act @ w_ada[l] + b_ada[l]
        sh1, sc1, g1, sh2, sc2, g2, sh3, sc3, g3 = jnp.split(mod, N_MOD, axis=-1)
        u = modulate(rmsnorm_2(h, norm_ff1[l]), sh1, sc1)
        h = h + FFN_RES * g1[:, None, :] * swiglu(u, w_ff1_gate[l], w_ff1_up[l], w_ff1_down[l])
        u = modulate(rmsnorm_2(h, norm_mix[l]), sh2, sc2)
        h = h + g2[:, None, :] * token_mixing(u, w_in[l], w_gla_lr[l], b_gla_lr[l], gla_norm[l], rel_bias,
                                              w_br_gla[l], w_br_moba[l], w_out[l])
        u = modulate(rmsnorm_2(h, norm_ff2[l]), sh3, sc3)
        h = h + FFN_RES * g3[:, None, :] * swiglu(u, w_ff2_gate[l], w_ff2_up[l], w_ff2_down[l])
    return rmsnorm_2(h, norm_final)


def setup_inputs(seed=0):
    out = dict(first_inputs(seed))
    for name, value in second_inputs(seed + 1).items():
        if name != "x":
            out[name + "_2"] = value
    return out


def reference(
    x, mem, norm_mix_g, norm_mem_g, norm_memsrc_g, norm_ff_g, mem_wq, mem_wk, mem_wv, mem_wo,
    ff_w1, ff_w2, conv_pw1_w, conv_pw1_b, conv_dw_w, conv_dw_b, conv_ln_g, conv_ln_b,
    conv_pw2_w, conv_pw2_b, kv_norm_g, kvf_w, fgate_b, fox_wq, fox_wo, final_norm_g, c_2,
    w_ada_2, b_ada_2, norm_ff1_2, w_ff1_gate_2, w_ff1_up_2, w_ff1_down_2, norm_mix_2, w_in_2,
    w_gla_lr_2, b_gla_lr_2, gla_norm_2, rel_bias_2, w_br_gla_2, w_br_moba_2, w_out_2,
    norm_ff2_2, w_ff2_gate_2, w_ff2_up_2, w_ff2_down_2, norm_final_2,
):
    x = first_block(
        x, mem, norm_mix_g, norm_mem_g, norm_memsrc_g, norm_ff_g, mem_wq, mem_wk, mem_wv,
        mem_wo, ff_w1, ff_w2, conv_pw1_w, conv_pw1_b, conv_dw_w, conv_dw_b, conv_ln_g,
        conv_ln_b, conv_pw2_w, conv_pw2_b, kv_norm_g, kvf_w, fgate_b, fox_wq, fox_wo,
        final_norm_g,
    )
    return second_block(
        x, c_2, w_ada_2, b_ada_2, norm_ff1_2, w_ff1_gate_2, w_ff1_up_2, w_ff1_down_2,
        norm_mix_2, w_in_2, w_gla_lr_2, b_gla_lr_2, gla_norm_2, rel_bias_2, w_br_gla_2,
        w_br_moba_2, w_out_2, norm_ff2_2, w_ff2_gate_2, w_ff2_up_2, w_ff2_down_2, norm_final_2,
    )


_drawn_inputs = setup_inputs


def setup_inputs(seed=0):
    import zlib

    import numpy as np

    out = dict(_drawn_inputs(seed))
    spreads = {}
    factors = {'norm_mix_g': 2.958,
     'norm_mem_g': 8.0,
     'norm_memsrc_g': 8.0,
     'conv_pw1_b': 7.222,
     'conv_dw_b': 3.766,
     'conv_ln_g': 2.925,
     'conv_ln_b': 8.0,
     'kv_norm_g': 5.936,
     'b_ada_2': 6.522,
     'norm_ff1_2': 7.2,
     'norm_mix_2': 4.668,
     'b_gla_lr_2': 8.0,
     'gla_norm_2': 8.0,
     'rel_bias_2': 4.323,
     'norm_ff2_2': 7.532}
    for name, (base, spread) in spreads.items():
        noise = np.random.default_rng([zlib.crc32(name.encode()), seed]).standard_normal(out[name].shape)
        drawn = base * np.exp(spread * noise) if base else spread * noise
        out[name] = __import__('jax').numpy.asarray(drawn.astype(out[name].dtype))
    for name, factor in factors.items():
        out[name] = (out[name] * factor).astype(out[name].dtype)
    return out
```

```python
from contextlib import ExitStack

import numpy as np

import concourse.bass as bass
from concourse import mybir

F32 = mybir.dt.float32
F32R = mybir.dt.float32r
BF16 = mybir.dt.bfloat16
ACT = mybir.ActivationFunctionType
ALU = mybir.AluOpType
AX = mybir.AxisListType

P = 128
D = 1024
T = 256
KT = D // P
PAIRS = KT // 2
TT = T // P
FF = 4096
KF = FF // P
FF2 = 2816
KF2 = FF2 // P
TAPS = 31
PAD = TAPS - 1
HEADS = 16
MEM_HEADS = 4
G_HEADS = 4
RMS_EPS = 1e-6
LN_EPS = 1e-5
RING = 4
MASKED = -1e30
LEVELS = [64, 32, 16, 8, 4, 2, 1]
NL = len(LEVELS)
SEGMENT = KT
N_MOD = 9
HALF = P // 2
SKEW = 512
BUCKETS = 32
V_TILES = 6

COLUMNS = [
    ("mix0", KT), ("mix1", KT), ("memq0", KT), ("memq1", KT), ("src0", KT), ("src1", KT),
    ("ff0", KT), ("ff1", KT), ("pw1_b", 2 * KT), ("dw_b", KT), ("ln_g", KT), ("ln_b", KT),
    ("pw2_b", KT), ("kv", KT), ("final1", KT), ("ffa", KT), ("mixn", KT), ("ffb", KT),
    ("final2", KT), ("gla", 1), ("ada_b", N_MOD * KT), ("cond", KT), ("fgate", HEADS),
]
COL = {}
_at = 0
for _name, _n in COLUMNS:
    COL[_name] = _at
    _at += _n
NCOL = _at


class Stage:

    def __init__(self, name, kind, chunks, elems, per_acc=1):
        self.name, self.kind, self.chunks, self.elems, self.per_acc = name, kind, chunks, elems, per_acc
        self.accs = chunks // per_acc


def plan():
    full = KT * 256
    seq = [
        Stage("pw1", "cols", 8, full), Stage("memk0", "cols", 4, full), Stage("memv0", "rows", 4, full),
        Stage("pw2", "cols", 4, full), Stage("memq0", "cols", 4, full), Stage("memo0", "cols", 4, full),
        Stage("up0", "cols", 16, full), Stage("down0", "deep32", 16, full, 4),
        Stage("foxk", "cols", 4, full), Stage("foxv", "rows", 4, full), Stage("foxf", "rows16", 1, KT * 16),
        Stage("foxq", "cols", 4, full),
        Stage("memk1", "cols", 4, full), Stage("memv1", "rows", 4, full),
        Stage("foxo", "cols", 4, full), Stage("memq1", "cols", 4, full), Stage("memo1", "cols", 4, full),
        Stage("up1", "cols", 16, full), Stage("down1", "deep32", 16, full, 4),
        Stage("gu1", "cols", KF2, full), Stage("dn1", "deep22", 16, 11 * P, 4),
        Stage("incols", "cols", 8, full), Stage("inrows", "rows", 4, full), Stage("inlr", "rows16", 1, KT * 16),
        Stage("ingates", "cols", 8, full), Stage("branch", "branch", 8, KT * P), Stage("out", "cols", 4, full),
        Stage("gu2", "cols", KF2, full), Stage("dn2", "deep22", 16, 11 * P, 4),
    ]
    base = acc = 0
    for s in seq:
        s.base, s.acc_base = base, acc
        base += s.chunks
        acc += s.accs
    return seq


PLAN = plan()
STAGE = {s.name: s for s in PLAN}
N_CHUNKS = PLAN[-1].base + PLAN[-1].chunks

X_UPDATES = ["pw2", "memo0", "down0", "foxo", "memo1", "down1", "final1", "dn1", "out", "dn2"]
NORMS = [("mix0", 1), ("mem0", 1), ("memq0", 1), ("ff0", 1), ("fox", 2), ("mem1", 1), ("memq1", 1),
         ("ff1", 1), ("final1", 0), ("ffa", 1), ("mixn", 1), ("ffb", 1), ("final2", 0)]
ATTENTIONS = [("mem0", MEM_HEADS, MEM_HEADS), ("fox", HEADS, HEADS // 2), ("mem1", MEM_HEADS, MEM_HEADS),
              ("moba", G_HEADS, G_HEADS)]


def elems_of(n):
    return next(s.elems for s in PLAN if s.base <= n < s.base + s.chunks)


def x_base(name):
    return PAIRS * X_UPDATES.index(name)


def norm_index(name):
    return [n for n, _ in NORMS].index(name)


def norm_base(name):
    return PAIRS * sum(k for _, k in NORMS[:norm_index(name)])


def head_base(name):
    i = [a[0] for a in ATTENTIONS].index(name)
    return sum(a[1] for a in ATTENTIONS[:i]), sum(a[2] for a in ATTENTIONS[:i])


def gla_at(h):
    return 2 * (h % 2) + h // 2


def spread(ap, n):
    return ap.unsqueeze(1).to_broadcast([ap.shape[0], n, ap.shape[1]])


def program(nc, dram, out):
    ctx = ExitStack()
    with ctx:
        cursor = [-(-nc.sbuf_base // 32) * 32]

        def place(name, shape, dt=F32, at=None):
            size = int(np.prod(shape[1:])) * (2 if dt == BF16 else 4)
            if at is None:
                at = cursor[0]
                cursor[0] += -(-size // 32) * 32
            return nc.alloc_sbuf_tensor_at(name, shape, dt, offset=at)

        raw = place("raw", [P, RING, KT * 256])
        wsplit = place("wsplit", [P, RING, 2, KT * 256], F32R)
        x = place("x", [P, KT, T])
        hA = place("hA", [P, KT, 2 * T], F32R)
        tsum = place("tsum", [P, 2, 2, T])
        aux = place("aux", [P, 2, 2, T])
        lowp = place("lowp", [P, 2, T])
        rstd = place("rstd", [P, T])
        var = place("var", [P, T])
        cols = place("cols", [P, NCOL])
        mod = place("mod", [P, N_MOD * KT])
        cact = place("cact", [P, KT])
        ones = place("ones", [P, P])
        ident = place("ident", [P, P])
        ident_bf = place("ident_bf", [P, P], BF16)
        mask_bf = place("mask_bf", [P, 2 * P], BF16)
        small = place("small", [P, 4, TT * HEADS])
        ada_w = place("ada_w", [P, 2, KT, HALF])
        ada_acc = place("ada_acc", [P, SEGMENT, P])

        region = cursor[0]
        KB = 1024

        def phased(name, shape, kb, dt=F32):
            return place(name, shape, dt, at=region + int(kb * KB))

        hid = phased("hid", [P, KF, 2 * T], 0, F32R)
        hM = phased("hM", [P, KT, 2 * T], 0, F32R)
        memx0 = phased("memx0", [P, KT, T], 16)
        mk0 = phased("mk0", [P, KT, T], 24)
        mv0 = phased("mv0", [P, TT, D], 32)
        upad = phased("upad", [P, KT, PAD + T], 40)
        conv = phased("conv", [P, KT, T], 49)
        taps = phased("taps", [P, TAPS, KT], 57)
        mu = phased("mu", [P, T], 58)
        relrep = phased("relrep", [BUCKETS + 1, G_HEADS, P], 59)
        onehot = phased("onehot", [BUCKETS + 1, SKEW], 61)
        relT = phased("relT", [BUCKETS + 1, G_HEADS], 63)
        pool_tmp = phased("pool_tmp", [P, T], 63.0625)
        mq0 = phased("mq0", [P, KT, T], 40)
        prob0 = phased("prob0", [P, 2, TT, T], 49)
        probT0 = phased("probT0", [P, 2, TT, T], 53)
        hB = phased("hB", [P, KT, 2 * T], 0, F32R)
        memx1 = phased("memx1", [P, KT, T], 16)
        mk1 = phased("mk1", [P, KT, T], 24)
        mv1 = phased("mv1", [P, TT, D], 32)
        fq = phased("fq", [P, KT, T], 40)
        fk = phased("fk", [P, KT, T], 48)
        fv = phased("fv", [P, TT, D], 56)
        negc_row = phased("negc_row", [P, HEADS, T], 0)
        tri = phased("tri", [P, TT, T], 16)
        negc = phased("negc", [P, T], 18)
        prob1 = phased("prob1", [P, 2, TT, T], 16)
        probT1 = phased("probT1", [P, 2, TT, T], 20)
        mq1 = phased("mq1", [P, KT, T], 40)
        inT = phased("inT", [P, 16, T], 0)
        inV = phased("inV", [P, TT, D], 16)
        gates = phased("gates", [P, KT, 2, T], 24)
        loga = phased("loga", [P, TT, T], 40)
        wlr = phased("wlr", [17, T], 42)
        decay = phased("decay", [P, 2, T], 42)
        qe = phased("qe", [P, 2, T], 44)
        ke = phased("ke", [P, 2, T], 46)
        za = phased("za", [P, TT, T], 44)
        zl = phased("zl", [P, TT, T], 46)
        A_same = phased("A_same", [P, 2 * G_HEADS, P], 48)
        A_next = phased("A_next", [P, G_HEADS, P], 52)
        spans = phased("spans", [P, NL + 2, P], 54)
        lmask = phased("lmask", [P, NL + 1, P], 58.5)
        glrT = phased("glrT", [32, T], 62.5)
        o_gla = phased("o_gla", [P, G_HEADS, T], 48)
        toep = phased("toep", [P, G_HEADS, 3 * P], 42)
        prob2 = phased("prob2", [P, 2, TT, T], 54)
        probT2 = phased("probT2", [P, 2, TT, T], 58)
        assert region + 64 * KB <= nc.sbuf_usable_end, (region + 64 * KB, nc.sbuf_usable_end)

        def pb(name, shape):
            return ctx.enter_context(nc.psum_tensor(name, shape, F32))

        acc = pb("acc", [P, 2, 2, 2 * T])
        score = pb("score", [P, 2, TT, T])
        turned = pb("turned", [P, TT, T])
        stat = pb("stat", [P, 2, T])

        skew_dram = nc.dram_tensor("skew_dram", (G_HEADS, P, SKEW), F32, kind="Internal").ap()

        sems = {}

        def S(name):
            if name not in sems:
                sems[name] = ctx.enter_context(nc.semaphore(name))
            return sems[name]

        def col(name, i=0, n=1):
            return cols[:, COL[name] + i:COL[name] + i + n]

        raw_loaded = [S(f"raw_loaded{i}") for i in range(RING)]
        ada_loaded = [S(f"ada_loaded{i}") for i in range(2)]

        def groups(eng, n_chunks, body, unroll=RING, lead=0, tail=0):
            first = lead
            last = max(first, (n_chunks - tail) // unroll * unroll)
            if last - first < 2 * unroll:
                first = last = 0
            for c in range(first):
                body(c, c)
            if last > first:
                with eng.Fori(first // unroll, last // unroll) as i:
                    for k in range(unroll):
                        body(i * unroll + k, first + k)
            for c in range(last, n_chunks):
                body(c, c)

        block = ctx.enter_context(nc.Block())

        @block.sync
        def _(sp):
            sp.dma_start(x[:], dram["xT"]).then_inc(S("x_loaded"), 16)
            sp.dma_start(cols[:], dram["cols"]).then_inc(S("consts_loaded"), 16)
            sp.dma_start(ones[:], dram["ones"]).then_inc(S("consts_loaded"), 16)
            sp.dma_start(ident[:], dram["ident"]).then_inc(S("consts_loaded"), 16)
            sp.dma_start(taps[:], dram["taps"]).then_inc(S("consts_loaded"), 16)
            sp.dma_start(onehot[:], dram["onehot"]).then_inc(S("consts_loaded"), 16)
            sp.dma_start(relT[:], dram["relT"]).then_inc(S("consts_loaded"), 16)
            sp.dma_start(mask_bf[:], dram["mask"]).then_inc(S("consts_loaded"), 16)
            sp.dma_start(memx0[:], dram["memT"]).then_inc(S("mem_loaded"), 16)

            def load(st, c, known):
                slot = (st.base + known) % RING
                if st.base + known >= RING:
                    sp.wait_ge(S("w_lo"), c + (st.base - RING + 1))
                sp.dma_start(raw[:, slot, 0:st.elems], dram[st.name][c]).then_inc(raw_loaded[slot], 16)

            for st in PLAN:
                groups(sp, st.chunks, lambda c, known: load(st, c, known), lead=RING if st.base == 0 else 0)
            for p in range(PAIRS):
                sp.wait_ge(S("final_ready"), p + 1)
                sp.dma_start(out[:, 2 * p:2 * p + 2, :], x[:, 2 * p:2 * p + 2, :]).then_inc(S("stored"), 16)
            sp.wait_ge(S("stored"), 16 * PAIRS)

        @block.tensor
        def _(pe):
            def weights_ready(st, c):
                pe.wait_ge(S("w_hi"), c + (st.base + 1))
                pe.wait_ge(S("w_lo"), c + (st.base + 1))

            def acc_free(st, a, known_a):
                if st.acc_base + known_a >= 2:
                    pe.wait_ge(S("acc_summed"), a + (st.acc_base - 1))

            def block_cols(dst, w, lo_w, h, start, stop):
                nc.tensor.matmul(dst, w, h, start=start, stop=False, skip_group_check=True)
                return nc.tensor.matmul(dst[:, 0:T], lo_w, h[:, 0:T], start=False, stop=stop,
                                        skip_group_check=True)

            def chunk_cols(st, slot, par, h, kts, cols_of, start, stop, ready):
                for i, kt in enumerate(kts):
                    if ready and kt in ready:
                        for sem, value in ready[kt]:
                            pe.wait_ge(sem, value)
                    for j, at in cols_of(i):
                        mm = block_cols(acc[:, par, j, :], wsplit[:, slot, 0, at:at + P],
                                        wsplit[:, slot, 1, at:at + P], h[:, kt, :],
                                        start and i == 0, stop and i == len(kts) - 1)
                return mm

            def linear(name, h, ready):
                st = STAGE[name]

                def body(c, known):
                    slot = (st.base + known) % RING
                    kt_all = list(range(KT))
                    if st.per_acc == 1:
                        a, known_a, q = c, known, 0
                    else:
                        q = known % st.per_acc
                        a, known_a = None, known // st.per_acc
                    weights_ready(st, c)
                    par = (st.acc_base + known_a) % 2
                    if st.per_acc == 1:
                        acc_free(st, a, known_a)
                    elif q == 0:
                        acc_free(st, known_a, known_a)
                    w = wsplit[:, slot, :, :]
                    if st.kind == "cols":
                        mm = chunk_cols(st, slot, par, h, kt_all,
                                        lambda i: [(j, i * 2 * P + j * P) for j in range(2)],
                                        True, True, ready)
                    elif st.kind == "deep32":
                        mm = chunk_cols(st, slot, par, h, [q * KT + i for i in range(KT)],
                                        lambda i: [(j, i * 2 * P + j * P) for j in range(2)],
                                        q == 0, q == 3, ready)
                    elif st.kind == "deep22":
                        mm = chunk_cols(st, slot, par, h, [(q % 2) * 11 + i for i in range(11)],
                                        lambda i: [(q // 2, i * P)], q % 2 == 0, q % 2 == 1, ready)
                    elif st.kind == "branch":
                        for br in range(2):
                            mm = chunk_cols(st, slot, par, h, [4 * br + i for i in range(4)],
                                            lambda i: [(br, (4 * br + i) * P)], True, True, ready)
                    else:
                        n = 256 if st.kind == "rows" else HEADS
                        for kt in range(KT):
                            if ready and kt in ready:
                                for sem, value in ready[kt]:
                                    pe.wait_ge(sem, value)
                            for tt in range(TT):
                                dst = acc[:, par, tt, 0:2 * n]
                                nc.tensor.matmul(dst.rearrange("p (s n) -> p s n", s=2),
                                                 h[:, kt, tt * P:(tt + 1) * P],
                                                 w[:, :, kt * n:(kt + 1) * n],
                                                 start=kt == 0, stop=False, skip_group_check=True)
                                mm = nc.tensor.matmul(dst[:, 0:n], h[:, kt, T + tt * P:T + (tt + 1) * P],
                                                      w[:, 0, kt * n:(kt + 1) * n],
                                                      start=False, stop=kt == KT - 1,
                                                      skip_group_check=True)
                    mm.then_inc(S("chunk_done"), 1)

                if st.per_acc == 1:
                    groups(pe, st.chunks, body, lead=RING if st.base == 0 else 0)
                else:
                    for c in range(st.chunks):
                        body(c, c)

            def pair_ready(base):
                return {2 * p: [(S("norm_lo"), base + p + 1)] for p in range(PAIRS)}

            def norm_sums(name):
                q = norm_index(name)
                for p in range(PAIRS):
                    pe.wait_ge(S("norm_sq"), PAIRS * q + p + 1)
                    if p == 0 and q > 0:
                        pe.wait_ge(S("norm_var"), q)
                        modulation_read()
                    for j in range(2):
                        mm = nc.tensor.matmul(stat[:, 0, :], ones[:], aux[:, p % 2, j, :],
                                              start=p == 0 and j == 0, stop=p == PAIRS - 1 and j == 1)
                    mm.then_inc(S("norm_stat"), 1)

            segments_summed = [0]

            def modulation_read():
                if segments_summed[0]:
                    pe.wait_ge(S("mod_made"), segments_summed[0])

            def ada(seg, sem, value):
                pe.wait_ge(S("ada_step"), 64 * (seg + 1))
                pe.wait_ge(sem, value)
                for m in range(SEGMENT):
                    mm = nc.tensor.matmul(stat[:, 1, m:m + 1], ada_acc[:, m, :], ones[:, 0:1],
                                          start=True, stop=True)
                mm.then_inc(S("ada_used"), 1)
                segments_summed[0] += 1

            def attention(name, q, k, v, prob, probT, extra, dh, first_ready):
                _, n_heads, n_groups = next(a for a in ATTENTIONS if a[0] == name)
                b, gb = head_base(name)
                per_group = n_heads // n_groups

                def scores(h):
                    if b + h >= 2:
                        pe.wait_ge(S("att_exp"), b + h - 1)
                    begun = extra(h) if extra else False
                    off = (h * dh) % P
                    rows = min(dh, P)
                    tiles = [h * dh // P + i for i in range(max(1, dh // P))]
                    for qt in range(TT):
                        for i, kt in enumerate(tiles):
                            mm = nc.tensor.matmul(score[:, h % 2, qt, :],
                                                  q[off:off + rows, kt, qt * P:(qt + 1) * P],
                                                  k[off:off + rows, kt, :],
                                                  start=not begun and i == 0, stop=i == len(tiles) - 1,
                                                  skip_group_check=True)
                    mm.then_inc(S("att_scores"), 1)

                for sem, value in first_ready:
                    pe.wait_ge(sem, value)
                modulation_read()
                scores(0)
                for h in range(n_heads):
                    if h + 1 < n_heads:
                        scores(h + 1)
                    pe.wait_ge(S("att_prob"), b + h + 1)
                    if b + h >= 1:
                        pe.wait_ge(S("att_turned"), b + h)
                    for kt in range(TT):
                        for qt in range(TT):
                            mm = nc.tensor.transpose(turned[:, kt, qt * P:(qt + 1) * P],
                                                     prob[:, h % 2, qt, kt * P:(kt + 1) * P], ident[:])
                    mm.then_inc(S("att_turn"), 1)
                    pe.wait_ge(S("att_turned"), b + h + 1)
                    g = h // per_group
                    if h % per_group == 0 and gb + g >= 1:
                        pe.wait_ge(S("att_lo"), gb + g)
                    if dh >= P:
                        for dt in range(dh // P):
                            for kt in range(TT):
                                mm = nc.tensor.matmul(stat[:, dt, :],
                                                      v(kt, h * dh + dt * P, P), probT[:, h % 2, kt, :],
                                                      start=kt == 0, stop=kt == TT - 1)
                    else:
                        off = (h * dh) % P
                        for kt in range(TT):
                            mm = nc.tensor.matmul(stat[off:off + dh, 0, :],
                                                  v(kt, h * dh, dh), probT[:, h % 2, kt, :],
                                                  start=kt == 0, stop=kt == TT - 1,
                                                  skip_group_check=True)
                    mm.then_inc(S("att_out"), 1)

            pe.wait_ge(S("consts_loaded"), 16 * 7)
            norm_sums("mix0")
            linear("pw1", hA, pair_ready(norm_base("mix0")))
            norm_sums("mem0")
            linear("memk0", hM, pair_ready(norm_base("mem0")))
            linear("memv0", hM, None)
            pe.wait_ge(S("rel_spread"), 1)
            for h in range(G_HEADS):
                if h:
                    pe.wait_ge(S("rel_copied"), h)
                nc.tensor.matmul(turned[:].rearrange("p a b -> p (a b)"), relrep[:, h, :], onehot[:],
                                 start=True, stop=True).then_inc(S("rel_made"), 1)
            pe.wait_ge(S("conv_step"), V_TILES * TAPS)
            pe.wait_ge(S("conv_pool_step"), (KT - V_TILES) * (2 * TAPS - 1))
            pe.wait_ge(S("norm_var"), norm_index("mem0") + 1)
            for kt in range(KT):
                mm = nc.tensor.matmul(stat[:, 0, :], ones[:], conv[:, kt, :], start=kt == 0, stop=kt == KT - 1)
            mm.then_inc(S("ln_stat"), 1)
            for p in range(PAIRS):
                pe.wait_ge(S("ln_sq"), p + 1)
                for j in range(2):
                    mm = nc.tensor.matmul(stat[:, 0, :], ones[:], aux[:, p % 2, j, :],
                                          start=p == 0 and j == 0, stop=p == PAIRS - 1 and j == 1)
                mm.then_inc(S("ln_stat"), 1)
            linear("pw2", hA, {2 * p: [(S("ln_lo"), p + 1)] for p in range(PAIRS)})
            ada(0, S("x_updated"), x_base("pw2") + PAIRS)
            norm_sums("memq0")
            linear("memq0", hA, pair_ready(norm_base("memq0")))

            def mem_v(v):
                return lambda kt, at, n: v[:, kt, at:at + n]

            s = STAGE["memq0"]
            attention("mem0", mq0, mk0, mem_v(mv0), prob0, probT0, None, 256,
                      [(S("acc_summed"), s.acc_base + s.accs)])
            gb = head_base("mem0")[1]
            linear("memo0", hA, {2 * p: [(S("att_lo"), gb + p + 1)] for p in range(PAIRS)})
            ada(1, S("x_updated"), x_base("memo0") + PAIRS)
            norm_sums("ff0")
            linear("up0", hA, pair_ready(norm_base("ff0")))
            ada(2, S("norm_var"), norm_index("ff0") + 1)
            linear("down0", hid, {2 * c: [(S("up0_lo"), c + 1)] for c in range(KF // 2)})
            ada(3, S("x_updated"), x_base("down0") + PAIRS)

            norm_sums("fox")
            nb = norm_base("fox")
            linear("foxk", hA, pair_ready(nb))
            linear("foxv", hA, None)
            linear("foxf", hA, None)
            linear("foxq", hB, pair_ready(nb + PAIRS))
            ada(4, S("norm_var"), norm_index("fox") + 1)
            norm_sums("mem1")
            linear("memk1", hA, pair_ready(norm_base("mem1")))
            linear("memv1", hA, None)
            pe.wait_ge(S("logf_ready"), 1)
            pe.wait_ge(S("tri_loaded"), 16)
            for tt in range(TT):
                mm = nc.tensor.matmul(turned[0:HEADS, 0, :], small[:, 3, tt * HEADS:(tt + 1) * HEADS],
                                      tri[:, tt, :], start=tt == 0, stop=tt == TT - 1)
            mm.then_inc(S("negc_made"), 1)

            def fox_bias(h):
                bank = score[:, h % 2, :, :]
                nc.tensor.matmul(bank[:, 0, :], ident_bf[:], mask_bf[:], start=True, stop=False,
                                 skip_group_check=True)
                nc.tensor.matmul(bank[:, 1, P:T], ident_bf[:], mask_bf[:, 0:P], start=False, stop=False,
                                 skip_group_check=True)
                for qt in range(TT):
                    nc.tensor.matmul(bank[:, qt, :], ones[0:1, :], negc_row[0:1, h, :], start=False,
                                     stop=False, skip_group_check=True)
                return True

            s = STAGE["memv1"]
            attention("fox", fq, fk, mem_v(fv), prob1, probT1, fox_bias, 64,
                      [(S("acc_summed"), s.acc_base + s.accs), (S("negc_placed"), 16), (S("ident_bf"), 1)])
            gb = head_base("fox")[1]
            linear("foxo", hA, {g: [(S("att_lo"), gb + g + 1)] for g in range(KT)})
            ada(5, S("x_updated"), x_base("foxo") + PAIRS)
            norm_sums("memq1")
            linear("memq1", hA, pair_ready(norm_base("memq1")))
            s = STAGE["memq1"]
            attention("mem1", mq1, mk1, mem_v(mv1), prob1, probT1, None, 256,
                      [(S("acc_summed"), s.acc_base + s.accs)])
            gb = head_base("mem1")[1]
            linear("memo1", hA, {2 * p: [(S("att_lo"), gb + p + 1)] for p in range(PAIRS)})
            ada(6, S("x_updated"), x_base("memo1") + PAIRS)
            norm_sums("ff1")
            linear("up1", hA, pair_ready(norm_base("ff1")))
            ada(7, S("norm_var"), norm_index("ff1") + 1)
            linear("down1", hid, {2 * c: [(S("up1_lo"), c + 1)] for c in range(KF // 2)})
            ada(8, S("x_updated"), x_base("down1") + PAIRS)
            norm_sums("final1")

            norm_sums("ffa")
            linear("gu1", hA, pair_ready(norm_base("ffa")))
            linear("dn1", hid, {c: [(S("gu1_lo"), c + 1)] for c in range(KF2)})
            norm_sums("mixn")
            linear("incols", hA, pair_ready(norm_base("mixn")))
            linear("inrows", hA, None)
            linear("inlr", hA, None)
            pe.wait_ge(S("acc_summed"), STAGE["inlr"].acc_base + 1)
            for tt in range(TT):
                mm = nc.tensor.transpose(turned[0:16, 0, tt * P:(tt + 1) * P],
                                         small[:, 0, tt * 16:(tt + 1) * 16], ident[:])
            mm.then_inc(S("lr_turn"), 1)
            linear("ingates", hA, None)
            pe.wait_ge(S("lr_turned"), 2)
            pe.wait_ge(S("wlr_loaded"), 16)
            for tt in range(TT):
                mm = nc.tensor.matmul(turned[:, tt, :], glrT[0:17, tt * P:(tt + 1) * P], wlr[:],
                                      start=True, stop=True)
            mm.then_inc(S("lr_logits"), 1)
            pe.wait_ge(S("loga_ready"), 1)
            pe.wait_ge(S("spans_loaded"), 32)
            s = STAGE["ingates"]
            pe.wait_ge(S("acc_summed"), s.acc_base + s.accs)
            moba_scores = head_base("moba")[0]

            def level_spans(lv):
                if lv == NL:
                    return
                i = lv if lv < NL else NL
                if i >= 2:
                    pe.wait_ge(S("gla_exp"), i - 1)
                for ct in range(2):
                    for tt in range(TT):
                        m = lv if lv < NL else NL + tt
                        mm = nc.tensor.matmul(score[:, i % 2, ct, tt * P:(tt + 1) * P],
                                              loga[:, tt, ct * P:(ct + 1) * P], spans[:, m, :],
                                              start=True, stop=True)
                mm.then_inc(S("gla_span"), 1)

            A_ps = [acc[:, i, :, :].rearrange("p a (b t) -> p (a b) t", b=4) for i in range(2)]

            def level_scores(lv):
                own = lv < NL + 1
                if lv < NL:
                    pe.wait_ge(S("gla_qk"), 2 * (lv + 1))
                elif lv == NL + 1:
                    pe.wait_ge(S("gla_qk"), 2 * (NL + 1))
                if lv >= 2:
                    pe.wait_ge(S("gla_masked"), 2 * (lv - 1) - 1)
                kk, qq = (inT[:, 2:4, :], inT[:, 0:2, :]) if lv == NL else (ke[:], qe[:])
                for h in range(G_HEADS):
                    off, ct = 64 * (h % 2), h // 2
                    for tt in range(TT if own else 1):
                        dst = A_ps[lv % 2][:, 2 * gla_at(h) + tt if own else 4 * (h % 2) + h // 2, :]
                        qt = tt if own else 1
                        mm = nc.tensor.matmul(dst, kk[off:off + 64, ct, tt * P:(tt + 1) * P],
                                              qq[off:off + 64, ct, qt * P:(qt + 1) * P],
                                              start=True, stop=True, skip_group_check=True)
                mm.then_inc(S("gla_scores"), 1)

            level_spans(0)
            for lv in range(NL + 2):
                if lv + 1 < NL:
                    level_spans(lv + 1)
                elif lv == NL:
                    level_spans(NL + 1)
                level_scores(lv)
            pe.wait_ge(S("gla_masked"), 2 * (NL + 1))
            for h in range(G_HEADS):
                dst = score[:, h // 2, h % 2, :]
                nc.tensor.matmul(dst[:, 0:P], inV[:, 0, h * P:(h + 1) * P], A_same[:, 2 * gla_at(h), :],
                                 start=True, stop=True, skip_group_check=True)
                nc.tensor.matmul(dst[:, P:T], inV[:, 0, h * P:(h + 1) * P], A_next[:, gla_at(h), :],
                                 start=True, stop=False, skip_group_check=True)
                mm = nc.tensor.matmul(dst[:, P:T], inV[:, 1, h * P:(h + 1) * P], A_same[:, 2 * gla_at(h) + 1, :],
                                      start=False, stop=True, skip_group_check=True)
            mm.then_inc(S("gla_out"), 1)
            pe.wait_ge(S("gla_sq"), 1)
            sums = acc[:, 0, :, :]
            for i in range(2):
                mm = nc.tensor.matmul(sums[:, i, :], ones[:], aux[:, i, :, :].rearrange("p a t -> p (a t)"),
                                      start=True, stop=True)
            mm.then_inc(S("gla_stat"), 1)

            def moba_bias(h):
                nc.tensor.matmul(score[:, h % 2, 0, :], ident[:], toep[:, h, P:3 * P], start=True,
                                 stop=False, skip_group_check=True)
                nc.tensor.matmul(score[:, h % 2, 1, :], ident[:], toep[:, h, 0:2 * P], start=False,
                                 stop=False, skip_group_check=True)
                return True

            attention("moba", inT[:, 8:12, :], inT[:, 12:16, :],
                      lambda kt, at, n: inV[:, kt, 512 + at:512 + at + n], prob2, probT2, moba_bias, P,
                      [(S("gla_o"), 1), (S("toep_loaded"), 16)])
            gb = head_base("moba")[1]
            linear("branch", hA, {0: [(S("gla_lo"), 1)], 4: [(S("att_lo"), gb + 1)], 5: [(S("att_lo"), gb + 2)],
                                  6: [(S("att_lo"), gb + 3)], 7: [(S("att_lo"), gb + 4)]})
            linear("out", hM, {c: [(S("branch_lo"), c + 1)] for c in range(KT)})
            norm_sums("ffb")
            linear("gu2", hA, pair_ready(norm_base("ffb")))
            linear("dn2", hid, {c: [(S("gu2_lo"), c + 1)] for c in range(KF2)})
            norm_sums("final2")

        @block.scalar
        def _(act):
            def wait(sem, value):
                act.wait_ge(S(sem), value)

            def split_hi(st, c, known):
                n = st.base + known
                slot = n % RING
                act.wait_ge(raw_loaded[slot], (c - known) * (16 // RING) + 16 * (n // RING + 1))
                if n >= RING:
                    wait("chunk_done", c + (st.base - RING + 1))
                nc.scalar.activation(wsplit[:, slot, 0, 0:elems_of(n)], raw[:, slot, 0:elems_of(n)],
                                     ACT.Copy).then_inc(S("w_hi"), 1)

            def low(st, a, known_a, bias=None, width=T):
                par = (st.acc_base + known_a) % 2
                wait("chunk_done", a * st.per_acc + (st.base + st.per_acc))
                if st.acc_base + known_a >= 1:
                    wait("acc_summed", a + st.acc_base)
                if bias is None:
                    src = acc[:, par, :, width:2 * width]
                    last = nc.scalar.activation(lowp[:, :, 0:width], src, ACT.Copy)
                else:
                    for j in range(2):
                        last = nc.scalar.activation(lowp[:, j, :], acc[:, par, j, T:2 * T], ACT.Identity,
                                                    bias=bias(known_a, j))
                last.then_inc(S("acc_low"), 1)

            def linear(name, bias=None, post=None, flush=None, width=T):
                st = STAGE[name]

                def body(c, known):
                    if st.per_acc == 1:
                        low(st, c, known, bias, width)
                        if post:
                            post(c, known)
                    elif known % st.per_acc == st.per_acc - 1:
                        low(st, known // st.per_acc, known // st.per_acc, bias, width)
                    if st.base + known + RING < N_CHUNKS:
                        split_hi(st, c + RING, known + RING)

                if st.per_acc == 1 and bias is None:
                    groups(act, st.chunks, body, lead=RING, tail=RING)
                else:
                    for c in range(st.chunks):
                        body(c, c)
                if flush:
                    flush()

            def norm_squares(name, src, ready):
                q = norm_index(name)
                for p in range(PAIRS):
                    for sem, value in ready(p):
                        wait(sem, value)
                    if p >= 2:
                        wait("norm_stat", PAIRS * q + p - 1)
                    nc.scalar.activation(aux[:, p % 2, :, :], src[:, 2 * p:2 * p + 2, :],
                                         ACT.Square).then_inc(S("norm_sq"), 1)

            def norm_root(name):
                wait("norm_var", norm_index(name) + 1)
                nc.scalar.activation(rstd[:], var[:], ACT.Sqrt).then_inc(S("norm_root"), 1)

            def norm_hi(name, dest, which=0, shift=None):
                nb = norm_base(name) + PAIRS * which
                for p in range(PAIRS):
                    wait("norm_h", nb + p + 1)
                    if shift is None:
                        last = nc.scalar.activation(dest[:, 2 * p:2 * p + 2, 0:T], tsum[:, p % 2, :, :], ACT.Copy)
                    else:
                        for j in range(2):
                            last = nc.scalar.activation(dest[:, 2 * p + j, 0:T], tsum[:, p % 2, j, :],
                                                        ACT.Identity, bias=mod[:, shift + 2 * p + j:shift + 2 * p + j + 1])
                    last.then_inc(S("norm_hi"), 1)

            def norm(name, src, ready, dests, shift=None):
                norm_squares(name, src, ready)
                norm_root(name)
                for i, dest in enumerate(dests):
                    norm_hi(name, dest, i, shift)

            def x_ready(stage):
                return lambda p: [("x_updated", x_base(stage) + p + 1)]

            def hidden_hi(name, dest):
                def post(c, known):
                    wait(f"{name}_r", c + 1)
                    par = (STAGE[name].acc_base + known) % 2
                    if dest is hid and name.startswith("up"):
                        out_ap = hid[:].rearrange("p (c j) t -> p c j t", j=2)[:, c, :, 0:T]
                        nc.scalar.activation(out_ap, tsum[:, par, :, :], ACT.Copy).then_inc(S(f"{name}_hi"), 1)
                    else:
                        nc.scalar.activation(dest[:, c, 0:T], tsum[:, par, 0, :],
                                             ACT.Copy).then_inc(S(f"{name}_hi"), 1)
                return post

            def feed_forward(up, down):
                hi = hidden_hi(up, hid)
                n = STAGE[up].chunks
                linear(up, post=lambda c, known: hi(c - 1, known - 1) if known >= 1 else None,
                       flush=lambda: hi(n - 1, n - 1))
                linear(down)

            def gated_feed_forward(gu, dn):
                hi = hidden_hi(gu, hid)
                n = STAGE[gu].chunks

                def post(c, known):
                    if known >= 1:
                        hi(c - 1, known - 1)
                    par = (STAGE[gu].acc_base + known) % 2
                    wait("acc_summed", c + (STAGE[gu].acc_base + 1))
                    nc.scalar.activation(aux[:, par, 0, :], tsum[:, par, 0, :],
                                         ACT.Sigmoid).then_inc(S(f"{gu}_sig"), 1)

                linear(gu, post=post, flush=lambda: hi(n - 1, n - 1))
                linear(dn)

            def attention(name, scale, prob, probT, dest_tile):
                _, n_heads, n_groups = next(a for a in ATTENTIONS if a[0] == name)
                b, gb = head_base(name)
                per_group = n_heads // n_groups
                tiles = 2 if name.startswith("mem") else 1

                def exps(h):
                    wait("att_max", 2 * (b + h + 1))
                    if h >= 2:
                        wait("att_turn", b + h - 1)
                    for qt in range(TT):
                        at = 2 * h + qt
                        last = nc.scalar.activation(prob[:, h % 2, qt, :], score[:, h % 2, qt, :], ACT.Exp,
                                                    bias=small[:, 1, at:at + 1], scale=scale,
                                                    accum_out=small[:, 2, at:at + 1])
                    last.then_inc(S("att_exp"), 1)

                def out_hi(g):
                    wait("att_out", b + per_group * (g + 1))
                    nc.scalar.activation(hA[:, dest_tile + g * tiles:dest_tile + (g + 1) * tiles, 0:T],
                                         stat[:, 0:tiles, :], ACT.Copy).then_inc(S("att_hi"), 1)

                exps(0)
                for h in range(n_heads):
                    if h + 1 < n_heads:
                        exps(h + 1)
                    if h >= 1 and h % per_group == 0:
                        out_hi(h // per_group - 1)
                    wait("att_turn", b + h + 1)
                    if h >= 2:
                        wait("att_out", b + h - 1)
                    nc.scalar.activation(probT[:, h % 2, :, :], turned[:], ACT.Copy).then_inc(S("att_turned"), 1)
                out_hi(n_groups - 1)

            def log_sigmoid(z, za_, zl_, sem, first):
                wait(sem, first)
                nc.scalar.activation(za_, z, ACT.Abs).then_inc(S(sem + "_ln"), 1)
                wait(sem + "_ln", 1)
                nc.scalar.activation(zl_, za_, ACT.Exp, scale=-1.0).then_inc(S(sem + "_ln"), 1)
                wait(sem + "_ln", 2)
                nc.scalar.activation(za_, zl_, ACT.Ln, bias=1.0).then_inc(S(sem + "_ln"), 1)

            for n in range(RING):
                split_hi(PLAN[0], n, n)
            wait("consts_loaded", 16 * 7)
            nc.scalar.activation(cact[:], col("cond", 0, KT), ACT.Sigmoid).then_inc(S("cond_sig"), 1)
            nc.scalar.activation(ident_bf[:], ident[:], ACT.Copy).then_inc(S("ident_bf"), 1)
            for h in range(G_HEADS):
                last = nc.scalar.activation(relrep[:, h, :], relT[:, h:h + 1].to_broadcast([BUCKETS + 1, P]), ACT.Copy)
            last.then_inc(S("rel_spread"), 1)
            norm("mix0", x, lambda p: [("x_loaded", 16)], [hA])

            def glu(c, known):
                wait("acc_summed", c + 1)
                if c >= 2:
                    wait("u_ready", c - 1)
                nc.scalar.activation(aux[:, c % 2, 0, :], tsum[:, c % 2, 1, :], ACT.Sigmoid).then_inc(S("pw1_sig"), 1)

            wait("norm_stat", PAIRS)
            linear("pw1", bias=lambda a, j: col("pw1_b", KT * j + a), post=glu)
            wait("u_ready", KT)
            norm("mem0", memx0, lambda p: [("mem_loaded", 16)], [hM])
            linear("memk0")
            linear("memv0")
            s = STAGE["memv0"]
            wait("acc_summed", s.acc_base + s.accs)
            for h in range(G_HEADS):
                wait("rel_made", h + 1)
                if h:
                    wait("skew_stored", 16 * h)
                nc.scalar.activation(lowp[:].rearrange("p a t -> p (a t)"), turned[:].rearrange("p a t -> p (a t)"),
                                     ACT.Copy, scale=float(P) ** 0.5).then_inc(S("rel_copied"), 1)
                wait("rel_copied", h + 1)
                act.dma_start(skew_dram[h], lowp[:].rearrange("p a t -> p (a t)")).then_inc(S("skew_stored"), 16)
            for p in range(PAIRS):
                wait("ln_centred", p + 1)
                if p >= 2:
                    wait("ln_stat", p)
                nc.scalar.activation(aux[:, p % 2, :, :], conv[:, 2 * p:2 * p + 2, :], ACT.Square).then_inc(S("ln_sq"), 1)
            wait("ln_var", 1)
            nc.scalar.activation(rstd[:], var[:], ACT.Sqrt).then_inc(S("ln_root"), 1)
            for p in range(PAIRS):
                wait("ln_y", p + 1)
                if p >= 2:
                    wait("ln_r", p - 1)
                for j in range(2):
                    kt = 2 * p + j
                    last = nc.scalar.activation(aux[:, p % 2, j, :], conv[:, kt, :], ACT.Sigmoid,
                                                bias=col("ln_b", kt), scale=col("ln_g", kt))
                last.then_inc(S("ln_sig"), 1)
                if p >= 1:
                    wait("ln_r", p)
                    nc.scalar.activation(hA[:, 2 * p - 2:2 * p, 0:T], tsum[:, (p - 1) % 2, :, :], ACT.Copy).then_inc(S("ln_hi"), 1)
            wait("ln_r", PAIRS)
            nc.scalar.activation(hA[:, KT - 2:KT, 0:T], tsum[:, 1, :, :], ACT.Copy).then_inc(S("ln_hi"), 1)
            wait("skew_stored", 16 * G_HEADS)
            linear("pw2", bias=lambda a, j: col("pw2_b", 2 * a + j))
            norm("memq0", x, x_ready("pw2"), [hA])
            linear("memq0")
            attention("mem0", 1 / 16, prob0, probT0, 0)
            linear("memo0")
            norm("ff0", x, x_ready("memo0"), [hA])
            feed_forward("up0", "down0")

            s = STAGE["down0"]
            wait("chunk_done", s.base + s.chunks)
            act.dma_start(memx1[:], dram["memT"]).then_inc(S("mem1_loaded"), 16)
            norm("fox", x, x_ready("down0"), [hA, hB])
            linear("foxk")
            linear("foxv")
            linear("foxf", width=HEADS)
            linear("foxq")
            norm("mem1", memx1, lambda p: [("mem1_loaded", 16)], [hA])
            wait("norm_h", norm_base("mem1") + PAIRS)
            act.dma_start(tri[:], dram["tri"]).then_inc(S("tri_loaded"), 16)
            log_sigmoid(small[:, 0, :], small[:, 1, :], small[:, 2, :], "fgate_z", 1)
            linear("memk1")
            linear("memv1")
            wait("negc_ready", 1)
            s = STAGE["foxq"]
            wait("chunk_done", s.base + s.chunks)
            act.dma_start(negc_row[0:1, :, :], negc[0:HEADS, :]).then_inc(S("negc_placed"), 16)
            wait("negc_placed", 16)
            attention("fox", 1 / 8, prob1, probT1, 0)
            linear("foxo")
            norm("memq1", x, x_ready("foxo"), [hA])
            linear("memq1")
            attention("mem1", 1 / 16, prob1, probT1, 0)
            linear("memo1")
            norm("ff1", x, x_ready("memo1"), [hA])
            feed_forward("up1", "down1")
            norm("final1", x, x_ready("down1"), [])

            norm("ffa", x, x_ready("final1"), [hA], shift=0)
            gated_feed_forward("gu1", "dn1")
            norm("mixn", x, x_ready("dn1"), [hA], shift=3 * KT)
            s = STAGE["dn1"]
            wait("chunk_done", s.base + s.chunks)
            act.dma_start(spans[:], dram["spans"]).then_inc(S("spans_loaded"), 16)
            act.dma_start(lmask[:], dram["lmask"]).then_inc(S("spans_loaded"), 16)
            act.dma_start(wlr[:], dram["wlr"]).then_inc(S("wlr_loaded"), 16)
            linear("incols")
            linear("inrows")
            linear("inlr", width=16)

            def gate(c, known):
                par = (STAGE["ingates"].acc_base + known) % 2
                wait("acc_summed", c + (STAGE["ingates"].acc_base + 1))
                nc.scalar.activation(gates[:, c, :, :], tsum[:, par, :, :], ACT.Sigmoid).then_inc(S("gate_ready"), 1)

            linear("ingates", post=gate)
            nc.scalar.activation(aux[:], inT[:, 4:8, :].rearrange("p (a b) t -> p a b t", a=2), ACT.Sigmoid).then_inc(S("og_sig"), 1)
            log_sigmoid(loga[:], za[:], zl[:], "lr_z", 1)
            for i in range(NL + 1):
                wait("gla_span", i + 1)
                if i >= 1:
                    wait("gla_qk", 2 * i)
                else:
                    wait("loga_ready", 1)
                nc.scalar.activation(decay[:], score[:, i % 2, :, :], ACT.Exp).then_inc(S("gla_exp"), 1)
            wait("gla_out", 1)
            wait("og_silu", 1)
            nc.scalar.activation(aux[:], score[:], ACT.Square).then_inc(S("gla_sq"), 1)
            skewed = bass.AP(tensor=skew_dram.tensor, offset=P - 1,
                             ap=[[SKEW - 1, P], [P * SKEW, G_HEADS], [1, 3 * P]])
            wait("gla_scores", NL + 2)
            act.dma_start(toep[:], skewed).then_inc(S("toep_loaded"), 16)
            wait("gla_var", 1)
            nc.scalar.activation(aux[:], tsum[:], ACT.Sqrt).then_inc(S("gla_root"), 1)
            wait("gla_o", 1)
            nc.scalar.activation(hA[:, 0:4, 0:T], o_gla[:], ACT.Copy).then_inc(S("gla_hi"), 1)
            attention("moba", float(P) ** -0.5, prob2, probT2, 4)
            hi = hidden_hi("branch", hM)
            linear("branch", post=lambda c, known: hi(c - 1, known - 1) if known >= 1 else None,
                   flush=lambda: hi(KT - 1, KT - 1))
            linear("out")
            norm("ffb", x, x_ready("out"), [hA], shift=6 * KT)
            gated_feed_forward("gu2", "dn2")
            norm("final2", x, x_ready("dn2"), [])

        @block.vector
        def _(dve):
            V = nc.vector

            def wait(sem, value):
                dve.wait_ge(S(sem), value)

            AHEAD = RING - 1

            def split_lo(st, c, known):
                n = st.base + known
                slot = n % RING
                wait("w_hi", c + (st.base + 1))
                e = elems_of(n)
                V.tensor_tensor(wsplit[:, slot, 1, 0:e], raw[:, slot, 0:e], wsplit[:, slot, 0, 0:e].bitcast(F32),
                                ALU.subtract).then_inc(S("w_lo"), 1)

            def total(st, a, known_a, dest=None, width=T):
                par = (st.acc_base + known_a) % 2
                wait("acc_low", a + (st.acc_base + 1))
                dst = tsum[:, par, :, :] if dest is None else dest
                V.tensor_tensor(dst, acc[:, par, :, 0:width], lowp[:, :, 0:width], ALU.add).then_inc(S("acc_summed"), 1)

            def linear(name, dest=None, before=None, early=None, post=None, flush=None, width=T, straight=False):
                st = STAGE[name]

                def body(c, known):
                    if before:
                        before(c, known)
                    last = known % st.per_acc == st.per_acc - 1
                    a, ka = (c, known) if st.per_acc == 1 else (known // st.per_acc, known // st.per_acc)
                    if last:
                        if dest is None:
                            done = st.base + known + AHEAD
                            wait("w_lo", N_CHUNKS if done >= N_CHUNKS else c + (st.base + AHEAD))
                        total(st, a, ka, dest(a) if dest else None, width)
                        if early:
                            early(a, ka)
                    if st.base + known + AHEAD < N_CHUNKS:
                        split_lo(st, c + AHEAD, known + AHEAD)
                    if last and post:
                        post(a, ka)

                if st.per_acc == 1 and not straight:
                    groups(dve, st.chunks, body, lead=RING, tail=RING)
                else:
                    for c in range(st.chunks):
                        body(c, c)
                if flush:
                    flush()

            def add_to_x(name, gain=None):
                st = STAGE[name]

                def post(a, ka):
                    par = (st.acc_base + ka) % 2
                    wait("acc_summed", st.acc_base + a + 1)
                    if gain is None:
                        last = V.tensor_tensor(x[:, 2 * a:2 * a + 2, :], x[:, 2 * a:2 * a + 2, :], tsum[:, par, :, :], ALU.add)
                    else:
                        for j in range(2):
                            kt = 2 * a + j
                            last = V.scalar_tensor_tensor(out=x[:, kt, :], in0=tsum[:, par, j, :],
                                                          scalar=mod[:, gain + kt:gain + kt + 1], in1=x[:, kt, :],
                                                          op0=ALU.mult, op1=ALU.add)
                    last.then_inc(S("x_updated"), 1)
                linear(name, post=post)

            def inverse_root(sem, n, v, r, tmp):
                V.reciprocal(tmp, r).then_inc(S(sem), 1)
                wait(sem, n + 1)
                V.scalar_tensor_tensor(out=r, in0=tmp, scalar=-0.5, in1=tmp, op0=ALU.mult, op1=ALU.mult).then_inc(S(sem), 1)
                wait(sem, n + 2)
                V.tensor_tensor(r, r, v, ALU.mult).then_inc(S(sem), 1)
                wait(sem, n + 3)
                V.scalar_tensor_tensor(out=r, in0=r, scalar=1.5, in1=tmp, op0=ALU.add, op1=ALU.mult).then_inc(S(sem), 1)
                wait(sem, n + 4)

            def norm_scale(name):
                q = norm_index(name)
                wait("norm_stat", PAIRS * (q + 1))
                V.tensor_scalar(var[:], stat[:, 0, :], 1.0 / D, RMS_EPS, ALU.mult, ALU.add).then_inc(S("norm_var"), 1)
                wait("norm_root", q + 1)
                inverse_root("norm_rstd", 4 * q, var[:], rstd[:], lowp[:, 0, :])

            def norm_apply(name, src, dest, gain, which=0, shift=None):
                nb = norm_base(name) + PAIRS * which

                def lo(p):
                    wait("norm_hi", nb + p + 1)
                    hi_ap = dest[:, 2 * p:2 * p + 2, 0:T].bitcast(F32)
                    if shift is None:
                        last = V.tensor_tensor(dest[:, 2 * p:2 * p + 2, T:2 * T], tsum[:, p % 2, :, :], hi_ap, ALU.subtract)
                    else:
                        for j in range(2):
                            kt = 2 * p + j
                            last = V.scalar_tensor_tensor(out=dest[:, kt, T:2 * T], in0=tsum[:, p % 2, j, :],
                                                          scalar=mod[:, shift + kt:shift + kt + 1],
                                                          in1=dest[:, kt, 0:T].bitcast(F32),
                                                          op0=ALU.add, op1=ALU.subtract)
                    last.then_inc(S("norm_lo"), 1)

                for p in range(PAIRS):
                    if which or p >= 2:
                        wait("norm_lo", nb + p - 1)
                    for j in range(2):
                        kt = 2 * p + j
                        last = V.scalar_tensor_tensor(out=tsum[:, p % 2, j, :], in0=src[:, kt, :], scalar=gain(kt),
                                                      in1=rstd[:], op0=ALU.mult, op1=ALU.mult)
                    last.then_inc(S("norm_h"), 1)
                    if p >= 1:
                        lo(p - 1)
                lo(PAIRS - 1)

            def norm(name, src, dests, shift=None):
                norm_scale(name)
                for i, (dest, gain) in enumerate(dests):
                    norm_apply(name, src, dest, gain, i, shift)

            def norm_in_place(name, sem):
                norm_scale(name)
                for p in range(PAIRS):
                    for j in range(2):
                        kt = 2 * p + j
                        last = V.scalar_tensor_tensor(out=x[:, kt, :], in0=x[:, kt, :],
                                                      scalar=col(name, kt),
                                                      in1=rstd[:], op0=ALU.mult, op1=ALU.mult)
                    last.then_inc(S(sem), 1)

            def lo_of(name, dest, pair):
                def lo(c, known):
                    wait(f"{name}_hi", c + 1)
                    par = (STAGE[name].acc_base + known) % 2
                    if pair:
                        d = hid[:].rearrange("p (c j) t -> p c j t", j=2)[:, c, :, :]
                        V.tensor_tensor(d[:, :, T:2 * T], tsum[:, par, :, :], d[:, :, 0:T].bitcast(F32),
                                        ALU.subtract).then_inc(S(f"{name}_lo"), 1)
                    else:
                        V.tensor_tensor(dest[:, c, T:2 * T], tsum[:, par, 0, :], dest[:, c, 0:T].bitcast(F32),
                                        ALU.subtract).then_inc(S(f"{name}_lo"), 1)
                return lo

            def feed_forward(up, down, segment):
                st = STAGE[up]
                lo = lo_of(up, hid, True)

                def square(c, known):
                    par = (st.acc_base + known) % 2
                    t = tsum[:, par, :, :]
                    wait("acc_summed", c + (st.acc_base + 1))
                    V.scalar_tensor_tensor(out=t, in0=t, scalar=0.0, in1=t, op0=ALU.max, op1=ALU.mult).then_inc(S(f"{up}_r"), 1)

                linear(up, early=lambda c, known: lo(c - 1, known - 1) if known >= 1 else None, post=square,
                       flush=lambda: lo(st.chunks - 1, st.chunks - 1))
                modulation(segment)
                add_to_x(down)

            def gated_feed_forward(gu, dn, gain):
                st = STAGE[gu]
                lo = lo_of(gu, hid, False)

                def gated(c, known):
                    par = (st.acc_base + known) % 2
                    t0, t1 = tsum[:, par, 0, :], tsum[:, par, 1, :]
                    wait(f"{gu}_sig", c + 1)
                    V.tensor_tensor(t0, t0, t1, ALU.mult).then_inc(S(f"{gu}_p"), 1)
                    wait(f"{gu}_p", c + 1)
                    V.tensor_tensor(t0, t0, aux[:, par, 0, :], ALU.mult).then_inc(S(f"{gu}_r"), 1)

                linear(gu, early=lambda c, known: lo(c - 1, known - 1) if known >= 1 else None, post=gated,
                       flush=lambda: lo(st.chunks - 1, st.chunks - 1))
                add_to_x(dn, gain)

            def plain(name, t):
                linear(name, dest=lambda a: t[:].rearrange("p (c j) t -> p c j t", j=2)[:, a, :, :])

            def rows(name, t):
                linear(name, dest=lambda a: t[:].rearrange("p r (c n) -> p r c n", n=T)[:, :, a, :])

            def attention(name, scale, prob, dest_tile):
                _, n_heads, n_groups = next(a for a in ATTENTIONS if a[0] == name)
                b, gb = head_base(name)
                per_group = n_heads // n_groups
                tiles = 2 if name.startswith("mem") else 1

                def largest(h):
                    wait("att_scores", b + h + 1)
                    V.tensor_reduce(small[:, 0, 2 * h:2 * h + 2], score[:, h % 2, :, :], AX.X, ALU.max).then_inc(S("att_max"), 1)
                    wait("att_max", 2 * (b + h) + 1)
                    V.tensor_scalar(small[:, 1, 2 * h:2 * h + 2], small[:, 0, 2 * h:2 * h + 2], -scale, None,
                                    ALU.mult).then_inc(S("att_max"), 1)

                def normalise(h):
                    wait("att_exp", b + h + 1)
                    V.reciprocal(small[:, 3, 2 * h:2 * h + 2], small[:, 2, 2 * h:2 * h + 2]).then_inc(S("att_inv"), 1)
                    wait("att_inv", b + h + 1)
                    V.tensor_tensor(prob[:, h % 2, :, :], prob[:, h % 2, :, :],
                                    small[:, 3, 2 * h:2 * h + 2].unsqueeze(2).to_broadcast([P, TT, T]),
                                    ALU.mult).then_inc(S("att_prob"), 1)

                def out_lo(g):
                    at = dest_tile + g * tiles
                    wait("att_hi", gb + g + 1)
                    V.tensor_tensor(hA[:, at:at + tiles, T:2 * T], stat[:, 0:tiles, :],
                                    hA[:, at:at + tiles, 0:T].bitcast(F32), ALU.subtract).then_inc(S("att_lo"), 1)

                largest(0)
                for h in range(n_heads):
                    if h + 1 < n_heads:
                        largest(h + 1)
                    normalise(h)
                    if h >= 1 and h % per_group == 0:
                        out_lo(h // per_group - 1)
                out_lo(n_groups - 1)

            def modulation(seg):
                wait("ada_used", seg + 1)
                V.tensor_tensor(mod[:, SEGMENT * seg:SEGMENT * (seg + 1)], stat[:, 1, 0:SEGMENT],
                                col("ada_b", SEGMENT * seg, SEGMENT), ALU.add).then_inc(S("mod_made"), 1)

            V.memset(upad[:, :, 0:PAD], 0.0).then_inc(S("pad_ready"), 1)
            for n in range(AHEAD):
                split_lo(PLAN[0], n, n)
            wait("consts_loaded", 16 * 7)
            norm("mix0", x, [(hA, lambda kt: col("mix0", kt))])

            steps = [(kt, tap) for kt in range(V_TILES) for tap in range(TAPS)]
            at_step = [0]

            def conv_taps(n):
                for _ in range(n):
                    if at_step[0] == len(steps):
                        return
                    kt, tap = steps[at_step[0]]
                    at_step[0] += 1
                    w = taps[:, tap, kt:kt + 1]
                    u = upad[:, kt, tap:tap + T]
                    if tap == 0:
                        wait("u_ready", kt + 1)
                        ins = V.tensor_scalar(conv[:, kt, :], u, w, col("dw_b", kt), ALU.mult, ALU.add)
                    else:
                        wait("conv_step", at_step[0] - 1)
                        ins = V.scalar_tensor_tensor(out=conv[:, kt, :], in0=u, scalar=w, in1=conv[:, kt, :],
                                                     op0=ALU.mult, op1=ALU.add)
                    ins.then_inc(S("conv_step"), 1)

            def glu(a, ka):
                wait("pw1_sig", a + 1)
                V.tensor_tensor(upad[:, a, PAD:PAD + T], tsum[:, ka % 2, 0, :], aux[:, ka % 2, 0, :],
                                ALU.mult).then_inc(S("u_ready"), 1)
                conv_taps(12 if a else 0)

            wait("pad_ready", 1)
            linear("pw1", post=glu, straight=True)
            norm("mem0", memx0, [(hM, lambda kt: col("src0", kt))])
            linear("memk0", dest=lambda a: mk0[:, 2 * a:2 * a + 2, :], post=lambda a, ka: conv_taps(12), straight=True)
            linear("memv0", dest=lambda a: mv0[:, :, a * T:(a + 1) * T], post=lambda a, ka: conv_taps(12), straight=True)
            conv_taps(len(steps))
            wait("conv_step", len(steps))
            for kt in range(V_TILES, KT):
                wait("conv_pool_step", (kt - V_TILES + 1) * (2 * TAPS - 1))
            wait("ln_stat", 1)
            V.tensor_scalar(mu[:], stat[:, 0, :], 1.0 / D, None, ALU.mult).then_inc(S("ln_mean"), 1)
            wait("ln_mean", 1)
            wait("conv_step", len(steps))
            for p in range(PAIRS):
                c2 = conv[:, 2 * p:2 * p + 2, :]
                V.tensor_tensor(c2, c2, spread(mu[:], 2), ALU.subtract).then_inc(S("ln_centred"), 1)
            wait("ln_stat", 1 + PAIRS)
            V.tensor_scalar(var[:], stat[:, 0, :], 1.0 / D, LN_EPS, ALU.mult, ALU.add).then_inc(S("ln_var"), 1)
            wait("ln_root", 1)
            wait("ln_centred", PAIRS)
            inverse_root("ln_rstd", 0, var[:], rstd[:], mu[:])

            def ln_lo(p):
                wait("ln_hi", p + 1)
                V.tensor_tensor(hA[:, 2 * p:2 * p + 2, T:2 * T], tsum[:, p % 2, :, :],
                                hA[:, 2 * p:2 * p + 2, 0:T].bitcast(F32), ALU.subtract).then_inc(S("ln_lo"), 1)

            for p in range(PAIRS):
                c2 = conv[:, 2 * p:2 * p + 2, :]
                V.tensor_tensor(c2, c2, spread(rstd[:], 2), ALU.mult).then_inc(S("ln_y"), 1)
                wait("ln_y", p + 1)
                if p >= 2:
                    wait("ln_lo", p - 1)
                for j in range(2):
                    kt = 2 * p + j
                    last = V.tensor_scalar(tsum[:, p % 2, j, :], conv[:, kt, :], col("ln_g", kt), col("ln_b", kt),
                                           ALU.mult, ALU.add)
                last.then_inc(S("ln_z"), 1)
                wait("ln_z", p + 1)
                wait("ln_sig", p + 1)
                V.tensor_tensor(tsum[:, p % 2, :, :], tsum[:, p % 2, :, :], aux[:, p % 2, :, :],
                                ALU.mult).then_inc(S("ln_r"), 1)
                if p >= 1:
                    ln_lo(p - 1)
            ln_lo(PAIRS - 1)
            add_to_x("pw2")
            modulation(0)
            norm("memq0", x, [(hA, lambda kt: col("memq0", kt))])
            plain("memq0", mq0)
            attention("mem0", 1 / 16, prob0, 0)
            add_to_x("memo0")
            modulation(1)
            norm("ff0", x, [(hA, lambda kt: col("ff0", kt))])
            feed_forward("up0", "down0", 2)
            modulation(3)

            norm("fox", x, [(hA, lambda kt: col("kv", kt)), (hB, lambda kt: col("mix1", kt))])
            plain("foxk", fk)
            rows("foxv", fv)
            linear("foxf", dest=lambda a: small[:, 0, :].rearrange("p (r n) -> p r n", r=TT), width=HEADS)
            wait("acc_summed", STAGE["foxf"].acc_base + 1)
            z = small[:, 0, :].rearrange("p (r n) -> p r n", r=TT)
            V.tensor_tensor(z, z, spread(col("fgate", 0, HEADS), TT), ALU.add).then_inc(S("fgate_z"), 1)
            plain("foxq", fq)
            modulation(4)
            norm("mem1", memx1, [(hA, lambda kt: col("src1", kt))])
            wait("fgate_z_ln", 3)
            V.scalar_tensor_tensor(out=small[:, 3, :], in0=small[:, 0, :], scalar=0.0, in1=small[:, 1, :],
                                   op0=ALU.min, op1=ALU.subtract).then_inc(S("logf_ready"), 1)
            plain("memk1", mk1)
            rows("memv1", mv1)
            wait("negc_made", 1)
            V.tensor_copy(negc[0:HEADS, :], turned[0:HEADS, 0, :]).then_inc(S("negc_ready"), 1)
            attention("fox", 1 / 8, prob1, 0)
            add_to_x("foxo")
            modulation(5)
            norm("memq1", x, [(hA, lambda kt: col("memq1", kt))])
            plain("memq1", mq1)
            attention("mem1", 1 / 16, prob1, 0)
            add_to_x("memo1")
            modulation(6)
            norm("ff1", x, [(hA, lambda kt: col("ff1", kt))])
            feed_forward("up1", "down1", 7)
            modulation(8)
            norm_in_place("final1", "x_updated")

            wait("mod_made", N_MOD)
            for seg, gain in ((1, "ffa"), (4, "mixn"), (7, "ffb")):
                m = mod[:, SEGMENT * seg:SEGMENT * (seg + 1)]
                V.scalar_tensor_tensor(out=m, in0=m, scalar=1.0, in1=col(gain, 0, KT), op0=ALU.add, op1=ALU.mult)
            for seg in (2, 8):
                m = mod[:, SEGMENT * seg:SEGMENT * (seg + 1)]
                last = V.tensor_scalar(m, m, 0.5, None, ALU.mult)
            last.then_inc(S("mod_used"), 1)
            wait("mod_used", 1)

            def modulated(seg):
                return lambda kt: mod[:, SEGMENT * seg + kt:SEGMENT * seg + kt + 1]

            norm("ffa", x, [(hA, modulated(1))], shift=0)
            gated_feed_forward("gu1", "dn1", 2 * SEGMENT)
            norm("mixn", x, [(hA, modulated(4))], shift=3 * SEGMENT)
            plain("incols", inT)
            rows("inrows", inV)
            V.memset(glrT[:], 1.0).then_inc(S("lr_turned"), 1)
            linear("inlr", dest=lambda a: small[:, 0, :].rearrange("p (r n) -> p r n", r=TT), width=16)
            wait("lr_turn", 1)
            wait("lr_turned", 1)
            V.tensor_copy(glrT[0:16, :], turned[0:16, 0, :]).then_inc(S("lr_turned"), 1)
            linear("ingates", before=lambda c, known: wait("gate_ready", c - 1) if known >= 2 else None)
            wait("og_sig", 1)
            og = inT[:, 4:8, :].rearrange("p (a b) t -> p a b t", a=2)
            V.tensor_tensor(og, og, aux[:], ALU.mult).then_inc(S("og_silu"), 1)
            wait("lr_logits", 1)
            V.tensor_copy(loga[:], turned[:]).then_inc(S("lr_z"), 1)
            wait("lr_z_ln", 3)
            V.scalar_tensor_tensor(out=loga[:], in0=loga[:], scalar=0.0, in1=za[:],
                                   op0=ALU.min, op1=ALU.subtract).then_inc(S("loga_ready"), 1)
            wait("gate_ready", KT)
            flat = tsum[:].rearrange("p a b t -> p (a b t)")
            product = flat.rearrange("p (n t) -> p n t", t=P)
            A_ps = [acc[:, i, :, :].rearrange("p a (b t) -> p (a b) t", b=4) for i in range(2)]
            for lv in range(NL + 1):
                wait("gla_scores", lv + 1)
                m = spread(lmask[:, lv, :], 2 * G_HEADS)
                if lv == 0:
                    V.tensor_tensor(A_same[:], A_ps[0], m, ALU.mult).then_inc(S("gla_masked"), 1)
                    continue
                wait("gla_masked", 2 * lv - 1)
                V.tensor_tensor(product, A_ps[lv % 2], m, ALU.mult).then_inc(S("gla_masked"), 1)
                wait("gla_masked", 2 * lv)
                V.tensor_tensor(A_same[:], A_same[:], product, ALU.add).then_inc(S("gla_masked"), 1)
            wait("gla_scores", NL + 2)
            V.tensor_scalar(A_next[:].rearrange("p (b h) t -> p b h t", b=2),
                            A_ps[(NL + 1) % 2].rearrange("p (b h) t -> p b h t", b=2)[:, :, 0:2, :],
                            1 / 8, None, ALU.mult).then_inc(S("gla_masked"), 1)
            wait("gla_stat", 1)
            wait("gla_masked", 2 * NL + 2)
            V.tensor_scalar(flat, acc[:, 0, :, :].rearrange("p a t -> p (a t)"), 1.0 / P, RMS_EPS, ALU.mult,
                            ALU.add).then_inc(S("gla_var"), 1)
            wait("gla_root", 1)
            auxf = aux[:].rearrange("p a b t -> p (a b t)")
            of = o_gla[:].rearrange("p a t -> p (a t)")
            inverse_root("gla_rstd", 0, flat, auxf, of)
            V.tensor_tensor(of, score[:].rearrange("p a b t -> p (a b t)"), auxf, ALU.mult).then_inc(S("gla_norm"), 1)
            wait("gla_norm", 1)
            V.scalar_tensor_tensor(out=of, in0=of, scalar=col("gla"), in1=inT[:, 4:8, :].rearrange("p a t -> p (a t)"),
                                   op0=ALU.mult, op1=ALU.mult).then_inc(S("gla_o"), 1)
            wait("gla_hi", 1)
            V.tensor_tensor(hA[:, 0:4, T:2 * T], o_gla[:], hA[:, 0:4, 0:T].bitcast(F32), ALU.subtract).then_inc(S("gla_lo"), 1)
            attention("moba", float(P) ** -0.5, prob2, 4)
            lo = lo_of("branch", hM, False)

            def merge(c, known):
                par = (STAGE["branch"].acc_base + known) % 2
                t = tsum[:, par, :, :]
                wait("acc_summed", c + (STAGE["branch"].acc_base + 1))
                V.tensor_tensor(t, t, gates[:, c, :, :], ALU.mult).then_inc(S("branch_p"), 1)
                wait("branch_p", c + 1)
                V.tensor_tensor(t[:, 0, :], t[:, 0, :], t[:, 1, :], ALU.add).then_inc(S("branch_r"), 1)

            linear("branch", early=lambda c, known: lo(c - 1, known - 1) if known >= 1 else None, post=merge,
                   flush=lambda: lo(KT - 1, KT - 1))
            add_to_x("out", 5 * SEGMENT)
            norm("ffb", x, [(hA, modulated(7))], shift=6 * SEGMENT)
            gated_feed_forward("gu2", "dn2", 8 * SEGMENT)
            norm_in_place("final2", "final_ready")

        @block.gpsimd
        def _(pool):
            G = nc.gpsimd

            def wait(sem, value):
                pool.wait_ge(S(sem), value)

            HALF_STEPS = 4

            def ada_load(m, half):
                pool.dma_start(ada_w[:, half, :, :], dram["ada"][m, half]).then_inc(ada_loaded[half], 16)

            def ada_tile(m, known, last):
                for half in range(2):
                    pool.wait_ge(ada_loaded[half], m * 16 + 16)
                    w = ada_w[:, half, :, :]
                    n = m * (2 * HALF_STEPS) + HALF_STEPS * half
                    G.tensor_tensor(w, w, cact[:].unsqueeze(2).to_broadcast([P, KT, HALF]), ALU.mult).then_inc(S("ada_step"), 1)
                    wait("ada_step", n + 1)
                    G.tensor_tensor(w[:, 0:4, :], w[:, 0:4, :], w[:, 4:8, :], ALU.add).then_inc(S("ada_step"), 1)
                    wait("ada_step", n + 2)
                    G.tensor_tensor(w[:, 0:2, :], w[:, 0:2, :], w[:, 2:4, :], ALU.add).then_inc(S("ada_step"), 1)
                    wait("ada_step", n + 3)
                    G.tensor_tensor(ada_acc[:, known % SEGMENT, half * HALF:(half + 1) * HALF], w[:, 0, :], w[:, 1, :],
                                    ALU.add).then_inc(S("ada_step"), 1)
                    if not last:
                        wait("ada_step", n + 4)
                        ada_load(m + 1, half)

            def ada_segment(seg, known, last=False):
                if known:
                    wait("ada_used", seg)
                for k in range(SEGMENT):
                    ada_tile(seg * SEGMENT + k, k, last and k == SEGMENT - 1)

            ada_load(0, 0)
            ada_load(0, 1)
            wait("consts_loaded", 16 * 7)
            wait("cond_sig", 1)
            G.tensor_tensor(cact[:], cact[:], col("cond", 0, KT), ALU.mult).then_inc(S("cond_silu"), 1)
            wait("cond_silu", 1)
            ada_segment(0, 0)
            n = 0
            for kt in range(V_TILES, KT):
                wait("u_ready", kt + 1)
                for tap in range(TAPS):
                    w = taps[:, tap, kt:kt + 1]
                    u = upad[:, kt, tap:tap + T]
                    if tap == 0:
                        G.tensor_scalar(conv[:, kt, :], u, w, col("dw_b", kt), ALU.mult, ALU.add).then_inc(S("conv_pool_step"), 1)
                        n += 1
                        continue
                    wait("conv_pool_step", n)
                    G.tensor_scalar(pool_tmp[:], u, w, None, ALU.mult).then_inc(S("conv_pool_step"), 1)
                    wait("conv_pool_step", n + 1)
                    G.tensor_tensor(conv[:, kt, :], conv[:, kt, :], pool_tmp[:], ALU.add).then_inc(S("conv_pool_step"), 1)
                    n += 2
            with pool.Fori(1, N_MOD - 1) as seg:
                ada_segment(seg, 1)
            ada_segment(N_MOD - 1, N_MOD - 1, True)
            for i in range(NL + 1):
                wait("gla_exp", i + 1)
                if i:
                    wait("gla_scores", i)
                G.tensor_tensor(qe[:], inT[:, 0:2, :], decay[:], ALU.mult).then_inc(S("gla_qk"), 1)
                G.tensor_tensor(ke[:], inT[:, 2:4, :], decay[:], ALU.mult).then_inc(S("gla_qk"), 1)


def bucket_of(dist):
    exact, far = BUCKETS // 2, 128
    if dist < exact:
        return dist
    return min(BUCKETS - 1, exact + int(np.log(dist / exact) / np.log(far / exact) * (BUCKETS - exact)))


def constants():
    i = np.arange(P)
    before = (i[:, None] <= i[None, :]).astype(np.float32)
    tri = np.zeros((P, TT, T), np.float32)
    tri[:, 0, :P], tri[:, 0, P:], tri[:, 1, P:] = before, 1, before
    spans = np.zeros((P, NL + 2, P), np.float32)
    lmask = np.zeros((P, NL + 1, P), np.float32)
    t, j = i[:, None], i[None, :]
    for lv, s in enumerate(LEVELS):
        mid = j // (2 * s) * (2 * s) + s - 1
        spans[:, lv, :] = ((t > j) & (t <= mid)) | ((t > mid) & (t <= j))
        lmask[:, lv, :] = (t // (2 * s) == j // (2 * s)) & (t % (2 * s) < s) & (j % (2 * s) >= s)
    spans[:, NL, :] = t > j
    spans[:, NL + 1, :] = t <= j
    lmask[:, NL, :] = t == j
    onehot = np.zeros((BUCKETS + 1, SKEW), np.float32)
    for c in range(SKEW):
        if c < T:
            onehot[bucket_of(T - 1 - c), c] = 1
        else:
            onehot[BUCKETS, c] = MASKED
    mask = np.full((P, 2 * P), MASKED, np.float32)
    mask[:, :P][i[:, None] >= i[None, :]] = 0
    return {
        "ones": np.ones((P, P), np.float32), "ident": np.eye(P, dtype=np.float32), "mask": mask,
        "tri": -8 * tri, "spans": spans / 16, "lmask": lmask / 8, "onehot": onehot,
    }


def tiles(w, k_tiles, columns):
    w3 = w.reshape(-1, P, w.shape[1])
    return np.stack([w3[kt][:, :, cs].transpose(1, 0, 2).reshape(P, -1) for kt, cs in zip(k_tiles, columns)])


def by_columns(w, width=256):
    n = w.shape[1] // width
    return tiles(w, [slice(None)] * n, [slice(c * width, (c + 1) * width) for c in range(n)])


def paired(w, step, n):
    return tiles(w, [slice(None)] * n, [np.r_[c * P:(c + 1) * P, (step + c) * P:(step + c + 1) * P] for c in range(n)])


def layout(a):
    def rows(v):
        return v.reshape(-1, P).T

    out = {}
    out["xT"] = a["x"][0].T.reshape(KT, P, T).transpose(1, 0, 2)
    out["memT"] = a["mem"][0].T.reshape(KT, P, T).transpose(1, 0, 2)
    vectors = {
        "mix0": a["norm_mix_g"][0], "mix1": a["norm_mix_g"][1], "memq0": a["norm_mem_g"][0],
        "memq1": a["norm_mem_g"][1], "src0": a["norm_memsrc_g"][0], "src1": a["norm_memsrc_g"][1],
        "ff0": a["norm_ff_g"][0], "ff1": a["norm_ff_g"][1], "pw1_b": a["conv_pw1_b"][0],
        "dw_b": a["conv_dw_b"][0], "ln_g": a["conv_ln_g"][0], "ln_b": a["conv_ln_b"][0],
        "pw2_b": a["conv_pw2_b"][0], "kv": a["kv_norm_g"], "final1": a["final_norm_g"],
        "ffa": a["norm_ff1_2"][0], "mixn": a["norm_mix_2"][0], "ffb": a["norm_ff2_2"][0],
        "final2": a["norm_final_2"], "gla": a["gla_norm_2"][0], "ada_b": a["b_ada_2"][0], "cond": a["c_2"][0],
    }
    packed = [rows(vectors[name]) if name in vectors else np.broadcast_to(a["fgate_b"], (P, HEADS))
              for name, _ in COLUMNS]
    out["cols"] = np.concatenate(packed, axis=1)
    out["taps"] = a["conv_dw_w"][0].reshape(TAPS, KT, P).transpose(2, 0, 1)
    out["relT"] = np.concatenate([a["rel_bias_2"].T, np.ones((1, G_HEADS), np.float32)])
    out["wlr"] = np.concatenate([a["w_gla_lr_2"][0], a["b_gla_lr_2"][0][None]])
    out["ada"] = a["w_ada_2"][0].reshape(KT, P, N_MOD * KT, 2, HALF).transpose(2, 3, 1, 0, 4)

    out["pw1"] = paired(a["conv_pw1_w"][0], KT, KT)
    out["pw2"] = by_columns(a["conv_pw2_w"][0])
    for layer in range(2):
        for s in "qkvo":
            out[f"mem{s}{layer}"] = by_columns(a[f"mem_w{s}"][layer])
        out[f"up{layer}"] = by_columns(a["ff_w1"][layer])
        out[f"down{layer}"] = tiles(a["ff_w2"][layer], [slice(q * KT, (q + 1) * KT) for _ in range(4) for q in range(4)],
                                    [slice(c * 256, (c + 1) * 256) for c in range(4) for _ in range(4)])
    kvf = a["kvf_w"]
    out["foxk"], out["foxv"], out["foxf"] = by_columns(kvf[:, :D]), by_columns(kvf[:, D:2 * D]), by_columns(kvf[:, 2 * D:], HEADS)
    out["foxq"], out["foxo"] = by_columns(a["fox_wq"][0]), by_columns(a["fox_wo"][0])
    for i in (1, 2):
        gu = np.concatenate([a[f"w_ff{i}_gate_2"][0], a[f"w_ff{i}_up_2"][0]], axis=1)
        out[f"gu{i}"] = paired(gu, KF2, KF2)
        out[f"dn{i}"] = tiles(a[f"w_ff{i}_down_2"][0], [slice(11 * (q % 2), 11 * (q % 2) + 11) for _ in range(4) for q in range(4)],
                              [slice(m * P, (m + 1) * P) for c in range(4) for m in (2 * c, 2 * c, 2 * c + 1, 2 * c + 1)])
    w = a["w_in_2"][0]
    sizes = [256, 256, 512, 16, 512, 512, 512, 512, D, D]
    gq, gk, gv, glr, gog, mq, mk, mv, ga, gb = np.split(w, np.cumsum(sizes)[:-1], axis=1)
    out["incols"] = by_columns(np.concatenate([gq, gk, gog, mq, mk], axis=1))
    out["inrows"] = by_columns(np.concatenate([gv, mv], axis=1))
    out["inlr"] = by_columns(glr, 16)
    out["ingates"] = paired(np.concatenate([ga, gb], axis=1), KT, KT)
    out["branch"] = by_columns(np.concatenate([a["w_br_gla_2"][0], a["w_br_moba_2"][0]]), P)
    out["out"] = by_columns(a["w_out_2"][0])
    out.update(constants())
    return out


def kernel(**inputs):
    import concourse.bacc as bacc
    import ml_dtypes
    from concourse.bass_utils import run_bass_kernel_spmd

    nc = bacc.Bacc("TRN2", target_bir_lowering=False, num_devices=1)
    arrays = {k: np.ascontiguousarray(v) for k, v in layout({k: np.asarray(v) for k, v in inputs.items()}).items()}
    arrays["mask"] = arrays["mask"].astype(ml_dtypes.bfloat16)
    dram = {}
    for name, v in arrays.items():
        dram[name] = nc.dram_tensor(f"in_{name}", v.shape, mybir.dt.from_np(v.dtype), kind="ExternalInput").ap()
    out = nc.dram_tensor("out_xT", (P, KT, T), F32, kind="ExternalOutput").ap()
    program(nc, dram, out)
    r = run_bass_kernel_spmd(nc, [{f"in_{k}": v for k, v in arrays.items()}], core_ids=[0])
    got = np.asarray(r.results[0]["out_xT"])
    return np.ascontiguousarray(got.transpose(1, 0, 2).reshape(D, T).T)[None]
```

```python
from contextlib import ExitStack

import numpy as np

import concourse.bass as bass
from concourse import mybir

F32 = mybir.dt.float32
F32R = mybir.dt.float32r
BF16 = mybir.dt.bfloat16
ACT = mybir.ActivationFunctionType
ALU = mybir.AluOpType
AX = mybir.AxisListType

P = 128
D = 1024
T = 256
KT = D // P
PAIRS = KT // 2
TT = T // P
FF = 4096
KF = FF // P
FF2 = 2816
KF2 = FF2 // P
TAPS = 31
PAD = TAPS - 1
HEADS = 16
MEM_HEADS = 4
G_HEADS = 4
RMS_EPS = 1e-6
LN_EPS = 1e-5
RING = 4
MASKED = -1e30
LEVELS = [64, 32, 16, 8, 4, 2, 1]
NL = len(LEVELS)
SEGMENT = KT
N_MOD = 9
HALF = P // 2
SKEW = 512
BUCKETS = 32
V_TILES = 6

COLUMNS = [
    ("mix0", KT), ("mix1", KT), ("memq0", KT), ("memq1", KT), ("src0", KT), ("src1", KT),
    ("ff0", KT), ("ff1", KT), ("pw1_b", 2 * KT), ("dw_b", KT), ("ln_g", KT), ("ln_b", KT),
    ("pw2_b", KT), ("kv", KT), ("final1", KT), ("ffa", KT), ("mixn", KT), ("ffb", KT),
    ("final2", KT), ("gla", 1), ("ada_b", N_MOD * KT), ("cond", KT), ("fgate", HEADS),
    ("rms_eps", 1), ("ln_eps", 1),
]
COL = {}
_at = 0
for _name, _n in COLUMNS:
    COL[_name] = _at
    _at += _n
NCOL = _at


class Stage:

    def __init__(self, name, kind, chunks, elems, per_acc=1):
        self.name, self.kind, self.chunks, self.elems, self.per_acc = name, kind, chunks, elems, per_acc
        self.accs = chunks // per_acc


def plan():
    full = KT * 256
    seq = [
        Stage("pw1", "cols", 8, full), Stage("memk0", "cols", 4, full), Stage("memv0", "rows", 4, full),
        Stage("pw2", "cols", 4, full), Stage("memq0", "cols", 4, full), Stage("memo0", "cols", 4, full),
        Stage("up0", "cols", 16, full), Stage("down0", "deep32", 16, full, 4),
        Stage("foxk", "cols", 4, full), Stage("foxv", "rows", 4, full), Stage("foxf", "rows16", 1, KT * 16),
        Stage("foxq", "cols", 4, full),
        Stage("memk1", "cols", 4, full), Stage("memv1", "rows", 4, full),
        Stage("foxo", "cols", 4, full), Stage("memq1", "cols", 4, full), Stage("memo1", "cols", 4, full),
        Stage("up1", "cols", 16, full), Stage("down1", "deep32", 16, full, 4),
        Stage("gu1", "cols", KF2, full), Stage("dn1", "deep22", 16, 11 * P, 4),
        Stage("incols", "cols", 8, full), Stage("inrows", "rows", 4, full), Stage("inlr", "rows16", 1, KT * 16),
        Stage("ingates", "cols", 8, full), Stage("branch", "branch", 8, KT * P), Stage("out", "cols", 4, full),
        Stage("gu2", "cols", KF2, full), Stage("dn2", "deep22", 16, 11 * P, 4),
    ]
    base = acc = 0
    for s in seq:
        s.base, s.acc_base = base, acc
        base += s.chunks
        acc += s.accs
    return seq


PLAN = plan()
STAGE = {s.name: s for s in PLAN}
N_CHUNKS = PLAN[-1].base + PLAN[-1].chunks

X_UPDATES = ["pw2", "memo0", "down0", "foxo", "memo1", "down1", "final1", "dn1", "out", "dn2"]
NORMS = [("mix0", 1), ("mem0", 1), ("memq0", 1), ("ff0", 1), ("fox", 2), ("mem1", 1), ("memq1", 1),
         ("ff1", 1), ("final1", 0), ("ffa", 1), ("mixn", 1), ("ffb", 1), ("final2", 0)]
ATTENTIONS = [("mem0", MEM_HEADS, MEM_HEADS), ("fox", HEADS, HEADS // 2), ("mem1", MEM_HEADS, MEM_HEADS),
              ("moba", G_HEADS, G_HEADS)]


def elems_of(n):
    return next(s.elems for s in PLAN if s.base <= n < s.base + s.chunks)


def x_base(name):
    return PAIRS * X_UPDATES.index(name)


def norm_index(name):
    return [n for n, _ in NORMS].index(name)


def norm_base(name):
    return PAIRS * sum(k for _, k in NORMS[:norm_index(name)])


def head_base(name):
    i = [a[0] for a in ATTENTIONS].index(name)
    return sum(a[1] for a in ATTENTIONS[:i]), sum(a[2] for a in ATTENTIONS[:i])


def gla_at(h):
    return 2 * (h % 2) + h // 2


def spread(ap, n):
    return ap.unsqueeze(1).to_broadcast([ap.shape[0], n, ap.shape[1]])


def program(nc, dram, out):
    ctx = ExitStack()
    with ctx:
        cursor = [-(-nc.sbuf_base // 32) * 32]

        def place(name, shape, dt=F32, at=None):
            size = int(np.prod(shape[1:])) * (2 if dt == BF16 else 4)
            if at is None:
                at = cursor[0]
                cursor[0] += -(-size // 32) * 32
            return nc.alloc_sbuf_tensor_at(name, shape, dt, offset=at)

        raw = place("raw", [P, RING, KT * 256])
        wsplit = place("wsplit", [P, RING, 2, KT * 256], F32R)
        x = place("x", [P, KT, T])
        hA = place("hA", [P, KT, 2 * T], F32R)
        tsum = place("tsum", [P, 2, 2, T])
        aux = place("aux", [P, 2, 2, T])
        lowp = place("lowp", [P, 2, T])
        rstd = place("rstd", [P, T])
        var = place("var", [P, T])
        cols = place("cols", [P, NCOL])
        mod = place("mod", [P, N_MOD * KT])
        cact = place("cact", [P, KT])
        ones = place("ones", [P, P])
        ident = place("ident", [P, P])
        ident_bf = place("ident_bf", [P, P], BF16)
        mask_bf = place("mask_bf", [P, 2 * P], BF16)
        ones_bf = place("ones_bf", [3, P], BF16)
        small = place("small", [P, 4, TT * HEADS])
        ada_w = place("ada_w", [P, 2, KT, HALF])
        ada_acc = place("ada_acc", [P, SEGMENT, P])

        region = cursor[0]
        KB = 1024

        def phased(name, shape, kb, dt=F32):
            return place(name, shape, dt, at=region + int(kb * KB))

        hid = phased("hid", [P, KF, 2 * T], 0, F32R)
        hM = phased("hM", [P, KT, 2 * T], 0, F32R)
        memx0 = phased("memx0", [P, KT, T], 16)
        mk0 = phased("mk0", [P, KT, T], 24)
        mv0 = phased("mv0", [P, TT, D], 32)
        upad = phased("upad", [P, KT, PAD + T], 40)
        conv = phased("conv", [P, KT, T], 49)
        taps = phased("taps", [P, TAPS, KT], 57)
        mu = phased("mu", [P, T], 58)
        relrep = phased("relrep", [BUCKETS + 1, G_HEADS, P], 59)
        onehot = phased("onehot", [BUCKETS + 1, SKEW], 61)
        relT = phased("relT", [BUCKETS + 1, G_HEADS], 57.96875)
        pool_tmp = phased("pool_tmp", [P, T], 63)
        mq0 = phased("mq0", [P, KT, T], 40)
        prob0 = phased("prob0", [P, 2, TT, T], 49)
        probT0 = phased("probT0", [P, 2, TT, T], 53)
        hB = phased("hB", [P, KT, 2 * T], 0, F32R)
        memx1 = phased("memx1", [P, KT, T], 16)
        mk1 = phased("mk1", [P, KT, T], 24)
        mv1 = phased("mv1", [P, TT, D], 32)
        fq = phased("fq", [P, KT, T], 40)
        fk = phased("fk", [P, KT, T], 48)
        fv = phased("fv", [P, TT, D], 56)
        fo = phased("fo", [P, 2, KT, T], 40, F32R)
        negc_row = phased("negc_row", [3, HEADS, T], 0, BF16)
        tri = phased("tri", [P, TT, T], 32)
        negc = phased("negc", [P, T], 34)
        negc_part = phased("negc_part", [P, 3, T], 35, BF16)
        prob1 = phased("prob1", [P, 2, TT, T], 16)
        probT1 = phased("probT1", [P, 2, TT, T], 20)
        mq1 = phased("mq1", [P, KT, T], 40)
        inT = phased("inT", [P, 16, T], 0)
        inV = phased("inV", [P, TT, D], 16)
        gates = phased("gates", [P, KT, 2, T], 24)
        loga = phased("loga", [P, TT, T], 40)
        wlr = phased("wlr", [17, T], 42)
        decay = phased("decay", [P, 2, T], 42)
        qe = phased("qe", [P, 2, T], 44)
        ke = phased("ke", [P, 2, T], 46)
        za = phased("za", [P, TT, T], 44)
        zl = phased("zl", [P, TT, T], 46)
        A_same = phased("A_same", [P, 2 * G_HEADS, P], 48)
        A_next = phased("A_next", [P, G_HEADS, P], 52)
        spans = phased("spans", [P, NL + 2, P], 54)
        lmask = phased("lmask", [P, NL + 1, P], 58.5)
        glrT = phased("glrT", [32, T], 62.5)
        o_gla = phased("o_gla", [P, G_HEADS, T], 48)
        toep = phased("toep", [P, G_HEADS, 3 * P], 42)
        prob2 = phased("prob2", [P, 2, TT, T], 54)
        probT2 = phased("probT2", [P, 2, TT, T], 58)
        assert region + 64 * KB <= nc.sbuf_usable_end, (region + 64 * KB, nc.sbuf_usable_end)

        def pb(name, shape):
            return ctx.enter_context(nc.psum_tensor(name, shape, F32))

        acc = pb("acc", [P, 2, 2, 2 * T])
        score = pb("score", [P, 2, TT, T])
        turned = pb("turned", [P, TT, T])
        stat = pb("stat", [P, 2, T])

        skew_dram = nc.dram_tensor("skew_dram", (G_HEADS, P, SKEW), F32, kind="Internal").ap()

        sems = {}

        def S(name):
            if name not in sems:
                sems[name] = ctx.enter_context(nc.semaphore(name))
            return sems[name]

        def col(name, i=0, n=1):
            return cols[:, COL[name] + i:COL[name] + i + n]

        raw_loaded = [S(f"raw_loaded{i}") for i in range(RING)]
        ada_loaded = [S(f"ada_loaded{i}") for i in range(2)]

        def groups(eng, n_chunks, body, unroll=RING, lead=0, tail=0, begun=0):
            first = lead
            last = max(first, (n_chunks - tail) // unroll * unroll)
            if last - first < 2 * unroll:
                first = last = begun
            for c in range(begun, first):
                body(c, c)
            if last > first:
                with eng.Fori(first // unroll, last // unroll) as i:
                    for k in range(unroll):
                        body(i * unroll + k, first + k)
            for c in range(last, n_chunks):
                body(c, c)

        def memory_between(keys, values):
            chunks = [(keys, c) for c in range(1, 4)] + [(values, c) for c in range(4)]
            return {2 * i: (lambda f=f, c=c: f(c, c)) for i, (f, c) in enumerate(chunks)}

        block = ctx.enter_context(nc.Block())

        @block.sync
        def _(sp):
            sp.dma_start(x[:], dram["xT"]).then_inc(S("x_loaded"), 16)
            sp.dma_start(cols[:], dram["cols"]).then_inc(S("consts_loaded"), 16)
            sp.dma_start(ones[:], dram["ones"]).then_inc(S("consts_loaded"), 16)
            sp.dma_start(ident[:], dram["ident"]).then_inc(S("consts_loaded"), 16)
            sp.dma_start(taps[:], dram["taps"]).then_inc(S("consts_loaded"), 16)
            sp.dma_start(onehot[:], dram["onehot"]).then_inc(S("consts_loaded"), 16)
            sp.dma_start(relT[:], dram["relT"]).then_inc(S("consts_loaded"), 16)
            sp.dma_start(mask_bf[:], dram["mask"]).then_inc(S("consts_loaded"), 16)
            sp.dma_start(memx0[:], dram["memT"]).then_inc(S("mem_loaded"), 16)

            def load(st, c, known):
                slot = (st.base + known) % RING
                if st.base + known >= RING:
                    sp.wait_ge(S("w_lo"), c + (st.base - RING + 1))
                sp.dma_start(raw[:, slot, 0:st.elems], dram[st.name][c]).then_inc(raw_loaded[slot], 16)

            for st in PLAN:
                groups(sp, st.chunks, lambda c, known: load(st, c, known), lead=RING if st.base == 0 else 0)
            for p in range(PAIRS):
                sp.wait_ge(S("final_ready"), p + 1)
                sp.dma_start(out[:, 2 * p:2 * p + 2, :], x[:, 2 * p:2 * p + 2, :]).then_inc(S("stored"), 16)
            sp.wait_ge(S("stored"), 16 * PAIRS)

        @block.tensor
        def _(pe):
            def weights_ready(st, c):
                pe.wait_ge(S("w_hi"), c + (st.base + 1))
                pe.wait_ge(S("w_lo"), c + (st.base + 1))

            def acc_free(st, a, known_a):
                if st.acc_base + known_a >= 2:
                    pe.wait_ge(S("acc_summed"), a + (st.acc_base - 1))

            def tile_of(hl):
                return lambda kt: hl[:, kt, :].rearrange("p (s t) -> p s t", s=2)

            def block_cols(dst, w, lo_w, h, start, stop):
                nc.tensor.matmul(dst.rearrange("p (s t) -> p s t", s=2), w, h, start=start, stop=False,
                                 skip_group_check=True)
                return nc.tensor.matmul(dst[:, 0:T], lo_w, h[:, 0, :], start=False, stop=stop,
                                        skip_group_check=True)

            def chunk_cols(st, slot, par, h, kts, cols_of, start, stop, ready):
                for i, kt in enumerate(kts):
                    if ready and kt in ready:
                        for sem, value in ready[kt]:
                            pe.wait_ge(sem, value)
                    for j, at in cols_of(i):
                        mm = block_cols(acc[:, par, j, :], wsplit[:, slot, 0, at:at + P],
                                        wsplit[:, slot, 1, at:at + P], h(kt),
                                        start and i == 0, stop and i == len(kts) - 1)
                return mm

            def linear(name, h, ready, after=None, steps=False):
                st = STAGE[name]
                h = h if callable(h) else tile_of(h)

                def body(c, known):
                    slot = (st.base + known) % RING
                    kt_all = list(range(KT))
                    if st.per_acc == 1:
                        a, known_a, q = c, known, 0
                    else:
                        q = known % st.per_acc
                        a, known_a = None, known // st.per_acc
                    weights_ready(st, c)
                    par = (st.acc_base + known_a) % 2
                    if st.per_acc == 1:
                        acc_free(st, a, known_a)
                    elif q == 0:
                        acc_free(st, known_a, known_a)
                    w = wsplit[:, slot, :, :]
                    if st.kind == "cols":
                        mm = chunk_cols(st, slot, par, h, kt_all,
                                        lambda i: [(j, i * 2 * P + j * P) for j in range(2)],
                                        True, True, ready)
                    elif st.kind == "deep32":
                        mm = chunk_cols(st, slot, par, h, [q * KT + i for i in range(KT)],
                                        lambda i: [(j, i * 2 * P + j * P) for j in range(2)],
                                        q == 0, q == 3, ready)
                    elif st.kind == "deep22":
                        mm = chunk_cols(st, slot, par, h, [(q % 2) * 11 + i for i in range(11)],
                                        lambda i: [(q // 2, i * P)], q % 2 == 0, q % 2 == 1, ready)
                    elif st.kind == "branch":
                        for br in range(2):
                            mm = chunk_cols(st, slot, par, h, [4 * br + i for i in range(4)],
                                            lambda i: [(br, (4 * br + i) * P)], True, True, ready)
                    else:
                        n = 256 if st.kind == "rows" else HEADS
                        for kt in range(KT):
                            if ready and kt in ready:
                                for sem, value in ready[kt]:
                                    pe.wait_ge(sem, value)
                            for tt in range(TT):
                                dst = acc[:, par, tt, 0:2 * n]
                                nc.tensor.matmul(dst.rearrange("p (s n) -> p s n", s=2),
                                                 h(kt)[:, 0, tt * P:(tt + 1) * P],
                                                 w[:, :, kt * n:(kt + 1) * n],
                                                 start=kt == 0, stop=False, skip_group_check=True)
                                mm = nc.tensor.matmul(dst[:, 0:n], h(kt)[:, 1, tt * P:(tt + 1) * P],
                                                      w[:, 0, kt * n:(kt + 1) * n],
                                                      start=False, stop=kt == KT - 1,
                                                      skip_group_check=True)
                    mm.then_inc(S("chunk_done"), 1)
                    if after and (st.per_acc > 1 or known < RING):
                        after(known)

                def part(c, p):
                    slot, par = (st.base + c) % RING, (st.acc_base + c) % 2
                    if p == 0:
                        weights_ready(st, c)
                        acc_free(st, c, c)
                    mm = chunk_cols(st, slot, par, h, [2 * p, 2 * p + 1],
                                    lambda i: [(j, (2 * p + i) * 2 * P + j * P) for j in range(2)],
                                    p == 0, p == PAIRS - 1, ready)
                    if p == PAIRS - 1:
                        mm.then_inc(S("chunk_done"), 1)
                        if after:
                            after(c)

                def begin():
                    for c, p in ((0, 0), (1, 0), (0, 1), (1, 1), (0, 2), (0, 3), (1, 2), (1, 3)):
                        part(c, p)

                if steps:
                    return begin, body
                if st.per_acc > 1:
                    for c in range(st.chunks):
                        body(c, c)
                elif st.kind == "cols" and ready:
                    begin()
                    groups(pe, st.chunks, body, lead=RING, begun=2)
                else:
                    groups(pe, st.chunks, body, lead=RING)

            def pair_ready(base):
                return {2 * p: [(S("norm_lo"), base + p + 1)] for p in range(PAIRS)}

            def norm_sums(name, pairs=range(PAIRS)):
                q = norm_index(name)
                for p in pairs:
                    pe.wait_ge(S("norm_sq"), PAIRS * q + p + 1)
                    if p == 0 and q > 0:
                        stat_read(q)
                    for j in range(2):
                        mm = nc.tensor.matmul(stat[:, 0, :], ones[:], aux[:, p % 2, j, :],
                                              start=p == 0 and j == 0, stop=p == PAIRS - 1 and j == 1)
                    mm.then_inc(S("norm_stat"), 1)

            def stat_read(q):
                pe.wait_ge(S("norm_var"), q)

            segments_summed = [0]

            def modulation_read():
                if segments_summed[0]:
                    pe.wait_ge(S("mod_made"), segments_summed[0])

            def residual(name, h, ready, norm, segments={}):
                per = STAGE[name].per_acc
                lag = 2 if per == 1 else 1
                early = []

                def after(c):
                    if c in segments:
                        ada(segments[c])
                    if (c + 1 - lag) % per == 0 and c + 1 > lag:
                        early.append((c + 1 - lag) // per - 1)
                        norm_sums(norm, early[-1:])

                linear(name, h, ready, after=after)
                norm_sums(norm, range(len(early), PAIRS))

            def ada(seg):
                pe.wait_ge(S("ada_step"), 64 * (seg + 1))
                modulation_read()
                for m in range(SEGMENT):
                    mm = nc.tensor.matmul(turned[:, 0, m:m + 1], ada_acc[:, m, :], ones[:, 0:1],
                                          start=True, stop=True)
                mm.then_inc(S("ada_used"), 1)
                segments_summed[0] += 1

            def attention(name, q, k, v, prob, probT, extra, dh, ready, leads=(), between={}):
                _, n_heads, n_groups = next(a for a in ATTENTIONS if a[0] == name)
                b, gb = head_base(name)
                per_group = n_heads // n_groups
                causal = extra is not None

                def scores(h):
                    for sem, value in ready.get(h, []):
                        pe.wait_ge(sem, value)
                    if b + h >= 2:
                        pe.wait_ge(S("att_exp"), b + h - 1)
                    if causal:
                        extra(h)
                    off = (h * dh) % P
                    rows = min(dh, P)
                    tiles = [h * dh // P + i for i in range(max(1, dh // P))]
                    for qt in range(TT):
                        keys = P * (qt + 1) if causal else T
                        for i, kt in enumerate(tiles):
                            mm = nc.tensor.matmul(score[:, h % 2, qt, 0:keys],
                                                  q[off:off + rows, kt, qt * P:(qt + 1) * P],
                                                  k[off:off + rows, kt, 0:keys],
                                                  start=not causal and i == 0, stop=i == len(tiles) - 1,
                                                  skip_group_check=True)
                    mm.then_inc(S("att_scores"), 1)

                def queries(kt):
                    first = P * kt if causal else 0
                    return first, T * kt - first

                def turn(h):
                    pe.wait_ge(S("att_prob"), b + h + 1)
                    if b + h >= 1:
                        pe.wait_ge(S("att_turned"), b + h)
                    flat = turned[:].rearrange("p a t -> p (a t)")
                    for kt in range(TT):
                        first, at = queries(kt)
                        for qt in range(first // P, TT):
                            mm = nc.tensor.transpose(flat[:, at + qt * P:at + (qt + 1) * P],
                                                     prob[:, h % 2, qt, kt * P:(kt + 1) * P], ident[:])
                    mm.then_inc(S("att_turn"), 1)

                def values(h):
                    pe.wait_ge(S("att_turned"), b + h + 1)
                    g = h // per_group
                    if h % per_group == 0 and gb + g >= 1:
                        pe.wait_ge(S("att_lo"), gb + g)
                    weights = probT[:, h % 2, :, :].rearrange("p a t -> p (a t)")
                    off = (h * dh) % P
                    rows = min(dh, P)
                    for dt in range(max(1, dh // P)):
                        for kt in range(TT):
                            first, at = queries(kt)
                            mm = nc.tensor.matmul(stat[off:off + rows, dt, first:T],
                                                  v(kt, h * dh + dt * P, rows), weights[:, at + first:at + T],
                                                  start=kt == 0, stop=kt == TT - 1, skip_group_check=True)
                    mm.then_inc(S("att_out"), 1)

                leads = list(leads) + [None] * 3
                for i in range(2):
                    if leads[i]:
                        leads[i]()
                    if i == 0:
                        modulation_read()
                    scores(i)
                if leads[2]:
                    leads[2]()
                for h in range(n_heads):
                    turn(h)
                    if h + 2 < n_heads:
                        scores(h + 2)
                    if h in between:
                        between[h]()
                    values(h)

            def memory_attention(layer, hl, q, k, v, prob, probT):
                st = STAGE[f"memq{layer}"]
                begin, chunk = linear(st.name, hl, pair_ready(norm_base(st.name)), steps=True)
                attention(f"mem{layer}", q, k, lambda kt, at, n: v[:, kt, at:at + n], prob, probT, None, 256,
                          {h: [(S("acc_summed"), st.acc_base + h + 1)] for h in range(MEM_HEADS)},
                          leads=[begin, lambda: chunk(2, 2), lambda: chunk(3, 3)])

            pe.wait_ge(S("consts_loaded"), 16 * 7)
            norm_sums("mix0")
            linear("pw1", hA, pair_ready(norm_base("mix0")))
            norm_sums("mem0")
            linear("memk0", hM, pair_ready(norm_base("mem0")))
            linear("memv0", hM, None)
            pe.wait_ge(S("rel_spread"), 1)
            for h in range(G_HEADS):
                if h:
                    pe.wait_ge(S("rel_copied"), h)
                nc.tensor.matmul(turned[:].rearrange("p a b -> p (a b)"), relrep[:, h, :], onehot[:],
                                 start=True, stop=True).then_inc(S("rel_made"), 1)
            pe.wait_ge(S("conv_step"), V_TILES * TAPS)
            pe.wait_ge(S("conv_pool_step"), (KT - V_TILES) * (2 * TAPS - 1))
            stat_read(norm_index("mem0") + 1)
            for kt in range(KT):
                mm = nc.tensor.matmul(stat[:, 0, :], ones[:], conv[:, kt, :], start=kt == 0, stop=kt == KT - 1)
            mm.then_inc(S("ln_stat"), 1)
            for p in range(PAIRS):
                pe.wait_ge(S("ln_sq"), p + 1)
                for j in range(2):
                    mm = nc.tensor.matmul(stat[:, 0, :], ones[:], aux[:, p % 2, j, :],
                                          start=p == 0 and j == 0, stop=p == PAIRS - 1 and j == 1)
                mm.then_inc(S("ln_stat"), 1)
            residual("pw2", hA, {2 * p: [(S("ln_lo"), p + 1)] for p in range(PAIRS)}, "memq0")
            memory_attention(0, hA, mq0, mk0, mv0, prob0, probT0)
            gb = head_base("mem0")[1]
            residual("memo0", hA, {2 * p: [(S("att_lo"), gb + p + 1)] for p in range(PAIRS)}, "ff0", {0: 0})
            linear("up0", hA, pair_ready(norm_base("ff0")))
            residual("down0", hid, {2 * c: [(S("up0_lo"), c + 1)] for c in range(KF // 2)}, "fox", {0: 1, 12: 2})

            nb = norm_base("fox")
            linear("foxk", hA, pair_ready(nb))
            linear("foxv", hA, None, after=lambda c: norm_sums("mem1", [2 * c, 2 * c + 1]) if c < 2 else None)
            linear("foxf", hA, None)

            def behind_queries(c):
                if c == 0:
                    ada(3)
                elif c == 2:
                    pe.wait_ge(S("logf_ready"), 1)
                    pe.wait_ge(S("tri_loaded"), 16)
                    modulation_read()
                    for tt in range(TT):
                        mm = nc.tensor.matmul(turned[0:HEADS, 0, :], small[:, 3, tt * HEADS:(tt + 1) * HEADS],
                                              tri[:, tt, :], start=tt == 0, stop=tt == TT - 1)
                    mm.then_inc(S("negc_made"), 1)

            linear("foxq", hB, pair_ready(nb + PAIRS), after=behind_queries)

            def fox_bias(h):
                bank = score[:, h % 2, :, :]
                nc.tensor.matmul(bank[:, 0, :], ident_bf[:], mask_bf[:], start=True, stop=False,
                                 skip_group_check=True)
                nc.tensor.matmul(bank[:, 1, P:T], ident_bf[:], mask_bf[:, 0:P], start=False, stop=False,
                                 skip_group_check=True)
                for qt in range(TT):
                    keys = P * (qt + 1)
                    nc.tensor.matmul(bank[:, qt, 0:keys], ones_bf[0:3, :], negc_row[0:3, h, 0:keys],
                                     start=False, stop=False, skip_group_check=True)

            _, memory_keys = linear("memk1", hA, pair_ready(norm_base("mem1")), steps=True)
            _, memory_values = linear("memv1", hA, None, steps=True)
            s = STAGE["foxq"]
            attention("fox", fq, fk, lambda kt, at, n: fv[:, kt, at:at + n], prob1, probT1, fox_bias, 64,
                      {0: [(S("acc_summed"), s.acc_base + s.accs), (S("negc_placed"), 48), (S("ident_bf"), 1)]},
                      leads=[lambda: memory_keys(0, 0)], between=memory_between(memory_keys, memory_values))
            gb = head_base("fox")[1]
            residual("foxo", lambda kt: fo[:, :, kt, :], {g: [(S("att_lo"), gb + g + 1)] for g in range(KT)}, "memq1", {0: 4})
            memory_attention(1, hA, mq1, mk1, mv1, prob1, probT1)
            gb = head_base("mem1")[1]
            residual("memo1", hA, {2 * p: [(S("att_lo"), gb + p + 1)] for p in range(PAIRS)}, "ff1", {0: 5})
            linear("up1", hA, pair_ready(norm_base("ff1")))
            residual("down1", hid, {2 * c: [(S("up1_lo"), c + 1)] for c in range(KF // 2)}, "final1", {0: 6, 12: 7})

            norm_sums("ffa")
            linear("gu1", hA, pair_ready(norm_base("ffa")))
            residual("dn1", hid, {c: [(S("gu1_lo"), c + 1)] for c in range(KF2)}, "mixn", {0: 8})
            linear("incols", hA, pair_ready(norm_base("mixn")))
            linear("inrows", hA, None)
            linear("inlr", hA, None)
            pe.wait_ge(S("acc_summed"), STAGE["inlr"].acc_base + 1)
            for tt in range(TT):
                mm = nc.tensor.transpose(turned[0:16, 0, tt * P:(tt + 1) * P],
                                         small[:, 0, tt * 16:(tt + 1) * 16], ident[:])
            mm.then_inc(S("lr_turn"), 1)
            linear("ingates", hA, None)
            pe.wait_ge(S("lr_turned"), 2)
            pe.wait_ge(S("wlr_loaded"), 16)
            for tt in range(TT):
                mm = nc.tensor.matmul(turned[:, tt, :], glrT[0:17, tt * P:(tt + 1) * P], wlr[:],
                                      start=True, stop=True)
            mm.then_inc(S("lr_logits"), 1)
            pe.wait_ge(S("loga_ready"), 1)
            pe.wait_ge(S("spans_loaded"), 32)
            s = STAGE["ingates"]
            pe.wait_ge(S("acc_summed"), s.acc_base + s.accs)
            moba_scores = head_base("moba")[0]

            def level_spans(lv):
                if lv == NL:
                    return
                i = lv if lv < NL else NL
                if i >= 2:
                    pe.wait_ge(S("gla_exp"), i - 1)
                for ct in range(2):
                    for tt in range(TT):
                        m = lv if lv < NL else NL + tt
                        mm = nc.tensor.matmul(score[:, i % 2, ct, tt * P:(tt + 1) * P],
                                              loga[:, tt, ct * P:(ct + 1) * P], spans[:, m, :],
                                              start=True, stop=True)
                mm.then_inc(S("gla_span"), 1)

            A_ps = [acc[:, i, :, :].rearrange("p a (b t) -> p (a b) t", b=4) for i in range(2)]

            def level_scores(lv):
                own = lv < NL + 1
                if lv < NL:
                    pe.wait_ge(S("gla_qk"), 2 * (lv + 1))
                elif lv == NL + 1:
                    pe.wait_ge(S("gla_qk"), 2 * (NL + 1))
                if lv >= 2:
                    pe.wait_ge(S("gla_masked"), 2 * (lv - 1) - 1)
                kk, qq = (inT[:, 2:4, :], inT[:, 0:2, :]) if lv == NL else (ke[:], qe[:])
                for h in range(G_HEADS):
                    off, ct = 64 * (h % 2), h // 2
                    for tt in range(TT if own else 1):
                        dst = A_ps[lv % 2][:, 2 * gla_at(h) + tt if own else 4 * (h % 2) + h // 2, :]
                        qt = tt if own else 1
                        mm = nc.tensor.matmul(dst, kk[off:off + 64, ct, tt * P:(tt + 1) * P],
                                              qq[off:off + 64, ct, qt * P:(qt + 1) * P],
                                              start=True, stop=True, skip_group_check=True)
                mm.then_inc(S("gla_scores"), 1)

            level_spans(0)
            for lv in range(NL + 2):
                if lv + 1 < NL:
                    level_spans(lv + 1)
                elif lv == NL:
                    level_spans(NL + 1)
                level_scores(lv)
            pe.wait_ge(S("gla_masked"), 2 * (NL + 1))
            for h in range(G_HEADS):
                dst = score[:, h // 2, h % 2, :]
                nc.tensor.matmul(dst[:, 0:P], inV[:, 0, h * P:(h + 1) * P], A_same[:, 2 * gla_at(h), :],
                                 start=True, stop=True, skip_group_check=True)
                nc.tensor.matmul(dst[:, P:T], inV[:, 0, h * P:(h + 1) * P], A_next[:, gla_at(h), :],
                                 start=True, stop=False, skip_group_check=True)
                mm = nc.tensor.matmul(dst[:, P:T], inV[:, 1, h * P:(h + 1) * P], A_same[:, 2 * gla_at(h) + 1, :],
                                      start=False, stop=True, skip_group_check=True)
            mm.then_inc(S("gla_out"), 1)
            pe.wait_ge(S("gla_sq"), 1)
            sums = acc[:, 0, :, :]
            for i in range(2):
                mm = nc.tensor.matmul(sums[:, i, :], ones[:], aux[:, i, :, :].rearrange("p a t -> p (a t)"),
                                      start=True, stop=True)
            mm.then_inc(S("gla_stat"), 1)

            def moba_bias(h):
                nc.tensor.matmul(score[:, h % 2, 0, :], ident[:], toep[:, h, P:3 * P], start=True,
                                 stop=False, skip_group_check=True)
                nc.tensor.matmul(score[:, h % 2, 1, :], ident[:], toep[:, h, 0:2 * P], start=False,
                                 stop=False, skip_group_check=True)

            attention("moba", inT[:, 8:12, :], inT[:, 12:16, :],
                      lambda kt, at, n: inV[:, kt, 512 + at:512 + at + n], prob2, probT2, moba_bias, P,
                      {0: [(S("gla_o"), 1), (S("toep_loaded"), 16)]})
            gb = head_base("moba")[1]
            linear("branch", hA, {0: [(S("gla_lo"), 1)], 4: [(S("att_lo"), gb + 1)], 5: [(S("att_lo"), gb + 2)],
                                  6: [(S("att_lo"), gb + 3)], 7: [(S("att_lo"), gb + 4)]})
            residual("out", hM, {c: [(S("branch_lo"), c + 1)] for c in range(KT)}, "ffb")
            linear("gu2", hA, pair_ready(norm_base("ffb")))
            residual("dn2", hid, {c: [(S("gu2_lo"), c + 1)] for c in range(KF2)}, "final2")

        @block.scalar
        def _(act):
            def wait(sem, value):
                act.wait_ge(S(sem), value)

            def split_hi(st, c, known):
                n = st.base + known
                slot = n % RING
                act.wait_ge(raw_loaded[slot], (c - known) * (16 // RING) + 16 * (n // RING + 1))
                if n >= RING:
                    wait("chunk_done", c + (st.base - RING + 1))
                nc.scalar.activation(wsplit[:, slot, 0, 0:elems_of(n)], raw[:, slot, 0:elems_of(n)],
                                     ACT.Copy).then_inc(S("w_hi"), 1)

            def low(st, a, known_a, bias=None, width=T):
                par = (st.acc_base + known_a) % 2
                wait("chunk_done", a * st.per_acc + (st.base + st.per_acc))
                if st.acc_base + known_a >= 1:
                    wait("acc_summed", a + st.acc_base)
                if bias is None:
                    src = acc[:, par, :, width:2 * width]
                    last = nc.scalar.activation(lowp[:, :, 0:width], src, ACT.Copy)
                else:
                    for j in range(2):
                        last = nc.scalar.activation(lowp[:, j, :], acc[:, par, j, T:2 * T], ACT.Identity,
                                                    bias=bias(known_a, j))
                last.then_inc(S("acc_low"), 1)

            def linear(name, bias=None, post=None, flush=None, width=T, steps=False, late=False):
                st = STAGE[name]

                def body(c, known):
                    if st.per_acc == 1:
                        low(st, c, known, bias, width)
                        if post:
                            post(c, known)
                    elif known % st.per_acc == st.per_acc - 1:
                        low(st, known // st.per_acc, known // st.per_acc, bias, width)
                    elif known % st.per_acc == 0 and post:
                        post(known // st.per_acc, known // st.per_acc)
                    if st.base + known + RING < N_CHUNKS and not (late and known == st.chunks - 1):
                        split_hi(st, c + RING, known + RING)

                if steps:
                    return body
                if st.per_acc == 1 and bias is None:
                    groups(act, st.chunks, body, lead=RING, tail=RING)
                else:
                    for c in range(st.chunks):
                        body(c, c)
                if flush:
                    flush()

            def norm_squares(name, src, ready, pairs=range(PAIRS)):
                q = norm_index(name)
                for p in pairs:
                    for sem, value in ready(p):
                        wait(sem, value)
                    if p >= 2:
                        wait("norm_stat", PAIRS * q + p - 1)
                    nc.scalar.activation(aux[:, p % 2, :, :], src[:, 2 * p:2 * p + 2, :],
                                         ACT.Square).then_inc(S("norm_sq"), 1)

            def inverse_root(sem, n, src, r, scale=1.0, bias=0.0):
                nc.scalar.activation(r, src, ACT.Ln, scale=scale, bias=bias).then_inc(S(sem), 1)
                wait(sem, n + 1)
                nc.scalar.activation(r, r, ACT.Exp, scale=-0.5).then_inc(S(sem), 1)

            def norm_root(name):
                q = norm_index(name)
                wait("norm_stat", PAIRS * (q + 1))
                wait("log_table", q + 1)
                inverse_root("norm_root", 2 * q, stat[:, 0, :], rstd[:], 1 / D, col("rms_eps"))

            def norm_hi(name, dest, which=0, shift=None):
                nb = norm_base(name) + PAIRS * which
                for p in range(PAIRS):
                    wait("norm_h", nb + p + 1)
                    if shift is None:
                        last = nc.scalar.activation(dest[:, 2 * p:2 * p + 2, 0:T], tsum[:, p % 2, :, :], ACT.Copy)
                    else:
                        for j in range(2):
                            last = nc.scalar.activation(dest[:, 2 * p + j, 0:T], tsum[:, p % 2, j, :],
                                                        ACT.Identity, bias=mod[:, shift + 2 * p + j:shift + 2 * p + j + 1])
                    last.then_inc(S("norm_hi"), 1)

            def log_table(name):
                nc.scalar.activation(rstd[:, 0:1], col("rms_eps"), ACT.Ln).then_inc(S("log_table"), 1)

            def norm(name, src, ready, dests, shift=None):
                norm_squares(name, src, ready)
                log_table(name)
                norm_root(name)
                for i, dest in enumerate(dests):
                    norm_hi(name, dest, i, shift)

            def x_ready(stage):
                return lambda p: [("x_updated", x_base(stage) + p + 1)]

            def residual(name, norm_name, dests, bias=None, shift=None):
                st = STAGE[name]

                def flush():
                    log_table(norm_name)
                    norm_squares(norm_name, x, x_ready(name), [PAIRS - 1])

                linear(name, bias=bias, late=True, flush=flush,
                       post=lambda a, ka: norm_squares(norm_name, x, x_ready(name), [a - 1]) if ka >= 1 else None)
                norm_root(norm_name)
                if st.base + st.chunks - 1 + RING < N_CHUNKS:
                    split_hi(st, st.chunks - 1 + RING, st.chunks - 1 + RING)
                for i, dest in enumerate(dests):
                    norm_hi(norm_name, dest, i, shift)

            def hidden_hi(name, dest):
                def post(c, known):
                    wait(f"{name}_r", c + 1)
                    par = (STAGE[name].acc_base + known) % 2
                    if dest is hid and name.startswith("up"):
                        out_ap = hid[:].rearrange("p (c j) t -> p c j t", j=2)[:, c, :, 0:T]
                        nc.scalar.activation(out_ap, tsum[:, par, :, :], ACT.Copy).then_inc(S(f"{name}_hi"), 1)
                    else:
                        nc.scalar.activation(dest[:, c, 0:T], tsum[:, par, 0, :],
                                             ACT.Copy).then_inc(S(f"{name}_hi"), 1)
                return post

            def feed_forward(up):
                hi = hidden_hi(up, hid)
                n = STAGE[up].chunks
                linear(up, post=lambda c, known: hi(c - 1, known - 1) if known >= 1 else None,
                       flush=lambda: hi(n - 1, n - 1))

            def gated_feed_forward(gu):
                hi = hidden_hi(gu, hid)
                n = STAGE[gu].chunks

                def post(c, known):
                    if known >= 1:
                        hi(c - 1, known - 1)
                    par = (STAGE[gu].acc_base + known) % 2
                    wait("acc_summed", c + (STAGE[gu].acc_base + 1))
                    nc.scalar.activation(aux[:, par, 0, :], tsum[:, par, 0, :],
                                         ACT.Sigmoid).then_inc(S(f"{gu}_sig"), 1)

                linear(gu, post=post, flush=lambda: hi(n - 1, n - 1))

            def attention(name, scale, prob, probT, dest, leads=(), between={}):
                _, n_heads, n_groups = next(a for a in ATTENTIONS if a[0] == name)
                b, gb = head_base(name)
                per_group = n_heads // n_groups
                tiles = 2 if name.startswith("mem") else 1

                def exps(h):
                    wait("att_max", 2 * (b + h + 1))
                    if h >= 2:
                        wait("att_turn", b + h - 1)
                    for qt in range(TT):
                        at = 2 * h + qt
                        last = nc.scalar.activation(prob[:, h % 2, qt, :], score[:, h % 2, qt, :], ACT.Exp,
                                                    bias=small[:, 1, at:at + 1], scale=scale,
                                                    accum_out=small[:, 2, at:at + 1])
                    last.then_inc(S("att_exp"), 1)

                def out_hi(g):
                    wait("att_out", b + per_group * (g + 1))
                    nc.scalar.activation(dest(g * tiles, tiles), stat[:, 0:tiles, :], ACT.Copy).then_inc(S("att_hi"), 1)

                leads = list(leads) + [None] * 3
                for i in range(3):
                    if leads[i]:
                        leads[i]()
                    if i < 2:
                        exps(i)
                for h in range(n_heads):
                    wait("att_turn", b + h + 1)
                    if h >= 2:
                        wait("att_out", b + h - 1)
                    src, dst = turned[:], probT[:, h % 2, :, :]
                    if name in ("fox", "moba"):
                        used = T + P
                        src = src.rearrange("p a t -> p (a t)")[:, 0:used]
                        dst = dst.rearrange("p a t -> p (a t)")[:, 0:used]
                    nc.scalar.activation(dst, src, ACT.Copy).then_inc(S("att_turned"), 1)
                    if h + 2 < n_heads:
                        exps(h + 2)
                    if h in between:
                        between[h]()
                    if (h + 1) % per_group == 0:
                        out_hi(h // per_group)

            def memory_attention(layer, prob, probT):
                chunk = linear(f"memq{layer}", steps=True)
                attention(f"mem{layer}", 1 / 16, prob, probT, lambda at, n: hA[:, at:at + n, 0:T],
                          leads=[lambda: (chunk(0, 0), chunk(1, 1)), lambda: chunk(2, 2), lambda: chunk(3, 3)])

            def log_sigmoid(z, za_, zl_, sem, first):
                wait(sem, first)
                nc.scalar.activation(za_, z, ACT.Abs).then_inc(S(sem + "_ln"), 1)
                wait(sem + "_ln", 1)
                nc.scalar.activation(zl_, za_, ACT.Exp, scale=-1.0).then_inc(S(sem + "_ln"), 1)
                wait(sem + "_ln", 2)
                nc.scalar.activation(za_, zl_, ACT.Ln, bias=1.0).then_inc(S(sem + "_ln"), 1)

            for n in range(RING):
                split_hi(PLAN[0], n, n)
            wait("consts_loaded", 16 * 7)
            nc.scalar.activation(cact[:], col("cond", 0, KT), ACT.Sigmoid).then_inc(S("cond_sig"), 1)
            nc.scalar.activation(ident_bf[:], ident[:], ACT.Copy).then_inc(S("ident_bf"), 1)
            for h in range(G_HEADS):
                last = nc.scalar.activation(relrep[:, h, :], relT[:, h:h + 1].to_broadcast([BUCKETS + 1, P]), ACT.Copy)
            last.then_inc(S("rel_spread"), 1)
            norm("mix0", x, lambda p: [("x_loaded", 16)], [hA])

            def glu(c, known):
                wait("acc_summed", c + 1)
                if c >= 2:
                    wait("u_ready", c - 1)
                nc.scalar.activation(aux[:, c % 2, 0, :], tsum[:, c % 2, 1, :], ACT.Sigmoid).then_inc(S("pw1_sig"), 1)

            wait("norm_stat", PAIRS)
            linear("pw1", bias=lambda a, j: col("pw1_b", KT * j + a), post=glu)
            wait("u_ready", KT)
            norm("mem0", memx0, lambda p: [("mem_loaded", 16)], [hM])
            linear("memk0")
            linear("memv0")
            s = STAGE["memv0"]
            wait("acc_summed", s.acc_base + s.accs)
            for h in range(G_HEADS):
                wait("rel_made", h + 1)
                if h:
                    wait("skew_stored", 16 * h)
                nc.scalar.activation(lowp[:].rearrange("p a t -> p (a t)"), turned[:].rearrange("p a t -> p (a t)"),
                                     ACT.Copy, scale=float(P) ** 0.5).then_inc(S("rel_copied"), 1)
                wait("rel_copied", h + 1)
                act.dma_start(skew_dram[h], lowp[:].rearrange("p a t -> p (a t)")).then_inc(S("skew_stored"), 16)
            for p in range(PAIRS):
                wait("ln_centred", p + 1)
                if p >= 2:
                    wait("ln_stat", p)
                nc.scalar.activation(aux[:, p % 2, :, :], conv[:, 2 * p:2 * p + 2, :], ACT.Square).then_inc(S("ln_sq"), 1)
            wait("ln_stat", 1 + PAIRS)
            inverse_root("ln_root", 0, stat[:, 0, :], rstd[:], 1 / D, col("ln_eps"))
            for p in range(PAIRS):
                wait("ln_y", p + 1)
                if p >= 2:
                    wait("ln_r", p - 1)
                for j in range(2):
                    kt = 2 * p + j
                    last = nc.scalar.activation(aux[:, p % 2, j, :], conv[:, kt, :], ACT.Sigmoid,
                                                bias=col("ln_b", kt), scale=col("ln_g", kt))
                last.then_inc(S("ln_sig"), 1)
                if p >= 1:
                    wait("ln_r", p)
                    nc.scalar.activation(hA[:, 2 * p - 2:2 * p, 0:T], tsum[:, (p - 1) % 2, :, :], ACT.Copy).then_inc(S("ln_hi"), 1)
            wait("ln_r", PAIRS)
            nc.scalar.activation(hA[:, KT - 2:KT, 0:T], tsum[:, 1, :, :], ACT.Copy).then_inc(S("ln_hi"), 1)
            wait("skew_stored", 16 * G_HEADS)
            residual("pw2", "memq0", [hA], bias=lambda a, j: col("pw2_b", 2 * a + j))
            memory_attention(0, prob0, probT0)
            residual("memo0", "ff0", [hA])
            feed_forward("up0")

            residual("down0", "fox", [hA, hB])
            s = STAGE["down0"]
            wait("chunk_done", s.base + s.chunks)
            act.dma_start(memx1[:], dram["memT"]).then_inc(S("mem1_loaded"), 16)
            act.dma_start(tri[:], dram["tri"]).then_inc(S("tri_loaded"), 16)
            linear("foxk")
            memory_ready = lambda p: [("mem1_loaded", 16)]
            norm_squares("mem1", memx1, memory_ready, [0, 1])
            linear("foxv", post=lambda c, known: norm_squares("mem1", memx1, memory_ready, [2, 3]) if known == 0 else None)
            log_table("mem1")
            linear("foxf", width=HEADS)
            norm_root("mem1")
            norm_hi("mem1", hA)
            log_sigmoid(small[:, 0, :], small[:, 1, :], small[:, 2, :], "fgate_z", 1)
            linear("foxq")
            for i in range(3):
                wait("negc_ready", i + 1)
                act.dma_start(negc_row[i:i + 1, :, :], negc_part[0:HEADS, i, :]).then_inc(S("negc_placed"), 16)
            memory_keys, memory_values = linear("memk1", steps=True), linear("memv1", steps=True)
            attention("fox", 1 / 8, prob1, probT1, lambda at, n: fo[:, 0, at:at + n, :],
                      leads=[lambda: memory_keys(0, 0)], between=memory_between(memory_keys, memory_values))
            residual("foxo", "memq1", [hA])
            memory_attention(1, prob1, probT1)
            residual("memo1", "ff1", [hA])
            feed_forward("up1")
            residual("down1", "final1", [])

            norm("ffa", x, x_ready("final1"), [hA], shift=0)
            gated_feed_forward("gu1")
            residual("dn1", "mixn", [hA], shift=3 * KT)
            s = STAGE["dn1"]
            wait("chunk_done", s.base + s.chunks)
            act.dma_start(spans[:], dram["spans"]).then_inc(S("spans_loaded"), 16)
            act.dma_start(lmask[:], dram["lmask"]).then_inc(S("spans_loaded"), 16)
            act.dma_start(wlr[:], dram["wlr"]).then_inc(S("wlr_loaded"), 16)
            linear("incols")
            linear("inrows")
            linear("inlr", width=16)

            def gate(c, known):
                par = (STAGE["ingates"].acc_base + known) % 2
                wait("acc_summed", c + (STAGE["ingates"].acc_base + 1))
                nc.scalar.activation(gates[:, c, :, :], tsum[:, par, :, :], ACT.Sigmoid).then_inc(S("gate_ready"), 1)

            linear("ingates", post=gate)
            nc.scalar.activation(aux[:], inT[:, 4:8, :].rearrange("p (a b) t -> p a b t", a=2), ACT.Sigmoid).then_inc(S("og_sig"), 1)
            log_sigmoid(loga[:], za[:], zl[:], "lr_z", 1)
            for i in range(NL + 1):
                wait("gla_span", i + 1)
                if i >= 1:
                    wait("gla_qk", 2 * i)
                else:
                    wait("loga_ready", 1)
                nc.scalar.activation(decay[:], score[:, i % 2, :, :], ACT.Exp).then_inc(S("gla_exp"), 1)
            wait("gla_out", 1)
            wait("og_silu", 1)
            nc.scalar.activation(aux[:], score[:], ACT.Square).then_inc(S("gla_sq"), 1)
            skewed = bass.AP(tensor=skew_dram.tensor, offset=P - 1,
                             ap=[[SKEW - 1, P], [P * SKEW, G_HEADS], [1, 3 * P]])
            wait("gla_scores", NL + 2)
            act.dma_start(toep[:], skewed).then_inc(S("toep_loaded"), 16)
            wait("gla_var", 1)
            inverse_root("gla_root", 0, tsum[:], aux[:])
            wait("gla_o", 1)
            nc.scalar.activation(hA[:, 0:4, 0:T], o_gla[:], ACT.Copy).then_inc(S("gla_hi"), 1)
            attention("moba", float(P) ** -0.5, prob2, probT2, lambda at, n: hA[:, 4 + at:4 + at + n, 0:T])
            hi = hidden_hi("branch", hM)
            linear("branch", post=lambda c, known: hi(c - 1, known - 1) if known >= 1 else None,
                   flush=lambda: hi(KT - 1, KT - 1))
            residual("out", "ffb", [hA], shift=6 * KT)
            gated_feed_forward("gu2")
            residual("dn2", "final2", [])

        @block.vector
        def _(dve):
            V = nc.vector

            def wait(sem, value):
                dve.wait_ge(S(sem), value)

            AHEAD = RING - 1

            def split_lo(st, c, known):
                n = st.base + known
                slot = n % RING
                wait("w_hi", c + (st.base + 1))
                e = elems_of(n)
                V.tensor_tensor(wsplit[:, slot, 1, 0:e], raw[:, slot, 0:e], wsplit[:, slot, 0, 0:e].bitcast(F32),
                                ALU.subtract).then_inc(S("w_lo"), 1)

            def total(st, a, known_a, dest=None, width=T):
                par = (st.acc_base + known_a) % 2
                wait("acc_low", a + (st.acc_base + 1))
                dst = tsum[:, par, :, :] if dest is None else dest
                V.tensor_tensor(dst, acc[:, par, :, 0:width], lowp[:, :, 0:width], ALU.add).then_inc(S("acc_summed"), 1)

            def linear(name, dest=None, before=None, early=None, post=None, flush=None, width=T, straight=False,
                       segments={}, steps=False):
                st = STAGE[name]

                def body(c, known):
                    if before:
                        before(c, known)
                    last = known % st.per_acc == st.per_acc - 1
                    a, ka = (c, known) if st.per_acc == 1 else (known // st.per_acc, known // st.per_acc)
                    if last:
                        if dest is None:
                            done = st.base + known + AHEAD
                            wait("w_lo", N_CHUNKS if done >= N_CHUNKS else c + (st.base + AHEAD))
                        total(st, a, ka, dest(a) if dest else None, width)
                        if early:
                            early(a, ka)
                    if st.base + known + AHEAD < N_CHUNKS:
                        split_lo(st, c + AHEAD, known + AHEAD)
                    if known in segments:
                        modulation(segments[known])
                    if last and post:
                        post(a, ka)

                if steps:
                    return body
                if st.per_acc == 1 and not straight:
                    groups(dve, st.chunks, body, lead=RING, tail=RING)
                else:
                    for c in range(st.chunks):
                        body(c, c)
                if flush:
                    flush()

            def add_to_x(name, gain=None, segments={}):
                st = STAGE[name]

                def early(a, ka):
                    par = (st.acc_base + ka) % 2
                    wait("acc_summed", st.acc_base + a + 1)
                    if gain is None:
                        last = V.tensor_tensor(x[:, 2 * a:2 * a + 2, :], x[:, 2 * a:2 * a + 2, :], tsum[:, par, :, :], ALU.add)
                    else:
                        for j in range(2):
                            kt = 2 * a + j
                            last = V.scalar_tensor_tensor(out=x[:, kt, :], in0=tsum[:, par, j, :],
                                                          scalar=mod[:, gain + kt:gain + kt + 1], in1=x[:, kt, :],
                                                          op0=ALU.mult, op1=ALU.add)
                    last.then_inc(S("x_updated"), 1)
                linear(name, early=early, segments=segments)

            def newton(sem, n, v, r, tmp):
                V.scalar_tensor_tensor(out=tmp, in0=r, scalar=-0.5, in1=r, op0=ALU.mult, op1=ALU.mult).then_inc(S(sem), 1)
                wait(sem, n + 1)
                V.tensor_tensor(tmp, tmp, v, ALU.mult).then_inc(S(sem), 1)
                wait(sem, n + 2)
                V.scalar_tensor_tensor(out=r, in0=tmp, scalar=1.5, in1=r, op0=ALU.add, op1=ALU.mult).then_inc(S(sem), 1)
                wait(sem, n + 3)

            def norm_scale(name):
                q = norm_index(name)
                wait("norm_root", 2 * q + 1)
                V.tensor_scalar(var[:], stat[:, 0, :], 1.0 / D, RMS_EPS, ALU.mult, ALU.add).then_inc(S("norm_var"), 1)
                wait("norm_var", q + 1)
                wait("norm_root", 2 * (q + 1))
                newton("norm_rstd", 3 * q, var[:], rstd[:], lowp[:, 0, :])

            def norm_apply(name, src, dest, gain, which=0, shift=None):
                nb = norm_base(name) + PAIRS * which

                def lo(p):
                    wait("norm_hi", nb + p + 1)
                    hi_ap = dest[:, 2 * p:2 * p + 2, 0:T].bitcast(F32)
                    if shift is None:
                        last = V.tensor_tensor(dest[:, 2 * p:2 * p + 2, T:2 * T], tsum[:, p % 2, :, :], hi_ap, ALU.subtract)
                    else:
                        for j in range(2):
                            kt = 2 * p + j
                            last = V.scalar_tensor_tensor(out=dest[:, kt, T:2 * T], in0=tsum[:, p % 2, j, :],
                                                          scalar=mod[:, shift + kt:shift + kt + 1],
                                                          in1=dest[:, kt, 0:T].bitcast(F32),
                                                          op0=ALU.add, op1=ALU.subtract)
                    last.then_inc(S("norm_lo"), 1)

                for p in range(PAIRS):
                    if which or p >= 2:
                        wait("norm_lo", nb + p - 1)
                    for j in range(2):
                        kt = 2 * p + j
                        last = V.scalar_tensor_tensor(out=tsum[:, p % 2, j, :], in0=src[:, kt, :], scalar=gain(kt),
                                                      in1=rstd[:], op0=ALU.mult, op1=ALU.mult)
                    last.then_inc(S("norm_h"), 1)
                    if p >= 1:
                        lo(p - 1)
                lo(PAIRS - 1)

            def norm(name, src, dests, shift=None):
                norm_scale(name)
                for i, (dest, gain) in enumerate(dests):
                    norm_apply(name, src, dest, gain, i, shift)

            def norm_in_place(name, sem):
                norm_scale(name)
                for p in range(PAIRS):
                    for j in range(2):
                        kt = 2 * p + j
                        last = V.scalar_tensor_tensor(out=x[:, kt, :], in0=x[:, kt, :],
                                                      scalar=col(name, kt),
                                                      in1=rstd[:], op0=ALU.mult, op1=ALU.mult)
                    last.then_inc(S(sem), 1)

            def lo_of(name, dest, pair):
                def lo(c, known):
                    wait(f"{name}_hi", c + 1)
                    par = (STAGE[name].acc_base + known) % 2
                    if pair:
                        d = hid[:].rearrange("p (c j) t -> p c j t", j=2)[:, c, :, :]
                        V.tensor_tensor(d[:, :, T:2 * T], tsum[:, par, :, :], d[:, :, 0:T].bitcast(F32),
                                        ALU.subtract).then_inc(S(f"{name}_lo"), 1)
                    else:
                        V.tensor_tensor(dest[:, c, T:2 * T], tsum[:, par, 0, :], dest[:, c, 0:T].bitcast(F32),
                                        ALU.subtract).then_inc(S(f"{name}_lo"), 1)
                return lo

            def feed_forward(up, down, segments):
                st = STAGE[up]
                lo = lo_of(up, hid, True)

                def square(c, known):
                    par = (st.acc_base + known) % 2
                    t = tsum[:, par, :, :]
                    wait("acc_summed", c + (st.acc_base + 1))
                    V.scalar_tensor_tensor(out=t, in0=t, scalar=0.0, in1=t, op0=ALU.max, op1=ALU.mult).then_inc(S(f"{up}_r"), 1)

                linear(up, early=lambda c, known: lo(c - 1, known - 1) if known >= 1 else None, post=square,
                       flush=lambda: lo(st.chunks - 1, st.chunks - 1))
                add_to_x(down, segments=segments)

            def gated_feed_forward(gu, dn, gain, segments={}):
                st = STAGE[gu]
                lo = lo_of(gu, hid, False)

                def gated(c, known):
                    par = (st.acc_base + known) % 2
                    t0, t1 = tsum[:, par, 0, :], tsum[:, par, 1, :]
                    wait(f"{gu}_sig", c + 1)
                    V.tensor_tensor(t0, t0, t1, ALU.mult).then_inc(S(f"{gu}_p"), 1)
                    wait(f"{gu}_p", c + 1)
                    V.tensor_tensor(t0, t0, aux[:, par, 0, :], ALU.mult).then_inc(S(f"{gu}_r"), 1)

                linear(gu, early=lambda c, known: lo(c - 1, known - 1) if known >= 1 else None, post=gated,
                       flush=lambda: lo(st.chunks - 1, st.chunks - 1))
                add_to_x(dn, gain, segments)

            def plain(name, t, segments={}, steps=False):
                return linear(name, dest=lambda a: t[:].rearrange("p (c j) t -> p c j t", j=2)[:, a, :, :],
                              segments=segments, steps=steps)

            def rows(name, t, steps=False):
                return linear(name, dest=lambda a: t[:].rearrange("p r (c n) -> p r c n", n=T)[:, :, a, :],
                              steps=steps)

            def attention(name, scale, prob, dest, leads=(), between={}):
                _, n_heads, n_groups = next(a for a in ATTENTIONS if a[0] == name)
                b, gb = head_base(name)
                per_group = n_heads // n_groups
                tiles = 2 if name.startswith("mem") else 1

                def largest(h):
                    wait("att_scores", b + h + 1)
                    V.tensor_reduce(small[:, 0, 2 * h:2 * h + 2], score[:, h % 2, :, :], AX.X, ALU.max).then_inc(S("att_max"), 1)
                    wait("att_max", 2 * (b + h) + 1)
                    V.tensor_scalar(small[:, 1, 2 * h:2 * h + 2], small[:, 0, 2 * h:2 * h + 2], -scale, None,
                                    ALU.mult).then_inc(S("att_max"), 1)

                def normalise(h):
                    wait("att_exp", b + h + 1)
                    V.reciprocal(small[:, 3, 2 * h:2 * h + 2], small[:, 2, 2 * h:2 * h + 2]).then_inc(S("att_inv"), 1)
                    wait("att_inv", b + h + 1)
                    V.tensor_tensor(prob[:, h % 2, :, :], prob[:, h % 2, :, :],
                                    small[:, 3, 2 * h:2 * h + 2].unsqueeze(2).to_broadcast([P, TT, T]),
                                    ALU.mult).then_inc(S("att_prob"), 1)

                def out_lo(g):
                    wait("att_hi", gb + g + 1)
                    V.tensor_tensor(dest(1, g * tiles, tiles), stat[:, 0:tiles, :],
                                    dest(0, g * tiles, tiles).bitcast(F32), ALU.subtract).then_inc(S("att_lo"), 1)

                leads = list(leads) + [None] * 3
                for i in range(2):
                    if leads[i]:
                        leads[i]()
                    largest(i)
                normalise(0)
                if leads[2]:
                    leads[2]()
                for h in range(n_heads):
                    if h + 1 < n_heads:
                        normalise(h + 1)
                    if h + 2 < n_heads:
                        largest(h + 2)
                    if h in between:
                        between[h]()
                    if (h + 1) % per_group == 0:
                        out_lo(h // per_group)

            def in_hl(first):
                return lambda part, at, n: hA[:, first + at:first + at + n, part * T:(part + 1) * T]

            def memory_attention(layer, queries, prob):
                chunk = plain(f"memq{layer}", queries, steps=True)
                attention(f"mem{layer}", 1 / 16, prob, in_hl(0),
                          leads=[lambda: (chunk(0, 0), chunk(1, 1)), lambda: chunk(2, 2), lambda: chunk(3, 3)])

            def modulation(seg):
                wait("ada_used", seg + 1)
                V.tensor_tensor(mod[:, SEGMENT * seg:SEGMENT * (seg + 1)], turned[:, 0, 0:SEGMENT],
                                col("ada_b", SEGMENT * seg, SEGMENT), ALU.add).then_inc(S("mod_made"), 1)

            V.memset(upad[:, :, 0:PAD], 0.0).then_inc(S("pad_ready"), 1)
            for n in range(AHEAD):
                split_lo(PLAN[0], n, n)
            wait("consts_loaded", 16 * 7)
            norm("mix0", x, [(hA, lambda kt: col("mix0", kt))])

            steps = [(kt, tap) for kt in range(V_TILES) for tap in range(TAPS)]
            at_step = [0]

            def conv_taps(n):
                for _ in range(n):
                    if at_step[0] == len(steps):
                        return
                    kt, tap = steps[at_step[0]]
                    at_step[0] += 1
                    w = taps[:, tap, kt:kt + 1]
                    u = upad[:, kt, tap:tap + T]
                    if tap == 0:
                        wait("u_ready", kt + 1)
                        ins = V.tensor_scalar(conv[:, kt, :], u, w, col("dw_b", kt), ALU.mult, ALU.add)
                    else:
                        wait("conv_step", at_step[0] - 1)
                        ins = V.scalar_tensor_tensor(out=conv[:, kt, :], in0=u, scalar=w, in1=conv[:, kt, :],
                                                     op0=ALU.mult, op1=ALU.add)
                    ins.then_inc(S("conv_step"), 1)

            def glu(a, ka):
                wait("pw1_sig", a + 1)
                V.tensor_tensor(upad[:, a, PAD:PAD + T], tsum[:, ka % 2, 0, :], aux[:, ka % 2, 0, :],
                                ALU.mult).then_inc(S("u_ready"), 1)
                conv_taps(12 if a else 0)

            wait("pad_ready", 1)
            linear("pw1", post=glu, straight=True)
            norm("mem0", memx0, [(hM, lambda kt: col("src0", kt))])
            linear("memk0", dest=lambda a: mk0[:, 2 * a:2 * a + 2, :], post=lambda a, ka: conv_taps(12), straight=True)
            linear("memv0", dest=lambda a: mv0[:, :, a * T:(a + 1) * T], post=lambda a, ka: conv_taps(12), straight=True)
            conv_taps(len(steps))
            wait("conv_step", len(steps))
            for kt in range(V_TILES, KT):
                wait("conv_pool_step", (kt - V_TILES + 1) * (2 * TAPS - 1))
            wait("ln_stat", 1)
            V.tensor_scalar(mu[:], stat[:, 0, :], 1.0 / D, None, ALU.mult).then_inc(S("ln_mean"), 1)
            wait("ln_mean", 1)
            wait("conv_step", len(steps))
            for p in range(PAIRS):
                c2 = conv[:, 2 * p:2 * p + 2, :]
                V.tensor_tensor(c2, c2, spread(mu[:], 2), ALU.subtract).then_inc(S("ln_centred"), 1)
            wait("ln_root", 1)
            V.tensor_scalar(var[:], stat[:, 0, :], 1.0 / D, LN_EPS, ALU.mult, ALU.add).then_inc(S("ln_var"), 1)
            wait("ln_var", 1)
            wait("ln_root", 2)
            wait("ln_centred", PAIRS)
            newton("ln_rstd", 0, var[:], rstd[:], mu[:])

            def ln_lo(p):
                wait("ln_hi", p + 1)
                V.tensor_tensor(hA[:, 2 * p:2 * p + 2, T:2 * T], tsum[:, p % 2, :, :],
                                hA[:, 2 * p:2 * p + 2, 0:T].bitcast(F32), ALU.subtract).then_inc(S("ln_lo"), 1)

            for p in range(PAIRS):
                c2 = conv[:, 2 * p:2 * p + 2, :]
                V.tensor_tensor(c2, c2, spread(rstd[:], 2), ALU.mult).then_inc(S("ln_y"), 1)
                wait("ln_y", p + 1)
                if p >= 2:
                    wait("ln_lo", p - 1)
                for j in range(2):
                    kt = 2 * p + j
                    last = V.tensor_scalar(tsum[:, p % 2, j, :], conv[:, kt, :], col("ln_g", kt), col("ln_b", kt),
                                           ALU.mult, ALU.add)
                last.then_inc(S("ln_z"), 1)
                wait("ln_z", p + 1)
                wait("ln_sig", p + 1)
                V.tensor_tensor(tsum[:, p % 2, :, :], tsum[:, p % 2, :, :], aux[:, p % 2, :, :],
                                ALU.mult).then_inc(S("ln_r"), 1)
                if p >= 1:
                    ln_lo(p - 1)
            ln_lo(PAIRS - 1)
            add_to_x("pw2")
            norm("memq0", x, [(hA, lambda kt: col("memq0", kt))])
            memory_attention(0, mq0, prob0)
            add_to_x("memo0", segments={0: 0})
            norm("ff0", x, [(hA, lambda kt: col("ff0", kt))])
            feed_forward("up0", "down0", {0: 1, 12: 2})

            norm("fox", x, [(hA, lambda kt: col("kv", kt)), (hB, lambda kt: col("mix1", kt))])
            plain("foxk", fk)
            rows("foxv", fv)
            linear("foxf", dest=lambda a: small[:, 0, :].rearrange("p (r n) -> p r n", r=TT), width=HEADS)
            wait("acc_summed", STAGE["foxf"].acc_base + 1)
            z = small[:, 0, :].rearrange("p (r n) -> p r n", r=TT)
            V.tensor_tensor(z, z, spread(col("fgate", 0, HEADS), TT), ALU.add).then_inc(S("fgate_z"), 1)
            norm("mem1", memx1, [(hA, lambda kt: col("src1", kt))])
            wait("fgate_z_ln", 3)
            V.scalar_tensor_tensor(out=small[:, 3, :], in0=small[:, 0, :], scalar=0.0, in1=small[:, 1, :],
                                   op0=ALU.min, op1=ALU.subtract).then_inc(S("logf_ready"), 1)
            plain("foxq", fq, {0: 3})
            V.memset(ones_bf[:], 1.0)
            wait("negc_made", 1)
            V.tensor_copy(negc_part[0:HEADS, 0, :], turned[0:HEADS, 0, :]).then_inc(S("negc_ready"), 1)
            wait("negc_ready", 1)
            V.tensor_tensor(negc[0:HEADS, :], turned[0:HEADS, 0, :], negc_part[0:HEADS, 0, :],
                            ALU.subtract).then_inc(S("negc_rest"), 1)
            wait("negc_rest", 1)
            V.tensor_copy(negc_part[0:HEADS, 1, :], negc[0:HEADS, :]).then_inc(S("negc_ready"), 1)
            wait("negc_ready", 2)
            V.tensor_tensor(negc_part[0:HEADS, 2, :], negc[0:HEADS, :], negc_part[0:HEADS, 1, :],
                            ALU.subtract).then_inc(S("negc_ready"), 1)
            memory_keys, memory_values = plain("memk1", mk1, steps=True), rows("memv1", mv1, steps=True)
            attention("fox", 1 / 8, prob1, lambda part, at, n: fo[:, part, at:at + n, :],
                      leads=[lambda: memory_keys(0, 0)], between=memory_between(memory_keys, memory_values))
            add_to_x("foxo", segments={0: 4})
            norm("memq1", x, [(hA, lambda kt: col("memq1", kt))])
            memory_attention(1, mq1, prob1)
            add_to_x("memo1", segments={0: 5})
            norm("ff1", x, [(hA, lambda kt: col("ff1", kt))])
            feed_forward("up1", "down1", {0: 6, 12: 7})
            norm_in_place("final1", "x_updated")

            def modulation_parts(parts):
                wait("mod_made", max(seg for seg, _ in parts) + 1)
                for seg, gain in parts:
                    m = mod[:, SEGMENT * seg:SEGMENT * (seg + 1)]
                    if gain:
                        V.scalar_tensor_tensor(out=m, in0=m, scalar=1.0, in1=col(gain, 0, KT), op0=ALU.add,
                                               op1=ALU.mult).then_inc(S("mod_used"), 1)
                    else:
                        V.tensor_scalar(m, m, 0.5, None, ALU.mult).then_inc(S("mod_used"), 1)

            def modulated(seg):
                return lambda kt: mod[:, SEGMENT * seg + kt:SEGMENT * seg + kt + 1]

            modulation_parts([(1, "ffa"), (2, None), (4, "mixn")])
            wait("mod_used", 3)
            norm("ffa", x, [(hA, modulated(1))], shift=0)
            gated_feed_forward("gu1", "dn1", 2 * SEGMENT, {0: 8})
            modulation_parts([(7, "ffb"), (8, None)])
            wait("mod_used", 5)
            norm("mixn", x, [(hA, modulated(4))], shift=3 * SEGMENT)
            plain("incols", inT)
            rows("inrows", inV)
            V.memset(glrT[:], 1.0).then_inc(S("lr_turned"), 1)
            linear("inlr", dest=lambda a: small[:, 0, :].rearrange("p (r n) -> p r n", r=TT), width=16)
            wait("lr_turn", 1)
            wait("lr_turned", 1)
            V.tensor_copy(glrT[0:16, :], turned[0:16, 0, :]).then_inc(S("lr_turned"), 1)
            linear("ingates", before=lambda c, known: wait("gate_ready", c - 1) if known >= 2 else None)
            wait("og_sig", 1)
            og = inT[:, 4:8, :].rearrange("p (a b) t -> p a b t", a=2)
            V.tensor_tensor(og, og, aux[:], ALU.mult).then_inc(S("og_silu"), 1)
            wait("lr_logits", 1)
            V.tensor_copy(loga[:], turned[:]).then_inc(S("lr_z"), 1)
            wait("lr_z_ln", 3)
            V.scalar_tensor_tensor(out=loga[:], in0=loga[:], scalar=0.0, in1=za[:],
                                   op0=ALU.min, op1=ALU.subtract).then_inc(S("loga_ready"), 1)
            wait("gate_ready", KT)
            flat = tsum[:].rearrange("p a b t -> p (a b t)")
            product = flat.rearrange("p (n t) -> p n t", t=P)
            A_ps = [acc[:, i, :, :].rearrange("p a (b t) -> p (a b) t", b=4) for i in range(2)]
            for lv in range(NL + 1):
                wait("gla_scores", lv + 1)
                m = spread(lmask[:, lv, :], 2 * G_HEADS)
                if lv == 0:
                    V.tensor_tensor(A_same[:], A_ps[0], m, ALU.mult).then_inc(S("gla_masked"), 1)
                    continue
                wait("gla_masked", 2 * lv - 1)
                V.tensor_tensor(product, A_ps[lv % 2], m, ALU.mult).then_inc(S("gla_masked"), 1)
                wait("gla_masked", 2 * lv)
                V.tensor_tensor(A_same[:], A_same[:], product, ALU.add).then_inc(S("gla_masked"), 1)
            wait("gla_scores", NL + 2)
            V.tensor_scalar(A_next[:].rearrange("p (b h) t -> p b h t", b=2),
                            A_ps[(NL + 1) % 2].rearrange("p (b h) t -> p b h t", b=2)[:, :, 0:2, :],
                            1 / 8, None, ALU.mult).then_inc(S("gla_masked"), 1)
            wait("gla_stat", 1)
            wait("gla_masked", 2 * NL + 2)
            V.tensor_scalar(flat, acc[:, 0, :, :].rearrange("p a t -> p (a t)"), 1.0 / P, RMS_EPS, ALU.mult,
                            ALU.add).then_inc(S("gla_var"), 1)
            wait("gla_var", 1)
            wait("gla_root", 2)
            auxf = aux[:].rearrange("p a b t -> p (a b t)")
            of = o_gla[:].rearrange("p a t -> p (a t)")
            newton("gla_rstd", 0, flat, auxf, of)
            V.tensor_tensor(of, score[:].rearrange("p a b t -> p (a b t)"), auxf, ALU.mult).then_inc(S("gla_norm"), 1)
            wait("gla_norm", 1)
            V.scalar_tensor_tensor(out=of, in0=of, scalar=col("gla"), in1=inT[:, 4:8, :].rearrange("p a t -> p (a t)"),
                                   op0=ALU.mult, op1=ALU.mult).then_inc(S("gla_o"), 1)
            wait("gla_hi", 1)
            V.tensor_tensor(hA[:, 0:4, T:2 * T], o_gla[:], hA[:, 0:4, 0:T].bitcast(F32), ALU.subtract).then_inc(S("gla_lo"), 1)
            attention("moba", float(P) ** -0.5, prob2, in_hl(4))
            lo = lo_of("branch", hM, False)

            def merge(c, known):
                par = (STAGE["branch"].acc_base + known) % 2
                t = tsum[:, par, :, :]
                wait("acc_summed", c + (STAGE["branch"].acc_base + 1))
                V.tensor_tensor(t, t, gates[:, c, :, :], ALU.mult).then_inc(S("branch_p"), 1)
                wait("branch_p", c + 1)
                V.tensor_tensor(t[:, 0, :], t[:, 0, :], t[:, 1, :], ALU.add).then_inc(S("branch_r"), 1)

            linear("branch", early=lambda c, known: lo(c - 1, known - 1) if known >= 1 else None, post=merge,
                   flush=lambda: lo(KT - 1, KT - 1))
            add_to_x("out", 5 * SEGMENT)
            norm("ffb", x, [(hA, modulated(7))], shift=6 * SEGMENT)
            gated_feed_forward("gu2", "dn2", 8 * SEGMENT)
            norm_in_place("final2", "final_ready")

        @block.gpsimd
        def _(pool):
            G = nc.gpsimd

            def wait(sem, value):
                pool.wait_ge(S(sem), value)

            HALF_STEPS = 4

            def ada_load(m, half):
                pool.dma_start(ada_w[:, half, :, :], dram["ada"][m, half]).then_inc(ada_loaded[half], 16)

            def ada_tile(m, known, last):
                for half in range(2):
                    pool.wait_ge(ada_loaded[half], m * 16 + 16)
                    w = ada_w[:, half, :, :]
                    n = m * (2 * HALF_STEPS) + HALF_STEPS * half
                    G.tensor_tensor(w, w, cact[:].unsqueeze(2).to_broadcast([P, KT, HALF]), ALU.mult).then_inc(S("ada_step"), 1)
                    wait("ada_step", n + 1)
                    G.tensor_tensor(w[:, 0:4, :], w[:, 0:4, :], w[:, 4:8, :], ALU.add).then_inc(S("ada_step"), 1)
                    wait("ada_step", n + 2)
                    G.tensor_tensor(w[:, 0:2, :], w[:, 0:2, :], w[:, 2:4, :], ALU.add).then_inc(S("ada_step"), 1)
                    wait("ada_step", n + 3)
                    G.tensor_tensor(ada_acc[:, known % SEGMENT, half * HALF:(half + 1) * HALF], w[:, 0, :], w[:, 1, :],
                                    ALU.add).then_inc(S("ada_step"), 1)
                    if not last:
                        wait("ada_step", n + 4)
                        ada_load(m + 1, half)

            def ada_segment(seg, known, last=False):
                if known:
                    wait("ada_used", seg)
                for k in range(SEGMENT):
                    ada_tile(seg * SEGMENT + k, k, last and k == SEGMENT - 1)

            ada_load(0, 0)
            ada_load(0, 1)
            wait("consts_loaded", 16 * 7)
            wait("cond_sig", 1)
            G.tensor_tensor(cact[:], cact[:], col("cond", 0, KT), ALU.mult).then_inc(S("cond_silu"), 1)
            wait("cond_silu", 1)
            n = 0
            for kt in range(V_TILES, KT):
                wait("u_ready", kt + 1)
                for tap in range(TAPS):
                    w = taps[:, tap, kt:kt + 1]
                    u = upad[:, kt, tap:tap + T]
                    if tap == 0:
                        G.tensor_scalar(conv[:, kt, :], u, w, col("dw_b", kt), ALU.mult, ALU.add).then_inc(S("conv_pool_step"), 1)
                        n += 1
                        continue
                    wait("conv_pool_step", n)
                    G.tensor_scalar(pool_tmp[:], u, w, None, ALU.mult).then_inc(S("conv_pool_step"), 1)
                    wait("conv_pool_step", n + 1)
                    G.tensor_tensor(conv[:, kt, :], conv[:, kt, :], pool_tmp[:], ALU.add).then_inc(S("conv_pool_step"), 1)
                    n += 2
            ada_segment(0, 0)
            with pool.Fori(1, N_MOD - 1) as seg:
                ada_segment(seg, 1)
            ada_segment(N_MOD - 1, N_MOD - 1, True)
            for i in range(NL + 1):
                wait("gla_exp", i + 1)
                if i:
                    wait("gla_scores", i)
                G.tensor_tensor(qe[:], inT[:, 0:2, :], decay[:], ALU.mult).then_inc(S("gla_qk"), 1)
                G.tensor_tensor(ke[:], inT[:, 2:4, :], decay[:], ALU.mult).then_inc(S("gla_qk"), 1)


def bucket_of(dist):
    exact, far = BUCKETS // 2, 128
    if dist < exact:
        return dist
    return min(BUCKETS - 1, exact + int(np.log(dist / exact) / np.log(far / exact) * (BUCKETS - exact)))


def constants():
    i = np.arange(P)
    before = (i[:, None] <= i[None, :]).astype(np.float32)
    tri = np.zeros((P, TT, T), np.float32)
    tri[:, 0, :P], tri[:, 0, P:], tri[:, 1, P:] = before, 1, before
    spans = np.zeros((P, NL + 2, P), np.float32)
    lmask = np.zeros((P, NL + 1, P), np.float32)
    t, j = i[:, None], i[None, :]
    for lv, s in enumerate(LEVELS):
        mid = j // (2 * s) * (2 * s) + s - 1
        spans[:, lv, :] = ((t > j) & (t <= mid)) | ((t > mid) & (t <= j))
        lmask[:, lv, :] = (t // (2 * s) == j // (2 * s)) & (t % (2 * s) < s) & (j % (2 * s) >= s)
    spans[:, NL, :] = t > j
    spans[:, NL + 1, :] = t <= j
    lmask[:, NL, :] = t == j
    onehot = np.zeros((BUCKETS + 1, SKEW), np.float32)
    for c in range(SKEW):
        if c < T:
            onehot[bucket_of(T - 1 - c), c] = 1
        else:
            onehot[BUCKETS, c] = MASKED
    mask = np.full((P, 2 * P), MASKED, np.float32)
    mask[:, :P][i[:, None] >= i[None, :]] = 0
    return {
        "ones": np.ones((P, P), np.float32), "ident": np.eye(P, dtype=np.float32), "mask": mask,
        "tri": -8 * tri, "spans": spans / 16, "lmask": lmask / 8, "onehot": onehot,
    }


def tiles(w, k_tiles, columns):
    w3 = w.reshape(-1, P, w.shape[1])
    return np.stack([w3[kt][:, :, cs].transpose(1, 0, 2).reshape(P, -1) for kt, cs in zip(k_tiles, columns)])


def by_columns(w, width=256):
    n = w.shape[1] // width
    return tiles(w, [slice(None)] * n, [slice(c * width, (c + 1) * width) for c in range(n)])


def paired(w, step, n):
    return tiles(w, [slice(None)] * n, [np.r_[c * P:(c + 1) * P, (step + c) * P:(step + c + 1) * P] for c in range(n)])


def layout(a):
    def rows(v):
        return v.reshape(-1, P).T

    out = {}
    out["xT"] = a["x"][0].T.reshape(KT, P, T).transpose(1, 0, 2)
    out["memT"] = a["mem"][0].T.reshape(KT, P, T).transpose(1, 0, 2)
    vectors = {
        "mix0": a["norm_mix_g"][0], "mix1": a["norm_mix_g"][1], "memq0": a["norm_mem_g"][0],
        "memq1": a["norm_mem_g"][1], "src0": a["norm_memsrc_g"][0], "src1": a["norm_memsrc_g"][1],
        "ff0": a["norm_ff_g"][0], "ff1": a["norm_ff_g"][1], "pw1_b": a["conv_pw1_b"][0],
        "dw_b": a["conv_dw_b"][0], "ln_g": a["conv_ln_g"][0], "ln_b": a["conv_ln_b"][0],
        "pw2_b": a["conv_pw2_b"][0], "kv": a["kv_norm_g"], "final1": a["final_norm_g"],
        "ffa": a["norm_ff1_2"][0], "mixn": a["norm_mix_2"][0], "ffb": a["norm_ff2_2"][0],
        "final2": a["norm_final_2"], "gla": a["gla_norm_2"][0], "ada_b": a["b_ada_2"][0], "cond": a["c_2"][0],
    }
    spread_rows = {"fgate": a["fgate_b"], "rms_eps": np.float32([RMS_EPS]), "ln_eps": np.float32([LN_EPS])}
    packed = [rows(vectors[name]) if name in vectors else np.broadcast_to(spread_rows[name], (P, n))
              for name, n in COLUMNS]
    out["cols"] = np.concatenate(packed, axis=1)
    out["taps"] = a["conv_dw_w"][0].reshape(TAPS, KT, P).transpose(2, 0, 1)
    out["relT"] = np.concatenate([a["rel_bias_2"].T, np.ones((1, G_HEADS), np.float32)])
    out["wlr"] = np.concatenate([a["w_gla_lr_2"][0], a["b_gla_lr_2"][0][None]])
    out["ada"] = a["w_ada_2"][0].reshape(KT, P, N_MOD * KT, 2, HALF).transpose(2, 3, 1, 0, 4)

    out["pw1"] = paired(a["conv_pw1_w"][0], KT, KT)
    out["pw2"] = by_columns(a["conv_pw2_w"][0])
    for layer in range(2):
        for s in "qkvo":
            out[f"mem{s}{layer}"] = by_columns(a[f"mem_w{s}"][layer])
        out[f"up{layer}"] = by_columns(a["ff_w1"][layer])
        out[f"down{layer}"] = tiles(a["ff_w2"][layer], [slice(q * KT, (q + 1) * KT) for _ in range(4) for q in range(4)],
                                    [slice(c * 256, (c + 1) * 256) for c in range(4) for _ in range(4)])
    kvf = a["kvf_w"]
    out["foxk"], out["foxv"], out["foxf"] = by_columns(kvf[:, :D]), by_columns(kvf[:, D:2 * D]), by_columns(kvf[:, 2 * D:], HEADS)
    out["foxq"], out["foxo"] = by_columns(a["fox_wq"][0]), by_columns(a["fox_wo"][0])
    for i in (1, 2):
        gu = np.concatenate([a[f"w_ff{i}_gate_2"][0], a[f"w_ff{i}_up_2"][0]], axis=1)
        out[f"gu{i}"] = paired(gu, KF2, KF2)
        out[f"dn{i}"] = tiles(a[f"w_ff{i}_down_2"][0], [slice(11 * (q % 2), 11 * (q % 2) + 11) for _ in range(4) for q in range(4)],
                              [slice(m * P, (m + 1) * P) for c in range(4) for m in (2 * c, 2 * c, 2 * c + 1, 2 * c + 1)])
    w = a["w_in_2"][0]
    sizes = [256, 256, 512, 16, 512, 512, 512, 512, D, D]
    gq, gk, gv, glr, gog, mq, mk, mv, ga, gb = np.split(w, np.cumsum(sizes)[:-1], axis=1)
    out["incols"] = by_columns(np.concatenate([gq, gk, gog, mq, mk], axis=1))
    out["inrows"] = by_columns(np.concatenate([gv, mv], axis=1))
    out["inlr"] = by_columns(glr, 16)
    out["ingates"] = paired(np.concatenate([ga, gb], axis=1), KT, KT)
    out["branch"] = by_columns(np.concatenate([a["w_br_gla_2"][0], a["w_br_moba_2"][0]]), P)
    out["out"] = by_columns(a["w_out_2"][0])
    out.update(constants())
    return out


def kernel(**inputs):
    import concourse.bacc as bacc
    import ml_dtypes
    from concourse.bass_utils import run_bass_kernel_spmd

    nc = bacc.Bacc("TRN2", target_bir_lowering=False, num_devices=1)
    arrays = {k: np.ascontiguousarray(v) for k, v in layout({k: np.asarray(v) for k, v in inputs.items()}).items()}
    arrays["mask"] = arrays["mask"].astype(ml_dtypes.bfloat16)
    dram = {}
    for name, v in arrays.items():
        dram[name] = nc.dram_tensor(f"in_{name}", v.shape, mybir.dt.from_np(v.dtype), kind="ExternalInput").ap()
    out = nc.dram_tensor("out_xT", (P, KT, T), F32, kind="ExternalOutput").ap()
    program(nc, dram, out)
    r = run_bass_kernel_spmd(nc, [{f"in_{k}": v for k, v in arrays.items()}], core_ids=[0])
    got = np.asarray(r.results[0]["out_xT"])
    return np.ascontiguousarray(got.transpose(1, 0, 2).reshape(D, T).T)[None]
```

```python
from contextlib import ExitStack

import numpy as np

import concourse.bass as bass
from concourse import mybir

F32 = mybir.dt.float32
F32R = mybir.dt.float32r
BF16 = mybir.dt.bfloat16
ACT = mybir.ActivationFunctionType
ALU = mybir.AluOpType
AX = mybir.AxisListType

P = 128
D = 1024
T = 256
KT = D // P
PAIRS = KT // 2
TT = T // P
FF = 4096
KF = FF // P
FF2 = 2816
KF2 = FF2 // P
TAPS = 31
PAD = TAPS - 1
HEADS = 16
MEM_HEADS = 4
G_HEADS = 4
RMS_EPS = 1e-6
LN_EPS = 1e-5
RING = 4
MASKED = -1e30
LEVELS = [64, 32, 16, 8, 4, 2, 1]
NL = len(LEVELS)
SEGMENT = KT
N_MOD = 9
HALF = P // 2
SKEW = 512
BUCKETS = 32
V_TILES = [1, 3, 5, 6, 7]
G_TILES = [0, 2, 4]

COLUMNS = [
    ("mix0", KT), ("mix1", KT), ("memq0", KT), ("memq1", KT), ("src0", KT), ("src1", KT),
    ("ff0", KT), ("ff1", KT), ("pw1_b", 2 * KT), ("dw_b", KT), ("ln_g", KT), ("ln_b", KT),
    ("pw2_b", KT), ("kv", KT), ("final1", KT), ("ffa", KT), ("mixn", KT), ("ffb", KT),
    ("final2", KT), ("gla", 1), ("ada_b", N_MOD * KT), ("cond", KT), ("fgate", HEADS),
    ("rms_eps", 1), ("ln_eps", 1),
]
COL = {}
_at = 0
for _name, _n in COLUMNS:
    COL[_name] = _at
    _at += _n
NCOL = _at


class Stage:

    def __init__(self, name, kind, chunks, elems, per_acc=1):
        self.name, self.kind, self.chunks, self.elems, self.per_acc = name, kind, chunks, elems, per_acc
        self.accs = chunks // per_acc


def plan():
    full = KT * 256
    seq = [
        Stage("pw1", "cols", 8, full), Stage("memk0", "cols", 4, full), Stage("memv0", "rows", 4, full),
        Stage("pw2", "cols", 4, full), Stage("memq0", "cols", 4, full), Stage("memo0", "cols", 4, full),
        Stage("up0", "cols", 16, full), Stage("down0", "deep32", 16, full, 4),
        Stage("foxk", "cols", 4, full), Stage("foxv", "rows", 4, full), Stage("foxf", "rows16", 1, KT * 16),
        Stage("foxq", "cols", 4, full),
        Stage("memk1", "cols", 4, full), Stage("memv1", "rows", 4, full),
        Stage("foxo", "cols", 4, full), Stage("memq1", "cols", 4, full), Stage("memo1", "cols", 4, full),
        Stage("up1", "cols", 16, full), Stage("down1", "deep32", 16, full, 4),
        Stage("gu1", "cols", KF2, full), Stage("dn1", "deep22", 16, 11 * P, 4),
        Stage("inlr", "rows16", 1, KT * 16), Stage("incols", "cols", 8, full), Stage("inrows", "rows", 4, full),
        Stage("ingates", "cols", 8, full), Stage("branch", "branch", 8, KT * P), Stage("out", "cols", 4, full),
        Stage("gu2", "cols", KF2, full), Stage("dn2", "deep22", 16, 11 * P, 4),
    ]
    base = acc = low = 0
    for s in seq:
        s.base, s.acc_base, s.low_base = base, acc, low
        base += s.chunks
        acc += s.accs
        if s.name not in RESIDUALS:
            low += s.accs
    return seq


RESIDUALS = ["pw2", "memo0", "down0", "foxo", "memo1", "down1", "dn1", "out", "dn2"]
PLAN = plan()
STAGE = {s.name: s for s in PLAN}
N_CHUNKS = PLAN[-1].base + PLAN[-1].chunks

NORMS = [("mix0", 1), ("mem0", 1), ("memq0", 1), ("ff0", 1), ("fox", 2), ("mem1", 1), ("memq1", 1),
         ("ff1", 1), ("final1", 0), ("ffa", 1), ("mixn", 1), ("ffb", 1), ("final2", 0)]
DEFERRED = {"pw1": "mix0", "memq0": "memq0", "up0": "ff0", "memq1": "memq1", "up1": "ff1"}
LN_TABLE = 3
ATTENTIONS = [("mem0", MEM_HEADS, MEM_HEADS), ("fox", HEADS, HEADS // 2), ("mem1", MEM_HEADS, MEM_HEADS),
              ("moba", G_HEADS, G_HEADS)]


def elems_of(n):
    return next(s.elems for s in PLAN if s.base <= n < s.base + s.chunks)


def x_ready(name, p):
    if name in RESIDUALS:
        return [("acc_summed", STAGE[name].acc_base + p + 1)]
    return [("x_normed", p + 1)]


def scaled_base(stage):
    names = list(DEFERRED)
    return sum(STAGE[n].accs for n in names[:names.index(stage)])


def norm_index(name):
    return [n for n, _ in NORMS].index(name)


def norm_base(name):
    return PAIRS * sum(k for _, k in NORMS[:norm_index(name)])


def head_base(name):
    i = [a[0] for a in ATTENTIONS].index(name)
    return sum(a[1] for a in ATTENTIONS[:i]), sum(a[2] for a in ATTENTIONS[:i])


def gla_at(h):
    return 2 * (h % 2) + h // 2


def spread(ap, n):
    return ap.unsqueeze(1).to_broadcast([ap.shape[0], n, ap.shape[1]])


def program(nc, dram, out):
    ctx = ExitStack()
    with ctx:
        cursor = [-(-nc.sbuf_base // 32) * 32]

        def place(name, shape, dt=F32, at=None):
            size = int(np.prod(shape[1:])) * (2 if dt == BF16 else 4)
            if at is None:
                at = cursor[0]
                cursor[0] += -(-size // 32) * 32
            return nc.alloc_sbuf_tensor_at(name, shape, dt, offset=at)

        raw = place("raw", [P, RING, KT * 256])
        wsplit = place("wsplit", [P, RING, 2, KT * 256], F32R)
        x = place("x", [P, KT, T])
        rel_rows = place("rel_rows", [P, G_HEADS, SKEW], at=cursor[0])
        hA = place("hA", [P, KT, 2 * T], F32R)
        tsum = place("tsum", [P, 2, 2, T])
        aux = place("aux", [P, 2, 2, T])
        lowp = place("lowp", [P, 2, T])
        rstd = place("rstd", [P, T])
        var = place("var", [P, T])
        cols = place("cols", [P, NCOL])
        mod = place("mod", [P, N_MOD * KT])
        cact = place("cact", [P, KT])
        ones = place("ones", [P, P])
        ident = place("ident", [P, P])
        ident_bf = place("ident_bf", [P, P], BF16)
        mask_bf = place("mask_bf", [P, 2 * P], BF16)
        ones_bf = place("ones_bf", [3, P], BF16)
        small = place("small", [P, 4, TT * HEADS])
        ada_w = place("ada_w", [P, 2, KT, HALF])
        ada_acc = place("ada_acc", [P, SEGMENT, P])

        region = cursor[0]
        KB = 1024

        def phased(name, shape, kb, dt=F32):
            return place(name, shape, dt, at=region + int(kb * KB))

        hid = phased("hid", [P, KF, 2 * T], 0, F32R)
        hM = phased("hM", [P, KT, 2 * T], 0, F32R)
        memx0 = phased("memx0", [P, KT, T], 16)
        mk0 = phased("mk0", [P, KT, T], 24)
        mv0 = phased("mv0", [P, TT, D], 32)
        upad = phased("upad", [P, KT, PAD + T], 40)
        conv = phased("conv", [P, KT, T], 49)
        taps = phased("taps", [P, TAPS, KT], 57)
        mu = phased("mu", [P, T], 58)
        relrep = phased("relrep", [BUCKETS + 1, G_HEADS, P], 59)
        onehot = phased("onehot", [BUCKETS + 1, SKEW], 61)
        relT = phased("relT", [BUCKETS + 1, G_HEADS], 57.96875)
        pool_tmp = phased("pool_tmp", [P, T], 63)
        mq0 = phased("mq0", [P, KT, T], 40)
        prob0 = phased("prob0", [P, 2, TT, T], 49)
        probT0 = phased("probT0", [P, 2, TT, T], 53)
        hB = phased("hB", [P, KT, 2 * T], 0, F32R)
        memx1 = phased("memx1", [P, KT, T], 16)
        mk1 = phased("mk1", [P, KT, T], 24)
        mv1 = phased("mv1", [P, TT, D], 32)
        fq = phased("fq", [P, KT, T], 40)
        fk = phased("fk", [P, KT, T], 48)
        fv = phased("fv", [P, TT, D], 56)
        fo = phased("fo", [P, 2, KT, T], 40, F32R)
        negc_row = phased("negc_row", [3, HEADS, T], 0, BF16)
        tri = phased("tri", [P, TT, T], 32)
        negc = phased("negc", [P, T], 34)
        negc_part = phased("negc_part", [P, 3, T], 35, BF16)
        prob1 = phased("prob1", [P, 2, TT, T], 16)
        probT1 = phased("probT1", [P, 2, TT, T], 20)
        mq1 = phased("mq1", [P, KT, T], 40)
        inT = phased("inT", [P, 16, T], 0)
        inV = phased("inV", [P, TT, D], 16)
        gates = phased("gates", [P, KT, 2, T], 24)
        loga = phased("loga", [P, TT, T], 40)
        wlr = phased("wlr", [17, T], 42)
        decay = phased("decay", [P, 2, T], 42)
        qe = phased("qe", [P, 2, T], 44)
        ke = phased("ke", [P, 2, T], 46)
        za = phased("za", [P, TT, T], 44)
        zl = phased("zl", [P, TT, T], 46)
        A_same = phased("A_same", [P, 2 * G_HEADS, P], 48)
        A_next = phased("A_next", [P, G_HEADS, P], 52)
        spans = phased("spans", [P, NL + 2, P], 54)
        lmask = phased("lmask", [P, NL + 1, P], 58.5)
        glrT = phased("glrT", [32, T], 62.5)
        o_gla = phased("o_gla", [P, G_HEADS, T], 48)
        toep = phased("toep", [P, G_HEADS, 3 * P], 42)
        prob2 = phased("prob2", [P, 2, TT, T], 54)
        probT2 = phased("probT2", [P, 2, TT, T], 58)
        assert region + 64 * KB <= nc.sbuf_usable_end, (region + 64 * KB, nc.sbuf_usable_end)

        def pb(name, shape):
            return ctx.enter_context(nc.psum_tensor(name, shape, F32))

        acc = pb("acc", [P, 2, 2, 2 * T])
        score = pb("score", [P, 2, TT, T])
        turned = pb("turned", [P, TT, T])
        stat = pb("stat", [P, 2, T])

        skew_dram = nc.dram_tensor("skew_dram", (G_HEADS, P, SKEW), F32, kind="Internal").ap()

        sems = {}

        def S(name):
            if name not in sems:
                sems[name] = ctx.enter_context(nc.semaphore(name))
            return sems[name]

        def col(name, i=0, n=1):
            return cols[:, COL[name] + i:COL[name] + i + n]

        raw_loaded = [S(f"raw_loaded{i}") for i in range(RING)]
        ada_loaded = [S(f"ada_loaded{i}") for i in range(2)]

        def groups(eng, n_chunks, body, unroll=RING, lead=0, tail=0, begun=0):
            first = lead
            last = max(first, (n_chunks - tail) // unroll * unroll)
            if last - first < 2 * unroll:
                first = last = begun
            for c in range(begun, first):
                body(c, c)
            if last > first:
                with eng.Fori(first // unroll, last // unroll) as i:
                    for k in range(unroll):
                        body(i * unroll + k, first + k)
            for c in range(last, n_chunks):
                body(c, c)

        def memory_chunks(keys, values):
            return [(keys, c) for c in range(1, 4)] + [(values, c) for c in range(4)]

        def memory_between(keys, values):
            return {2 * i + 1: (lambda f=f, c=c: f(c, c)) for i, (f, c) in enumerate(memory_chunks(keys, values))}

        LEVEL_SLOTS = [("inrows", c) for c in range(4)] + [("ingates", c) for c in range(NL + 2 - 4)]
        LEVEL_OF = {slot: lv for lv, slot in enumerate(LEVEL_SLOTS)}
        VALUES_AT = NL + 2 - 4
        SUMS_AT = VALUES_AT + 1
        span_banks = [turned, stat]
        A_ps = score[:].rearrange("p a b (c t) -> p (a b c) t", c=2)

        block = ctx.enter_context(nc.Block())

        @block.sync
        def _(sp):
            sp.dma_start(x[:], dram["xT"]).then_inc(S("x_loaded"), 16)
            sp.dma_start(cols[:], dram["cols"]).then_inc(S("cols_loaded"), 16)
            sp.dma_start(ones[:], dram["ones"]).then_inc(S("ones_loaded"), 16)

            def load(st, c, known):
                slot = (st.base + known) % RING
                if st.base + known >= RING:
                    sp.wait_ge(S("w_lo"), c + (st.base - RING + 1))
                sp.dma_start(raw[:, slot, 0:st.elems], dram[st.name][c]).then_inc(raw_loaded[slot], 16)

            for c in range(RING):
                load(PLAN[0], c, c)
                if c == 1:
                    for tensor, name in ((taps, "taps"), (ident, "ident"), (onehot, "onehot"), (relT, "relT"),
                                         (mask_bf, "mask")):
                        sp.dma_start(tensor[:], dram[name]).then_inc(S("consts_loaded"), 16)
            sp.dma_start(memx0[:], dram["memT"]).then_inc(S("mem_loaded"), 16)
            for st in PLAN:
                groups(sp, st.chunks, lambda c, known: load(st, c, known), begun=RING if st.base == 0 else 0,
                       lead=RING if st.base == 0 else 0)
            for p in range(PAIRS):
                sp.wait_ge(S("final_ready"), p + 1)
                sp.dma_start(out[:, 2 * p:2 * p + 2, :], x[:, 2 * p:2 * p + 2, :]).then_inc(S("stored"), 16)
            sp.wait_ge(S("stored"), 16 * PAIRS)

        @block.tensor
        def _(pe):
            def weights_ready(st, c):
                pe.wait_ge(S("w_hi"), c + (st.base + 1))
                pe.wait_ge(S("w_lo"), c + (st.base + 1))

            def acc_free(st, a, known_a):
                if st.acc_base + known_a >= 2:
                    pe.wait_ge(S("acc_summed"), a + (st.acc_base - 1))

            def tile_of(hl):
                return lambda kt: hl[:, kt, :].rearrange("p (s t) -> p s t", s=2)

            def block_cols(dst, w, lo_w, h, start, stop):
                nc.tensor.matmul(dst.rearrange("p (s t) -> p s t", s=2), w, h, start=start, stop=False,
                                 skip_group_check=True)
                return nc.tensor.matmul(dst[:, 0:T], lo_w, h[:, 0, :], start=False, stop=stop,
                                        skip_group_check=True)

            def chunk_cols(st, slot, par, h, kts, cols_of, start, stop, ready):
                for i, kt in enumerate(kts):
                    if ready and kt in ready:
                        for sem, value in ready[kt]:
                            pe.wait_ge(sem, value)
                    for j, at in cols_of(i):
                        mm = block_cols(acc[:, par, j, :], wsplit[:, slot, 0, at:at + P],
                                        wsplit[:, slot, 1, at:at + P], h(kt),
                                        start and i == 0, stop and i == len(kts) - 1)
                return mm

            def linear(name, h, ready, after=None, steps=False):
                st = STAGE[name]
                h = h if callable(h) else tile_of(h)

                def body(c, known, half=None):
                    slot = (st.base + known) % RING
                    kt_all = list(range(KT)) if half is None else list(range(half * PAIRS, (half + 1) * PAIRS))
                    begins, ends = half in (None, 0), half in (None, 1)
                    if st.per_acc == 1:
                        a, known_a, q = c, known, 0
                    else:
                        q = known % st.per_acc
                        a, known_a = None, known // st.per_acc
                    if begins:
                        weights_ready(st, c)
                    par = (st.acc_base + known_a) % 2
                    if st.per_acc == 1 and begins:
                        acc_free(st, a, known_a)
                    elif st.per_acc > 1 and q == 0:
                        acc_free(st, known_a, known_a)
                    w = wsplit[:, slot, :, :]
                    if st.kind == "cols":
                        mm = chunk_cols(st, slot, par, h, kt_all,
                                        lambda i: [(j, (kt_all[0] + i) * 2 * P + j * P) for j in range(2)],
                                        begins, ends, ready)
                    elif st.kind == "deep32":
                        mm = chunk_cols(st, slot, par, h, [q * KT + i for i in range(KT)],
                                        lambda i: [(j, i * 2 * P + j * P) for j in range(2)],
                                        q == 0, q == 3, ready)
                    elif st.kind == "deep22":
                        mm = chunk_cols(st, slot, par, h, [(q % 2) * 11 + i for i in range(11)],
                                        lambda i: [(q // 2, i * P)], q % 2 == 0, q % 2 == 1, ready)
                    elif st.kind == "branch":
                        for br in range(2):
                            mm = chunk_cols(st, slot, par, h, [4 * br + i for i in range(4)],
                                            lambda i: [(br, (4 * br + i) * P)], True, True, ready)
                    else:
                        n = 256 if st.kind == "rows" else HEADS
                        for kt in kt_all:
                            if ready and kt in ready:
                                for sem, value in ready[kt]:
                                    pe.wait_ge(sem, value)
                            for tt in range(TT):
                                dst = acc[:, par, tt, 0:2 * n]
                                nc.tensor.matmul(dst.rearrange("p (s n) -> p s n", s=2),
                                                 h(kt)[:, 0, tt * P:(tt + 1) * P],
                                                 w[:, :, kt * n:(kt + 1) * n],
                                                 start=kt == 0, stop=False, skip_group_check=True)
                                mm = nc.tensor.matmul(dst[:, 0:n], h(kt)[:, 1, tt * P:(tt + 1) * P],
                                                      w[:, 0, kt * n:(kt + 1) * n],
                                                      start=False, stop=kt == KT - 1,
                                                      skip_group_check=True)
                    if ends:
                        mm.then_inc(S("chunk_done"), 1)
                        if after and (st.per_acc > 1 or known < RING or st.chunks < 3 * RING):
                            after(known)

                def part(c, p):
                    slot, par = (st.base + c) % RING, (st.acc_base + c) % 2
                    if p == 0:
                        weights_ready(st, c)
                        acc_free(st, c, c)
                    mm = chunk_cols(st, slot, par, h, [2 * p, 2 * p + 1],
                                    lambda i: [(j, (2 * p + i) * 2 * P + j * P) for j in range(2)],
                                    p == 0, p == PAIRS - 1, ready)
                    if p == PAIRS - 1:
                        mm.then_inc(S("chunk_done"), 1)
                        if after:
                            after(c)

                def begin():
                    for c, p in ((0, 0), (1, 0), (0, 1), (1, 1), (0, 2), (0, 3), (1, 2), (1, 3)):
                        part(c, p)
                        if (c, p) == (1, 0) and name in DEFERRED and name != "pw1":
                            norm_sums(DEFERRED[name], [PAIRS - 2, PAIRS - 1])

                if steps:
                    return begin, body
                if st.per_acc > 1:
                    for c in range(st.chunks):
                        body(c, c)
                elif st.kind == "cols" and ready:
                    begin()
                    groups(pe, st.chunks, body, lead=RING, begun=2)
                else:
                    groups(pe, st.chunks, body, lead=RING)

            def pair_ready(base):
                return {2 * p: [(S("norm_lo"), base + p + 1)] for p in range(PAIRS)}

            def norm_sums(name, pairs=range(PAIRS)):
                q = norm_index(name)
                for p in pairs:
                    pe.wait_ge(S("norm_sq"), PAIRS * q + p + 1)
                    if p == 0 and q > 0:
                        stat_read(q)
                    for j in range(2):
                        mm = nc.tensor.matmul(stat[:, 0, :], ones[:], aux[:, p % 2, j, :],
                                              start=p == 0 and j == 0, stop=p == PAIRS - 1 and j == 1)
                    mm.then_inc(S("norm_stat"), 1)

            def stat_read(q):
                pe.wait_ge(S("norm_var"), q)

            segments_summed = [0]

            def modulation_read():
                if segments_summed[0]:
                    pe.wait_ge(S("mod_made"), segments_summed[0])

            def keep_clock(n):
                pe.wait_ge(S("ident_bf"), 1)
                modulation_read()
                for _ in range(n):
                    nc.tensor.matmul(turned[:, 0, :], ident_bf[:], mask_bf[:], start=True, stop=True)

            def residual(name, h, ready, norm, segments={}):
                per = STAGE[name].per_acc
                lag = 2 if per == 1 else 1
                early = []

                def after(c):
                    if c in segments:
                        ada(segments[c])
                    if (c + 1 - lag) % per == 0 and c + 1 > lag:
                        early.append((c + 1 - lag) // per - 1)
                        norm_sums(norm, early[-1:])

                linear(name, h, ready, after=after)
                if norm in DEFERRED.values():
                    return
                norm_sums(norm, range(len(early), PAIRS - 1))
                keep_clock(10)
                norm_sums(norm, [PAIRS - 1])
                if norm != "final2":
                    keep_clock(40)

            def ada(seg):
                pe.wait_ge(S("ada_step"), 64 * (seg + 1))
                modulation_read()
                for m in range(SEGMENT):
                    mm = nc.tensor.matmul(turned[:, 0, m:m + 1], ada_acc[:, m, :], ones[:, 0:1],
                                          start=True, stop=True)
                mm.then_inc(S("ada_used"), 1)
                segments_summed[0] += 1

            def attention(name, q, k, v, prob, probT, extra, dh, ready, leads=(), between={}):
                _, n_heads, n_groups = next(a for a in ATTENTIONS if a[0] == name)
                b, gb = head_base(name)
                per_group = n_heads // n_groups
                causal = extra is not None

                def scores(h):
                    for sem, value in ready.get(h, []):
                        pe.wait_ge(sem, value)
                    if b + h >= 2:
                        pe.wait_ge(S("att_exp"), b + h - 1)
                    if causal:
                        extra(h)
                    off = (h * dh) % P
                    rows = min(dh, P)
                    tiles = [h * dh // P + i for i in range(max(1, dh // P))]
                    for qt in range(TT):
                        keys = P * (qt + 1) if causal else T
                        for i, kt in enumerate(tiles):
                            mm = nc.tensor.matmul(score[:, h % 2, qt, 0:keys],
                                                  q[off:off + rows, kt, qt * P:(qt + 1) * P],
                                                  k[off:off + rows, kt, 0:keys],
                                                  start=not causal and i == 0, stop=i == len(tiles) - 1,
                                                  skip_group_check=True)
                    mm.then_inc(S("att_scores"), 1)

                def queries(kt):
                    first = P * kt if causal else 0
                    return first, T * kt - first

                def turn(h):
                    pe.wait_ge(S("att_prob"), b + h + 1)
                    if b + h >= 1:
                        pe.wait_ge(S("att_turned"), b + h)
                    flat = turned[:].rearrange("p a t -> p (a t)")
                    for kt in range(TT):
                        first, at = queries(kt)
                        for qt in range(first // P, TT):
                            mm = nc.tensor.transpose(flat[:, at + qt * P:at + (qt + 1) * P],
                                                     prob[:, h % 2, qt, kt * P:(kt + 1) * P], ident[:])
                    mm.then_inc(S("att_turn"), 1)

                def values(h):
                    pe.wait_ge(S("att_turned"), b + h + 1)
                    g = h // per_group
                    if h % per_group == 0 and gb + g >= 1:
                        pe.wait_ge(S("att_lo"), gb + g)
                    weights = probT[:, h % 2, :, :].rearrange("p a t -> p (a t)")
                    off = (h * dh) % P
                    rows = min(dh, P)
                    for dt in range(max(1, dh // P)):
                        for kt in range(TT):
                            first, at = queries(kt)
                            mm = nc.tensor.matmul(stat[off:off + rows, dt, first:T],
                                                  v(kt, h * dh + dt * P, rows), weights[:, at + first:at + T],
                                                  start=kt == 0, stop=kt == TT - 1, skip_group_check=True)
                    mm.then_inc(S("att_out"), 1)

                leads = list(leads) + [None] * 3
                for i in range(2):
                    if leads[i]:
                        leads[i]()
                    if i == 0:
                        modulation_read()
                    scores(i)
                if leads[2]:
                    leads[2]()
                for h in range(n_heads):
                    turn(h)
                    if h + 2 < n_heads:
                        scores(h + 2)
                    if h in between:
                        between[h]()
                    values(h)

            def memory_attention(layer, hl, q, k, v, prob, probT):
                st = STAGE[f"memq{layer}"]
                begin, chunk = linear(st.name, hl, pair_ready(norm_base(st.name)), steps=True)
                attention(f"mem{layer}", q, k, lambda kt, at, n: v[:, kt, at:at + n], prob, probT, None, 256,
                          {h: [(S("acc_summed"), st.acc_base + h + 1)] for h in range(MEM_HEADS)},
                          leads=[begin, lambda: chunk(2, 2), lambda: chunk(3, 3)])

            pe.wait_ge(S("ones_loaded"), 16)
            norm_sums("mix0")
            linear("pw1", hA, pair_ready(norm_base("mix0")),
                   after=lambda c: norm_sums("mem0", [c - 3, c - 2]) if c in (3, 5) else None)

            def relative_biases(c):
                if c == 0:
                    pe.wait_ge(S("consts_loaded"), 16 * 5)
                    pe.wait_ge(S("rel_spread"), 1)
                else:
                    pe.wait_ge(S("rel_copied"), c)
                nc.tensor.matmul(turned[:].rearrange("p a b -> p (a b)"), relrep[:, c, :], onehot[:],
                                 start=True, stop=True).then_inc(S("rel_made"), 1)

            linear("memk0", hM, pair_ready(norm_base("mem0")), after=relative_biases)
            linear("memv0", hM, None)
            stat_read(norm_index("mem0") + 1)
            order = [0, 1, 3, 2, 5, 4, 6, 7]
            for i, kt in enumerate(order):
                if kt in G_TILES:
                    pe.wait_ge(S("conv_pool_step"), (G_TILES.index(kt) + 1) * (2 * TAPS - 1))
                else:
                    pe.wait_ge(S("conv_tile"), V_TILES.index(kt) + 1)
                mm = nc.tensor.matmul(stat[:, 0, :], ones[:], conv[:, kt, :], start=i == 0, stop=i == KT - 1)
            mm.then_inc(S("ln_stat"), 1)
            for p in range(PAIRS):
                pe.wait_ge(S("ln_sq"), p + 1)
                for j in range(2):
                    mm = nc.tensor.matmul(stat[:, 0, :], ones[:], aux[:, p % 2, j, :],
                                          start=p == 0 and j == 0, stop=p == PAIRS - 1 and j == 1)
                mm.then_inc(S("ln_stat"), 1)
            residual("pw2", hM, {2 * p: [(S("ln_lo"), p + 1)] for p in range(PAIRS)}, "memq0")
            memory_attention(0, hA, mq0, mk0, mv0, prob0, probT0)
            gb = head_base("mem0")[1]
            residual("memo0", hM, {2 * p: [(S("att_lo"), gb + p + 1)] for p in range(PAIRS)}, "ff0", {0: 0})
            linear("up0", hA, pair_ready(norm_base("ff0")))
            residual("down0", hid, {2 * c: [(S("up0_lo"), c + 1)] for c in range(KF // 2)}, "fox", {0: 1, 12: 2})

            nb = norm_base("fox")
            linear("foxk", hA, pair_ready(nb))
            linear("foxv", hA, None, after=lambda c: norm_sums("mem1", [2 * c, 2 * c + 1]) if c < 2 else None)
            linear("foxf", hA, None)

            def behind_queries(c):
                if c == 0:
                    ada(3)
                elif c == 2:
                    pe.wait_ge(S("logf_ready"), 1)
                    pe.wait_ge(S("tri_loaded"), 16)
                    modulation_read()
                    for tt in range(TT):
                        mm = nc.tensor.matmul(turned[0:HEADS, 0, :], small[:, 3, tt * HEADS:(tt + 1) * HEADS],
                                              tri[:, tt, :], start=tt == 0, stop=tt == TT - 1)
                    mm.then_inc(S("negc_made"), 1)

            linear("foxq", hB, pair_ready(nb + PAIRS), after=behind_queries)

            def fox_bias(h):
                bank = score[:, h % 2, :, :]
                nc.tensor.matmul(bank[:, 0, :], ident_bf[:], mask_bf[:], start=True, stop=False,
                                 skip_group_check=True)
                nc.tensor.matmul(bank[:, 1, P:T], ident_bf[:], mask_bf[:, 0:P], start=False, stop=False,
                                 skip_group_check=True)
                for qt in range(TT):
                    keys = P * (qt + 1)
                    nc.tensor.matmul(bank[:, qt, 0:keys], ones_bf[0:3, :], negc_row[0:3, h, 0:keys],
                                     start=False, stop=False, skip_group_check=True)

            _, memory_keys = linear("memk1", hA, pair_ready(norm_base("mem1")), steps=True)
            _, memory_values = linear("memv1", hA, None, steps=True)
            s = STAGE["foxq"]
            attention("fox", fq, fk, lambda kt, at, n: fv[:, kt, at:at + n], prob1, probT1, fox_bias, 64,
                      {0: [(S("acc_summed"), s.acc_base + s.accs), (S("negc_placed"), 48), (S("ident_bf"), 1)]},
                      leads=[lambda: memory_keys(0, 0)],
                      between={2 * i + half: (lambda f=f, c=c, half=half: f(c, c, half)) for half in range(2)
                               for i, (f, c) in enumerate(memory_chunks(memory_keys, memory_values))})
            gb = head_base("fox")[1]
            residual("foxo", lambda kt: fo[:, :, kt, :], {g: [(S("att_lo"), gb + g + 1)] for g in range(KT)}, "memq1", {0: 4})
            memory_attention(1, hA, mq1, mk1, mv1, prob1, probT1)
            gb = head_base("mem1")[1]
            residual("memo1", hB, {2 * p: [(S("att_lo"), gb + p + 1)] for p in range(PAIRS)}, "ff1", {0: 5})
            linear("up1", hA, pair_ready(norm_base("ff1")))
            residual("down1", hid, {2 * c: [(S("up1_lo"), c + 1)] for c in range(KF // 2)}, "final1", {0: 6, 12: 7})

            norm_sums("ffa")
            linear("gu1", hA, pair_ready(norm_base("ffa")))
            residual("dn1", hid, {c: [(S("gu1_lo"), c + 1)] for c in range(KF2)}, "mixn", {0: 8})
            linear("inlr", hA, pair_ready(norm_base("mixn")))
            def level_spans(lv):
                i = lv if lv < NL else NL
                if i >= 2:
                    pe.wait_ge(S("gla_exp"), i - 1)
                for ct in range(2):
                    for tt in range(TT):
                        m = lv if lv < NL else NL + tt
                        mm = nc.tensor.matmul(span_banks[i % 2][:, ct, tt * P:(tt + 1) * P],
                                              loga[:, tt, ct * P:(ct + 1) * P], spans[:, m, :],
                                              start=True, stop=True)
                mm.then_inc(S("gla_span"), 1)

            def level_scores(lv):
                own = lv < NL + 1
                if lv < NL:
                    pe.wait_ge(S("gla_qk"), 2 * (lv + 1))
                elif lv == NL + 1:
                    pe.wait_ge(S("gla_qk"), 2 * (NL + 1))
                if lv >= 1:
                    pe.wait_ge(S("gla_masked"), max(1, 2 * (lv - 1)))
                kk, qq = (inT[:, 2:4, :], inT[:, 0:2, :]) if lv == NL else (ke[:], qe[:])
                for h in range(G_HEADS):
                    off, ct = 64 * (h % 2), h // 2
                    for tt in range(TT if own else 1):
                        dst = A_ps[:, 2 * gla_at(h) + tt if own else 4 * (h % 2) + h // 2, :]
                        qt = tt if own else 1
                        mm = nc.tensor.matmul(dst, kk[off:off + 64, ct, tt * P:(tt + 1) * P],
                                              qq[off:off + 64, ct, qt * P:(qt + 1) * P],
                                              start=True, stop=True, skip_group_check=True)
                mm.then_inc(S("gla_scores"), 1)

            def gla_values():
                pe.wait_ge(S("gla_masked"), 2 * (NL + 1))
                for h in range(G_HEADS):
                    dst = score[:, h // 2, h % 2, :]
                    nc.tensor.matmul(dst[:, 0:P], inV[:, 0, h * P:(h + 1) * P], A_same[:, 2 * gla_at(h), :],
                                     start=True, stop=True, skip_group_check=True)
                    nc.tensor.matmul(dst[:, P:T], inV[:, 0, h * P:(h + 1) * P], A_next[:, gla_at(h), :],
                                     start=True, stop=False, skip_group_check=True)
                    mm = nc.tensor.matmul(dst[:, P:T], inV[:, 1, h * P:(h + 1) * P], A_same[:, 2 * gla_at(h) + 1, :],
                                          start=False, stop=True, skip_group_check=True)
                mm.then_inc(S("gla_out"), 1)

            def gla_sums():
                pe.wait_ge(S("gla_sq"), 1)
                pe.wait_ge(S("gla_exp"), NL + 1)
                for i in range(2):
                    mm = nc.tensor.matmul(span_banks[i][:].rearrange("p a t -> p (a t)"), ones[:],
                                          aux[:, i, :, :].rearrange("p a t -> p (a t)"), start=True, stop=True)
                mm.then_inc(S("gla_stat"), 1)

            def behind_incols(c):
                if c == 0:
                    pe.wait_ge(S("acc_summed"), STAGE["inlr"].acc_base + 1)
                    for tt in range(TT):
                        mm = nc.tensor.transpose(turned[0:16, 0, tt * P:(tt + 1) * P],
                                                 small[:, 0, tt * 16:(tt + 1) * 16], ident[:])
                    mm.then_inc(S("lr_turn"), 1)
                elif c == 1:
                    pe.wait_ge(S("lr_turned"), 2)
                    pe.wait_ge(S("wlr_loaded"), 16)
                    for tt in range(TT):
                        mm = nc.tensor.matmul(turned[:, tt, :], glrT[0:17, tt * P:(tt + 1) * P], wlr[:],
                                              start=True, stop=True)
                    mm.then_inc(S("lr_logits"), 1)
                elif c == 5:
                    pe.wait_ge(S("loga_ready"), 1)
                    pe.wait_ge(S("spans_loaded"), 32)
                    level_spans(0)

            def behind_mixing(stage):
                def after(c):
                    lv = LEVEL_OF.get((stage, c))
                    if lv is not None:
                        if lv == 0:
                            stat_read(norm_index("mixn") + 1)
                        if lv + 1 < NL:
                            level_spans(lv + 1)
                        elif lv == NL:
                            level_spans(NL + 1)
                        level_scores(lv)
                    elif stage == "ingates" and c == VALUES_AT:
                        gla_values()
                    elif stage == "ingates" and c == SUMS_AT:
                        gla_sums()
                return after

            linear("incols", hA, None, after=behind_incols)
            linear("inrows", hA, None, after=behind_mixing("inrows"))
            _, gate_chunk = linear("ingates", hA, None, after=behind_mixing("ingates"), steps=True)
            for c in range(KT - 1):
                gate_chunk(c, c)

            def moba_bias(h):
                nc.tensor.matmul(score[:, h % 2, 0, :], ident[:], toep[:, h, P:3 * P], start=True,
                                 stop=False, skip_group_check=True)
                nc.tensor.matmul(score[:, h % 2, 1, :], ident[:], toep[:, h, 0:2 * P], start=False,
                                 stop=False, skip_group_check=True)

            attention("moba", inT[:, 8:12, :], inT[:, 12:16, :],
                      lambda kt, at, n: inV[:, kt, 512 + at:512 + at + n], prob2, probT2, moba_bias, P,
                      {0: [(S("gla_kept"), 1), (S("toep_loaded"), 16)], 1: [(S("gla_var"), 2)]},
                      leads=[None, lambda: gate_chunk(KT - 1, KT - 1)])
            gb = head_base("moba")[1]
            linear("branch", hA, {0: [(S("gla_lo"), 1)], 4: [(S("att_lo"), gb + 1)], 5: [(S("att_lo"), gb + 2)],
                                  6: [(S("att_lo"), gb + 3)], 7: [(S("att_lo"), gb + 4)]})
            residual("out", hM, {c: [(S("branch_lo"), c + 1)] for c in range(KT)}, "ffb")
            linear("gu2", hA, pair_ready(norm_base("ffb")))
            residual("dn2", hid, {c: [(S("gu2_lo"), c + 1)] for c in range(KF2)}, "final2")

        @block.scalar
        def _(act):
            def wait(sem, value):
                act.wait_ge(S(sem), value)

            def split_hi(st, c, known):
                n = st.base + known
                slot = n % RING
                act.wait_ge(raw_loaded[slot], (c - known) * (16 // RING) + 16 * (n // RING + 1))
                if n >= RING:
                    wait("chunk_done", c + (st.base - RING + 1))
                nc.scalar.activation(wsplit[:, slot, 0, 0:elems_of(n)], raw[:, slot, 0:elems_of(n)],
                                     ACT.Copy).then_inc(S("w_hi"), 1)

            def low(st, a, known_a, width=T):
                par = (st.acc_base + known_a) % 2
                wait("chunk_done", a * st.per_acc + (st.base + st.per_acc))
                if st.acc_base + known_a >= 1:
                    wait("acc_summed", a + st.acc_base)
                last = nc.scalar.activation(lowp[:, :, 0:width], acc[:, par, :, width:2 * width], ACT.Copy)
                last.then_inc(S("acc_low"), 1)

            def linear(name, post=None, flush=None, width=T, steps=False, late=False):
                st = STAGE[name]

                def body(c, known):
                    if st.per_acc == 1:
                        if name not in RESIDUALS:
                            low(st, c, known, width)
                        if post:
                            post(c, known)
                    elif known % st.per_acc == 0 and post:
                        post(known // st.per_acc, known // st.per_acc)
                    if st.base + known + RING < N_CHUNKS and not (late and known == st.chunks - 1):
                        split_hi(st, c + RING, known + RING)

                if steps:
                    return body
                if st.per_acc == 1 and name != "pw1":
                    groups(act, st.chunks, body, lead=RING, tail=RING)
                else:
                    for c in range(st.chunks):
                        body(c, c)
                if flush:
                    flush()

            def norm_squares(name, src, ready, pairs=range(PAIRS)):
                q = norm_index(name)
                for p in pairs:
                    for sem, value in ready(p):
                        wait(sem, value)
                    if p >= 2:
                        wait("norm_stat", PAIRS * q + p - 1)
                    nc.scalar.activation(aux[:, p % 2, :, :], src[:, 2 * p:2 * p + 2, :],
                                         ACT.Square).then_inc(S("norm_sq"), 1)

            def inverse_root(sem, n, src, r, scale=1.0, bias=0.0):
                nc.scalar.activation(r, src, ACT.Ln, scale=scale, bias=bias).then_inc(S(sem), 1)
                wait(sem, n + 1)
                nc.scalar.activation(r, r, ACT.Exp, scale=-0.5).then_inc(S(sem), 1)

            def norm_root(name):
                q = norm_index(name)
                wait("norm_stat", PAIRS * (q + 1))
                wait("log_table", q + (1 if q < LN_TABLE - 1 else 2))
                inverse_root("norm_root", 2 * q, stat[:, 0, :], rstd[:], 1 / D, col("rms_eps"))

            def norm_hi(name, dest, which=0, shift=None, pairs=range(PAIRS)):
                nb = norm_base(name) + PAIRS * which
                for p in pairs:
                    wait("norm_h", nb + p + 1)
                    if shift is None:
                        last = nc.scalar.activation(dest[:, 2 * p:2 * p + 2, 0:T], tsum[:, p % 2, :, :], ACT.Copy)
                    else:
                        for j in range(2):
                            last = nc.scalar.activation(dest[:, 2 * p + j, 0:T], tsum[:, p % 2, j, :],
                                                        ACT.Identity, bias=mod[:, shift + 2 * p + j:shift + 2 * p + j + 1])
                    last.then_inc(S("norm_hi"), 1)

            def log_table(name):
                nc.scalar.activation(rstd[:, 0:1], col("rms_eps"), ACT.Ln).then_inc(S("log_table"), 1)

            def norm(name, src, ready, dests, shift=None):
                norm_squares(name, src, ready)
                log_table(name)
                norm_root(name)
                for i, dest in enumerate(dests):
                    norm_hi(name, dest, i, shift)

            def residual(name, norm_name, dests, shift=None):
                st = STAGE[name]

                def ready(p):
                    return x_ready(name, p)

                deferred = norm_name in DEFERRED.values()

                def pair_done(p):
                    norm_squares(norm_name, x, ready, [p])
                    if deferred:
                        norm_hi(norm_name, dests[0], pairs=[p])

                def flush():
                    log_table(norm_name)
                    pair_done(PAIRS - 1)

                linear(name, late=not deferred, flush=flush,
                       post=lambda a, ka: pair_done(a - 1) if ka >= 1 else None)
                norm_root(norm_name)
                if deferred:
                    return
                if st.base + st.chunks - 1 + RING < N_CHUNKS:
                    split_hi(st, st.chunks - 1 + RING, st.chunks - 1 + RING)
                for i, dest in enumerate(dests):
                    norm_hi(norm_name, dest, i, shift)

            def hidden_hi(name, dest):
                def post(c, known):
                    wait(f"{name}_r", c + 1)
                    par = (STAGE[name].acc_base + known) % 2
                    if dest is hid and name.startswith("up"):
                        out_ap = hid[:].rearrange("p (c j) t -> p c j t", j=2)[:, c, :, 0:T]
                        nc.scalar.activation(out_ap, tsum[:, par, :, :], ACT.Copy).then_inc(S(f"{name}_hi"), 1)
                    else:
                        nc.scalar.activation(dest[:, c, 0:T], tsum[:, par, 0, :],
                                             ACT.Copy).then_inc(S(f"{name}_hi"), 1)
                return post

            def feed_forward(up):
                hi = hidden_hi(up, hid)
                n = STAGE[up].chunks
                linear(up, post=lambda c, known: hi(c - 1, known - 1) if known >= 1 else None,
                       flush=lambda: hi(n - 1, n - 1))

            def gated_feed_forward(gu):
                hi = hidden_hi(gu, hid)
                n = STAGE[gu].chunks

                def post(c, known):
                    if known >= 1:
                        hi(c - 1, known - 1)
                    par = (STAGE[gu].acc_base + known) % 2
                    wait("acc_summed", c + (STAGE[gu].acc_base + 1))
                    nc.scalar.activation(aux[:, par, 0, :], tsum[:, par, 0, :],
                                         ACT.Sigmoid).then_inc(S(f"{gu}_sig"), 1)

                linear(gu, post=post, flush=lambda: hi(n - 1, n - 1))

            def attention(name, scale, prob, probT, dest, leads=(), between={}):
                _, n_heads, n_groups = next(a for a in ATTENTIONS if a[0] == name)
                b, gb = head_base(name)
                per_group = n_heads // n_groups
                tiles = 2 if name.startswith("mem") else 1

                def exps(h):
                    wait("att_max", 2 * (b + h + 1))
                    if h >= 2:
                        wait("att_turn", b + h - 1)
                    for qt in range(TT):
                        at = 2 * h + qt
                        last = nc.scalar.activation(prob[:, h % 2, qt, :], score[:, h % 2, qt, :], ACT.Exp,
                                                    bias=small[:, 1, at:at + 1], scale=scale,
                                                    accum_out=small[:, 2, at:at + 1])
                    last.then_inc(S("att_exp"), 1)

                def out_hi(g):
                    wait("att_out", b + per_group * (g + 1))
                    nc.scalar.activation(dest(g * tiles, tiles), stat[:, 0:tiles, :], ACT.Copy).then_inc(S("att_hi"), 1)

                leads = list(leads) + [None] * 3
                for i in range(3):
                    if leads[i]:
                        leads[i]()
                    if i < 2:
                        exps(i)
                for h in range(n_heads):
                    wait("att_turn", b + h + 1)
                    if h >= 2:
                        wait("att_out", b + h - 1)
                    src, dst = turned[:], probT[:, h % 2, :, :]
                    if name in ("fox", "moba"):
                        used = T + P
                        src = src.rearrange("p a t -> p (a t)")[:, 0:used]
                        dst = dst.rearrange("p a t -> p (a t)")[:, 0:used]
                    nc.scalar.activation(dst, src, ACT.Copy).then_inc(S("att_turned"), 1)
                    if h + 2 < n_heads:
                        exps(h + 2)
                    if h in between:
                        between[h]()
                    if (h + 1) % per_group == 0:
                        out_hi(h // per_group)

            def memory_attention(layer, prob, probT, dest):
                chunk = linear(f"memq{layer}", steps=True)
                attention(f"mem{layer}", 1 / 16, prob, probT, lambda at, n: dest[:, at:at + n, 0:T],
                          leads=[lambda: (chunk(0, 0), chunk(1, 1)), lambda: chunk(2, 2), lambda: chunk(3, 3)])

            def log_sigmoid(z, za_, zl_, sem, first):
                wait(sem, first)
                nc.scalar.activation(za_, z, ACT.Abs).then_inc(S(sem + "_ln"), 1)
                wait(sem + "_ln", 1)
                nc.scalar.activation(zl_, za_, ACT.Exp, scale=-1.0).then_inc(S(sem + "_ln"), 1)
                wait(sem + "_ln", 2)
                nc.scalar.activation(za_, zl_, ACT.Ln, bias=1.0).then_inc(S(sem + "_ln"), 1)

            wait("cols_loaded", 16)
            log_table("mix0")
            for p in range(PAIRS):
                norm_squares("mix0", x, lambda p: [("x_loaded", 16)], [p])
                norm_hi("mix0", hA, pairs=[p])
            for n in range(2):
                split_hi(PLAN[0], n, n)
            norm_root("mix0")
            for n in range(2, RING):
                split_hi(PLAN[0], n, n)

            def glu(c, known):
                wait("acc_summed", c + 1)
                nc.scalar.activation(upad[:, c, PAD:PAD + T], tsum[:, c % 2, 1, :], ACT.Sigmoid,
                                     bias=col("pw1_b", KT + c)).then_inc(S("pw1_sig"), 1)
                if c in (2, 4):
                    norm_squares("mem0", memx0, lambda p: [("mem_loaded", 16)], [c - 2, c - 1])

            linear("pw1", post=glu)
            log_table("mem0")
            norm_root("mem0")
            norm_hi("mem0", hM)
            wait("consts_loaded", 16 * 5)
            nc.scalar.activation(cact[:], col("cond", 0, KT), ACT.Sigmoid).then_inc(S("cond_sig"), 1)
            nc.scalar.activation(ident_bf[:], ident[:], ACT.Copy).then_inc(S("ident_bf"), 1)
            for h in range(G_HEADS):
                last = nc.scalar.activation(relrep[:, h, :], relT[:, h:h + 1].to_broadcast([BUCKETS + 1, P]), ACT.Copy)
            last.then_inc(S("rel_spread"), 1)

            def copy_biases(c, known):
                row = rel_rows[:, c, :]
                wait("rel_made", c + 1)
                nc.scalar.activation(row, turned[:].rearrange("p a t -> p (a t)"),
                                     ACT.Copy, scale=float(P) ** 0.5).then_inc(S("rel_copied"), 1)
                wait("rel_copied", c + 1)
                act.dma_start(skew_dram[c], row).then_inc(S("skew_stored"), 16)

            linear("memk0", post=copy_biases)
            linear("memv0")
            nc.scalar.activation(rstd[:, 0:1], col("ln_eps"), ACT.Ln).then_inc(S("log_table"), 1)
            for p in range(PAIRS):
                wait("ln_centred", p + 1)
                if p >= 2:
                    wait("ln_stat", p)
                nc.scalar.activation(aux[:, p % 2, :, :], conv[:, 2 * p:2 * p + 2, :], ACT.Square).then_inc(S("ln_sq"), 1)
            wait("log_table", LN_TABLE)
            wait("ln_stat", 1 + PAIRS)
            inverse_root("ln_root", 0, stat[:, 0, :], rstd[:], 1 / D, col("ln_eps"))
            wait("skew_stored", 16 * G_HEADS)
            for p in range(PAIRS):
                wait("ln_y", p + 1)
                if p >= 2:
                    wait("ln_lo", p - 1)
                for j in range(2):
                    kt = 2 * p + j
                    nc.scalar.activation(aux[:, p % 2, j, :], conv[:, kt, :], ACT.Sigmoid,
                                         bias=col("ln_b", kt), scale=col("ln_g", kt))
                    last = nc.scalar.activation(tsum[:, p % 2, j, :], conv[:, kt, :], ACT.Identity,
                                                bias=col("ln_b", kt), scale=col("ln_g", kt))
                last.then_inc(S("ln_sig"), 1)
                if p >= 1:
                    wait("ln_r", p)
                    nc.scalar.activation(hM[:, 2 * p - 2:2 * p, 0:T], tsum[:, (p - 1) % 2, :, :], ACT.Copy).then_inc(S("ln_hi"), 1)
            wait("ln_r", PAIRS)
            nc.scalar.activation(hM[:, KT - 2:KT, 0:T], tsum[:, 1, :, :], ACT.Copy).then_inc(S("ln_hi"), 1)
            residual("pw2", "memq0", [hA])
            memory_attention(0, prob0, probT0, hM)
            residual("memo0", "ff0", [hA])
            feed_forward("up0")

            residual("down0", "fox", [hA, hB])
            s = STAGE["down0"]
            wait("chunk_done", s.base + s.chunks)
            act.dma_start(memx1[:], dram["memT"]).then_inc(S("mem1_loaded"), 16)
            act.dma_start(tri[:], dram["tri"]).then_inc(S("tri_loaded"), 16)
            linear("foxk")
            memory_ready = lambda p: [("mem1_loaded", 16)]
            norm_squares("mem1", memx1, memory_ready, [0, 1])
            linear("foxv", post=lambda c, known: norm_squares("mem1", memx1, memory_ready, [2, 3]) if known == 0 else None)
            log_table("mem1")
            linear("foxf", width=HEADS)
            norm_root("mem1")
            norm_hi("mem1", hA)
            log_sigmoid(small[:, 0, :], small[:, 1, :], small[:, 2, :], "fgate_z", 1)
            linear("foxq")
            for i in range(3):
                wait("negc_ready", i + 1)
                act.dma_start(negc_row[i:i + 1, :, :], negc_part[0:HEADS, i, :]).then_inc(S("negc_placed"), 16)
            memory_keys, memory_values = linear("memk1", steps=True), linear("memv1", steps=True)
            attention("fox", 1 / 8, prob1, probT1, lambda at, n: fo[:, 0, at:at + n, :],
                      leads=[lambda: memory_keys(0, 0)], between=memory_between(memory_keys, memory_values))
            residual("foxo", "memq1", [hA])
            memory_attention(1, prob1, probT1, hB)
            residual("memo1", "ff1", [hA])
            feed_forward("up1")
            residual("down1", "final1", [])

            norm("ffa", x, lambda p: x_ready("final1", p), [hA], shift=0)
            gated_feed_forward("gu1")
            residual("dn1", "mixn", [hA], shift=3 * KT)
            s = STAGE["dn1"]
            wait("chunk_done", s.base + s.chunks)
            act.dma_start(spans[:], dram["spans"]).then_inc(S("spans_loaded"), 16)
            act.dma_start(lmask[:], dram["lmask"]).then_inc(S("spans_loaded"), 16)
            act.dma_start(wlr[:], dram["wlr"]).then_inc(S("wlr_loaded"), 16)
            linear("inlr", width=16)

            def level_decay(i):
                wait("gla_span", i + 1)
                if i >= 1:
                    wait("gla_qk", 2 * i)
                nc.scalar.activation(decay[:], span_banks[i % 2][:], ACT.Exp).then_inc(S("gla_exp"), 1)

            def behind_incols(c, known):
                if c == 2:
                    log_sigmoid(loga[:], za[:], zl[:], "lr_z", 1)
                elif c == 4:
                    nc.scalar.activation(aux[:], inT[:, 4:8, :].rearrange("p (a b) t -> p a b t", a=2),
                                         ACT.Sigmoid).then_inc(S("og_sig"), 1)
                elif c == 6:
                    wait("loga_ready", 1)
                    level_decay(0)

            def behind_mixing(stage):
                def post(c, known):
                    lv = LEVEL_OF.get((stage, c))
                    if lv is not None:
                        if lv + 1 < NL:
                            level_decay(lv + 1)
                        elif lv == NL:
                            level_decay(NL)
                    elif stage == "ingates" and c == VALUES_AT:
                        wait("gla_out", 1)
                        wait("og_silu", 1)
                        nc.scalar.activation(aux[:], score[:], ACT.Square).then_inc(S("gla_sq"), 1)
                        nc.scalar.activation(o_gla[:], score[:].rearrange("p a b t -> p (a b) t"),
                                             ACT.Copy).then_inc(S("gla_kept"), 1)
                        wait("gla_scores", NL + 2)
                        act.dma_start(toep[:], skewed).then_inc(S("toep_loaded"), 16)
                    elif stage == "ingates" and c == KT - 1:
                        wait("gla_var", 2)
                        inverse_root("gla_root", 0, tsum[:], aux[:])
                return post

            skewed = bass.AP(tensor=skew_dram.tensor, offset=P - 1,
                             ap=[[SKEW - 1, P], [P * SKEW, G_HEADS], [1, 3 * P]])
            linear("incols", post=behind_incols)
            linear("inrows", post=behind_mixing("inrows"))
            gate_chunk = linear("ingates", post=behind_mixing("ingates"), steps=True)
            for c in range(KT - 1):
                gate_chunk(c, c)

            def gla_hi():
                wait("gla_o", 1)
                nc.scalar.activation(hA[:, 0:4, 0:T], o_gla[:], ACT.Copy).then_inc(S("gla_hi"), 1)

            attention("moba", float(P) ** -0.5, prob2, probT2, lambda at, n: hA[:, 4 + at:4 + at + n, 0:T],
                      leads=[None, lambda: gate_chunk(KT - 1, KT - 1)], between={2: gla_hi})
            hi = hidden_hi("branch", hM)

            def branch(c, known):
                nc.scalar.activation(gates[:, c, :, :], gates[:, c, :, :], ACT.Sigmoid).then_inc(S("gate_ready"), 1)
                if known >= 1:
                    hi(c - 1, known - 1)

            linear("branch", post=branch, flush=lambda: hi(KT - 1, KT - 1))
            residual("out", "ffb", [hA], shift=6 * KT)
            gated_feed_forward("gu2")
            residual("dn2", "final2", [])

        @block.vector
        def _(dve):
            V = nc.vector

            def wait(sem, value):
                dve.wait_ge(S(sem), value)

            AHEAD = RING - 1

            def split_lo(st, c, known):
                n = st.base + known
                slot = n % RING
                wait("w_hi", c + (st.base + 1))
                e = elems_of(n)
                V.tensor_tensor(wsplit[:, slot, 1, 0:e], raw[:, slot, 0:e], wsplit[:, slot, 0, 0:e].bitcast(F32),
                                ALU.subtract).then_inc(S("w_lo"), 1)

            def total(st, a, known_a, dest=None, width=T):
                par = (st.acc_base + known_a) % 2
                wait("acc_low", a + (st.low_base + 1))
                dst = tsum[:, par, :, :] if dest is None else dest
                if st.name in DEFERRED:
                    t = tsum[:, par, :, :]
                    V.tensor_tensor(t, acc[:, par, :, 0:width], lowp[:, :, 0:width], ALU.add).then_inc(S("unscaled"), 1)
                    wait("unscaled", a + (scaled_base(st.name) + 1))
                    V.tensor_tensor(dst, t, spread(rstd[:], 2), ALU.mult).then_inc(S("acc_summed"), 1)
                    return
                V.tensor_tensor(dst, acc[:, par, :, 0:width], lowp[:, :, 0:width], ALU.add).then_inc(S("acc_summed"), 1)

            def linear(name, dest=None, before=None, early=None, post=None, flush=None, width=T, straight=False,
                       segments={}, steps=False, combine=None):
                st = STAGE[name]

                def body(c, known):
                    if before:
                        before(c, known)
                    last = known % st.per_acc == st.per_acc - 1
                    a, ka = (c, known) if st.per_acc == 1 else (known // st.per_acc, known // st.per_acc)
                    if last and combine:
                        combine(a, ka)
                    elif last:
                        if known == 0 and name in DEFERRED:
                            wait("norm_lo", norm_base(DEFERRED[name]) + PAIRS)
                        if dest is None or name in DEFERRED:
                            done = st.base + known + AHEAD
                            wait("w_lo", N_CHUNKS if done >= N_CHUNKS else c + (st.base + AHEAD))
                        total(st, a, ka, dest(a) if dest else None, width)
                        if early:
                            early(a, ka)
                    if st.base + known + AHEAD < N_CHUNKS:
                        split_lo(st, c + AHEAD, known + AHEAD)
                    if known in segments:
                        modulation(segments[known])
                    if last and post:
                        post(a, ka)

                if steps:
                    return body
                if st.per_acc == 1 and not straight:
                    groups(dve, st.chunks, body, lead=RING, tail=RING)
                else:
                    for c in range(st.chunks):
                        body(c, c)
                if flush:
                    flush()

            def operand_h(norm_name, p, src, gain):
                if p >= 2:
                    wait("norm_lo", norm_base(norm_name) + p - 1)
                for j in range(2):
                    kt = 2 * p + j
                    last = V.tensor_scalar(tsum[:, p % 2, j, :], src[:, kt, :], gain(kt), None, ALU.mult)
                last.then_inc(S("norm_h"), 1)

            def operand_lo(norm_name, p, dest):
                wait("norm_hi", norm_base(norm_name) + p + 1)
                V.tensor_tensor(dest[:, 2 * p:2 * p + 2, T:2 * T], tsum[:, p % 2, :, :],
                                dest[:, 2 * p:2 * p + 2, 0:T].bitcast(F32), ALU.subtract).then_inc(S("norm_lo"), 1)

            def add_to_x(name, gain=None, bias=None, segments={}, operand=None):
                st = STAGE[name]
                n = PAIRS * RESIDUALS.index(name)

                def add(a, ka, part, scalars, op):
                    par = (st.acc_base + ka) % 2
                    halves = acc[:, par, :, part * T:(part + 1) * T]
                    if scalars is None:
                        pair = x[:, 2 * a:2 * a + 2, :]
                        return V.tensor_tensor(pair, pair, halves, ALU.add)
                    for j in range(2):
                        kt = 2 * a + j
                        last = V.scalar_tensor_tensor(out=x[:, kt, :], in0=halves[:, j, :], scalar=scalars(kt),
                                                      in1=x[:, kt, :], op0=op, op1=ALU.add)
                    return last

                def combine(a, ka):
                    wait("chunk_done", (a + 1) * st.per_acc + st.base)
                    first = bias or gain
                    add(a, ka, 0, first, ALU.add if bias else ALU.mult).then_inc(S("x_half"), 1)
                    wait("x_half", n + a + 1)
                    add(a, ka, 1, gain, ALU.mult).then_inc(S("acc_summed"), 1)
                    if operand:
                        wait("acc_summed", st.acc_base + a + 1)
                        operand_h(operand[0], a, x, operand[2])

                linear(name, combine=combine, segments=segments,
                       before=lambda c, known: operand_lo(operand[0], c - 1, operand[1]) if operand and known >= 1 else None,
                       flush=lambda: operand_lo(operand[0], PAIRS - 1, operand[1]) if operand else None)
                if operand:
                    norm_scale(operand[0])

            def newton(sem, n, v, r, tmp):
                V.scalar_tensor_tensor(out=tmp, in0=r, scalar=-0.5, in1=r, op0=ALU.mult, op1=ALU.mult).then_inc(S(sem), 1)
                wait(sem, n + 1)
                V.tensor_tensor(tmp, tmp, v, ALU.mult).then_inc(S(sem), 1)
                wait(sem, n + 2)
                V.scalar_tensor_tensor(out=r, in0=tmp, scalar=1.5, in1=r, op0=ALU.add, op1=ALU.mult).then_inc(S(sem), 1)
                wait(sem, n + 3)

            def norm_scale(name):
                q = norm_index(name)
                wait("norm_root", 2 * q + 1)
                V.tensor_scalar(var[:], stat[:, 0, :], 1.0 / D, RMS_EPS, ALU.mult, ALU.add).then_inc(S("norm_var"), 1)
                wait("norm_var", q + 1)
                wait("norm_root", 2 * (q + 1))
                tmp = aux[:, 0, 0, :] if name in DEFERRED.values() else lowp[:, 0, :]
                newton("norm_rstd", 3 * q, var[:], rstd[:], tmp)

            def norm_apply(name, src, dest, gain, which=0, shift=None):
                nb = norm_base(name) + PAIRS * which

                def lo(p):
                    wait("norm_hi", nb + p + 1)
                    hi_ap = dest[:, 2 * p:2 * p + 2, 0:T].bitcast(F32)
                    if shift is None:
                        last = V.tensor_tensor(dest[:, 2 * p:2 * p + 2, T:2 * T], tsum[:, p % 2, :, :], hi_ap, ALU.subtract)
                    else:
                        for j in range(2):
                            kt = 2 * p + j
                            last = V.scalar_tensor_tensor(out=dest[:, kt, T:2 * T], in0=tsum[:, p % 2, j, :],
                                                          scalar=mod[:, shift + kt:shift + kt + 1],
                                                          in1=dest[:, kt, 0:T].bitcast(F32),
                                                          op0=ALU.add, op1=ALU.subtract)
                    last.then_inc(S("norm_lo"), 1)

                for p in range(PAIRS):
                    if which or p >= 2:
                        wait("norm_lo", nb + p - 1)
                    for j in range(2):
                        kt = 2 * p + j
                        last = V.scalar_tensor_tensor(out=tsum[:, p % 2, j, :], in0=src[:, kt, :], scalar=gain(kt),
                                                      in1=rstd[:], op0=ALU.mult, op1=ALU.mult)
                    last.then_inc(S("norm_h"), 1)
                    if p >= 1:
                        lo(p - 1)
                lo(PAIRS - 1)

            def norm(name, src, dests, shift=None):
                norm_scale(name)
                for i, (dest, gain) in enumerate(dests):
                    norm_apply(name, src, dest, gain, i, shift)

            def norm_in_place(name, sem):
                norm_scale(name)
                for p in range(PAIRS):
                    for j in range(2):
                        kt = 2 * p + j
                        last = V.scalar_tensor_tensor(out=x[:, kt, :], in0=x[:, kt, :],
                                                      scalar=col(name, kt),
                                                      in1=rstd[:], op0=ALU.mult, op1=ALU.mult)
                    last.then_inc(S(sem), 1)

            def lo_of(name, dest, pair):
                def lo(c, known):
                    wait(f"{name}_hi", c + 1)
                    par = (STAGE[name].acc_base + known) % 2
                    if pair:
                        d = hid[:].rearrange("p (c j) t -> p c j t", j=2)[:, c, :, :]
                        V.tensor_tensor(d[:, :, T:2 * T], tsum[:, par, :, :], d[:, :, 0:T].bitcast(F32),
                                        ALU.subtract).then_inc(S(f"{name}_lo"), 1)
                    else:
                        V.tensor_tensor(dest[:, c, T:2 * T], tsum[:, par, 0, :], dest[:, c, 0:T].bitcast(F32),
                                        ALU.subtract).then_inc(S(f"{name}_lo"), 1)
                return lo

            def feed_forward(up, down, segments):
                st = STAGE[up]
                lo = lo_of(up, hid, True)

                def square(c, known):
                    par = (st.acc_base + known) % 2
                    t = tsum[:, par, :, :]
                    wait("acc_summed", c + (st.acc_base + 1))
                    V.scalar_tensor_tensor(out=t, in0=t, scalar=0.0, in1=t, op0=ALU.max, op1=ALU.mult).then_inc(S(f"{up}_r"), 1)

                linear(up, early=lambda c, known: lo(c - 1, known - 1) if known >= 1 else None, post=square,
                       flush=lambda: lo(st.chunks - 1, st.chunks - 1))
                add_to_x(down, segments=segments)

            def gated_feed_forward(gu, dn, gain, segments={}):
                st = STAGE[gu]
                lo = lo_of(gu, hid, False)

                def gated(c, known):
                    par = (st.acc_base + known) % 2
                    t0, t1 = tsum[:, par, 0, :], tsum[:, par, 1, :]
                    wait(f"{gu}_sig", c + 1)
                    V.tensor_tensor(t0, t0, t1, ALU.mult).then_inc(S(f"{gu}_p"), 1)
                    wait(f"{gu}_p", c + 1)
                    V.tensor_tensor(t0, t0, aux[:, par, 0, :], ALU.mult).then_inc(S(f"{gu}_r"), 1)

                linear(gu, early=lambda c, known: lo(c - 1, known - 1) if known >= 1 else None, post=gated,
                       flush=lambda: lo(st.chunks - 1, st.chunks - 1))
                add_to_x(dn, gain, segments=segments)

            def plain(name, t, segments={}, steps=False):
                return linear(name, dest=lambda a: t[:].rearrange("p (c j) t -> p c j t", j=2)[:, a, :, :],
                              segments=segments, steps=steps)

            def rows(name, t, steps=False):
                return linear(name, dest=lambda a: t[:].rearrange("p r (c n) -> p r c n", n=T)[:, :, a, :],
                              steps=steps)

            def attention(name, scale, prob, dest, leads=(), between={}):
                _, n_heads, n_groups = next(a for a in ATTENTIONS if a[0] == name)
                b, gb = head_base(name)
                per_group = n_heads // n_groups
                tiles = 2 if name.startswith("mem") else 1

                def largest(h):
                    wait("att_scores", b + h + 1)
                    V.tensor_reduce(small[:, 0, 2 * h:2 * h + 2], score[:, h % 2, :, :], AX.X, ALU.max).then_inc(S("att_max"), 1)
                    wait("att_max", 2 * (b + h) + 1)
                    V.tensor_scalar(small[:, 1, 2 * h:2 * h + 2], small[:, 0, 2 * h:2 * h + 2], -scale, None,
                                    ALU.mult).then_inc(S("att_max"), 1)

                def normalise(h):
                    wait("att_exp", b + h + 1)
                    V.reciprocal(small[:, 3, 2 * h:2 * h + 2], small[:, 2, 2 * h:2 * h + 2]).then_inc(S("att_inv"), 1)
                    wait("att_inv", b + h + 1)
                    V.tensor_tensor(prob[:, h % 2, :, :], prob[:, h % 2, :, :],
                                    small[:, 3, 2 * h:2 * h + 2].unsqueeze(2).to_broadcast([P, TT, T]),
                                    ALU.mult).then_inc(S("att_prob"), 1)

                def out_lo(g):
                    wait("att_hi", gb + g + 1)
                    V.tensor_tensor(dest(1, g * tiles, tiles), stat[:, 0:tiles, :],
                                    dest(0, g * tiles, tiles).bitcast(F32), ALU.subtract).then_inc(S("att_lo"), 1)

                leads = list(leads) + [None] * 3
                for i in range(2):
                    if leads[i]:
                        leads[i]()
                    largest(i)
                normalise(0)
                if leads[2]:
                    leads[2]()
                for h in range(n_heads):
                    if h + 1 < n_heads:
                        normalise(h + 1)
                    if h + 2 < n_heads:
                        largest(h + 2)
                    if h in between:
                        between[h]()
                    if (h + 1) % per_group == 0:
                        out_lo(h // per_group)

            def in_hl(dest, first):
                return lambda part, at, n: dest[:, first + at:first + at + n, part * T:(part + 1) * T]

            def memory_attention(layer, queries, prob, dest):
                chunk = plain(f"memq{layer}", queries, steps=True)
                attention(f"mem{layer}", 1 / 16, prob, in_hl(dest, 0),
                          leads=[lambda: (chunk(0, 0), chunk(1, 1)), lambda: chunk(2, 2), lambda: chunk(3, 3)])

            def modulation(seg):
                wait("ada_used", seg + 1)
                V.tensor_tensor(mod[:, SEGMENT * seg:SEGMENT * (seg + 1)], turned[:, 0, 0:SEGMENT],
                                col("ada_b", SEGMENT * seg, SEGMENT), ALU.add).then_inc(S("mod_made"), 1)

            V.memset(upad[:, :, 0:PAD], 0.0).then_inc(S("pad_ready"), 1)
            wait("cols_loaded", 16)
            wait("x_loaded", 16)
            for p in range(PAIRS):
                operand_h("mix0", p, x, lambda kt: col("mix0", kt))
                if p >= 1:
                    operand_lo("mix0", p - 1, hA)
            operand_lo("mix0", PAIRS - 1, hA)
            for n in range(2):
                split_lo(PLAN[0], n, n)
            norm_scale("mix0")
            for n in range(2, AHEAD):
                split_lo(PLAN[0], n, n)
            wait("consts_loaded", 16 * 5)

            taps_done = {kt: 0 for kt in V_TILES}
            latest = {}
            at_step = [0]

            def conv_taps(n, made):
                for i in range(n):
                    begun = [kt for kt in V_TILES if kt < made and taps_done[kt] < TAPS][:2]
                    if not begun:
                        return
                    kt = begun[i % len(begun)]
                    tap = taps_done[kt]
                    w = taps[:, tap, kt:kt + 1]
                    u = upad[:, kt, tap:tap + T]
                    if tap == 0:
                        wait("u_ready", kt + 1)
                        ins = V.tensor_scalar(conv[:, kt, :], u, w, col("dw_b", kt), ALU.mult, ALU.add)
                    else:
                        wait("conv_step", latest[kt])
                        ins = V.scalar_tensor_tensor(out=conv[:, kt, :], in0=u, scalar=w, in1=conv[:, kt, :],
                                                     op0=ALU.mult, op1=ALU.add)
                    taps_done[kt] = tap + 1
                    if tap == TAPS - 1:
                        ins.then_inc(S("conv_tile"), 1)
                    else:
                        ins.then_inc(S("conv_step"), 1)
                        at_step[0] += 1
                        latest[kt] = at_step[0]

            def glu(a, ka):
                wait("pw1_sig", a + 1)
                u = upad[:, a, PAD:PAD + T]
                V.scalar_tensor_tensor(out=u, in0=tsum[:, ka % 2, 0, :], scalar=col("pw1_b", a), in1=u,
                                       op0=ALU.add, op1=ALU.mult).then_inc(S("u_ready"), 1)
                conv_taps(9 if a < KT - 1 else 0, a + 1)

            wait("pad_ready", 1)
            linear("pw1", post=glu, straight=True)
            norm("mem0", memx0, [(hM, lambda kt: col("src0", kt))])
            conv_taps(24, KT)
            linear("memk0", dest=lambda a: mk0[:, 2 * a:2 * a + 2, :], post=lambda a, ka: conv_taps(12, KT), straight=True)
            linear("memv0", dest=lambda a: mv0[:, :, a * T:(a + 1) * T], post=lambda a, ka: conv_taps(12, KT), straight=True)
            conv_taps(len(V_TILES) * TAPS, KT)
            wait("conv_tile", len(V_TILES))
            wait("conv_pool_step", len(G_TILES) * (2 * TAPS - 1))
            wait("ln_stat", 1)
            V.tensor_scalar(mu[:], stat[:, 0, :], 1.0 / D, None, ALU.mult).then_inc(S("ln_mean"), 1)
            wait("ln_mean", 1)
            for p in range(PAIRS):
                c2 = conv[:, 2 * p:2 * p + 2, :]
                V.tensor_tensor(c2, c2, spread(mu[:], 2), ALU.subtract).then_inc(S("ln_centred"), 1)
            wait("ln_root", 1)
            V.tensor_scalar(var[:], stat[:, 0, :], 1.0 / D, LN_EPS, ALU.mult, ALU.add).then_inc(S("ln_var"), 1)
            wait("ln_var", 1)
            wait("ln_root", 2)
            wait("ln_centred", PAIRS)
            newton("ln_rstd", 0, var[:], rstd[:], mu[:])

            def ln_lo(p):
                wait("ln_hi", p + 1)
                V.tensor_tensor(hM[:, 2 * p:2 * p + 2, T:2 * T], tsum[:, p % 2, :, :],
                                hM[:, 2 * p:2 * p + 2, 0:T].bitcast(F32), ALU.subtract).then_inc(S("ln_lo"), 1)

            for p in range(PAIRS):
                c2 = conv[:, 2 * p:2 * p + 2, :]
                V.tensor_tensor(c2, c2, spread(rstd[:], 2), ALU.mult).then_inc(S("ln_y"), 1)
            for p in range(PAIRS):
                wait("ln_sig", p + 1)
                V.tensor_tensor(tsum[:, p % 2, :, :], tsum[:, p % 2, :, :], aux[:, p % 2, :, :],
                                ALU.mult).then_inc(S("ln_r"), 1)
                if p >= 1:
                    ln_lo(p - 1)
            ln_lo(PAIRS - 1)
            add_to_x("pw2", bias=lambda kt: col("pw2_b", kt), operand=("memq0", hA, lambda kt: col("memq0", kt)))
            memory_attention(0, mq0, prob0, hM)
            add_to_x("memo0", segments={0: 0}, operand=("ff0", hA, lambda kt: col("ff0", kt)))
            feed_forward("up0", "down0", {0: 1, 12: 2})

            norm("fox", x, [(hA, lambda kt: col("kv", kt)), (hB, lambda kt: col("mix1", kt))])
            plain("foxk", fk)
            rows("foxv", fv)
            linear("foxf", dest=lambda a: small[:, 0, :].rearrange("p (r n) -> p r n", r=TT), width=HEADS)
            wait("acc_summed", STAGE["foxf"].acc_base + 1)
            z = small[:, 0, :].rearrange("p (r n) -> p r n", r=TT)
            V.tensor_tensor(z, z, spread(col("fgate", 0, HEADS), TT), ALU.add).then_inc(S("fgate_z"), 1)
            norm("mem1", memx1, [(hA, lambda kt: col("src1", kt))])
            wait("fgate_z_ln", 3)
            V.scalar_tensor_tensor(out=small[:, 3, :], in0=small[:, 0, :], scalar=0.0, in1=small[:, 1, :],
                                   op0=ALU.min, op1=ALU.subtract).then_inc(S("logf_ready"), 1)
            plain("foxq", fq, {0: 3})
            V.memset(ones_bf[:], 1.0)
            wait("negc_made", 1)
            V.tensor_copy(negc_part[0:HEADS, 0, :], turned[0:HEADS, 0, :]).then_inc(S("negc_ready"), 1)
            wait("negc_ready", 1)
            V.tensor_tensor(negc[0:HEADS, :], turned[0:HEADS, 0, :], negc_part[0:HEADS, 0, :],
                            ALU.subtract).then_inc(S("negc_rest"), 1)
            wait("negc_rest", 1)
            V.tensor_copy(negc_part[0:HEADS, 1, :], negc[0:HEADS, :]).then_inc(S("negc_ready"), 1)
            wait("negc_ready", 2)
            V.tensor_tensor(negc_part[0:HEADS, 2, :], negc[0:HEADS, :], negc_part[0:HEADS, 1, :],
                            ALU.subtract).then_inc(S("negc_ready"), 1)
            memory_keys, memory_values = plain("memk1", mk1, steps=True), rows("memv1", mv1, steps=True)
            attention("fox", 1 / 8, prob1, lambda part, at, n: fo[:, part, at:at + n, :],
                      leads=[lambda: memory_keys(0, 0)], between=memory_between(memory_keys, memory_values))
            add_to_x("foxo", segments={0: 4}, operand=("memq1", hA, lambda kt: col("memq1", kt)))
            memory_attention(1, mq1, prob1, hB)
            add_to_x("memo1", segments={0: 5}, operand=("ff1", hA, lambda kt: col("ff1", kt)))
            feed_forward("up1", "down1", {0: 6, 12: 7})
            norm_in_place("final1", "x_normed")

            def modulation_parts(parts):
                wait("mod_made", max(seg for seg, _ in parts) + 1)
                for seg, gain in parts:
                    m = mod[:, SEGMENT * seg:SEGMENT * (seg + 1)]
                    if gain:
                        V.scalar_tensor_tensor(out=m, in0=m, scalar=1.0, in1=col(gain, 0, KT), op0=ALU.add,
                                               op1=ALU.mult).then_inc(S("mod_used"), 1)
                    else:
                        V.tensor_scalar(m, m, 0.5, None, ALU.mult).then_inc(S("mod_used"), 1)

            def modulated(seg):
                return lambda kt: mod[:, SEGMENT * seg + kt:SEGMENT * seg + kt + 1]

            modulation_parts([(1, "ffa"), (2, None), (4, "mixn")])
            wait("mod_used", 3)
            norm("ffa", x, [(hA, modulated(1))], shift=0)
            gated_feed_forward("gu1", "dn1", modulated(2), {0: 8})
            modulation_parts([(7, "ffb"), (8, None)])
            wait("mod_used", 5)
            norm("mixn", x, [(hA, modulated(4))], shift=3 * SEGMENT)
            V.memset(glrT[:], 1.0).then_inc(S("lr_turned"), 1)
            linear("inlr", dest=lambda a: small[:, 0, :].rearrange("p (r n) -> p r n", r=TT), width=16)

            def behind_incols(c, known):
                if c == 0:
                    wait("lr_turn", 1)
                    wait("lr_turned", 1)
                    V.tensor_copy(glrT[0:16, :], turned[0:16, 0, :]).then_inc(S("lr_turned"), 1)
                elif c == 1:
                    wait("lr_logits", 1)
                    V.tensor_copy(loga[:], turned[:]).then_inc(S("lr_z"), 1)
                elif c == 3:
                    wait("lr_z_ln", 3)
                    V.scalar_tensor_tensor(out=loga[:], in0=loga[:], scalar=0.0, in1=za[:],
                                           op0=ALU.min, op1=ALU.subtract).then_inc(S("loga_ready"), 1)
                elif c == 5:
                    wait("og_sig", 1)
                    og = inT[:, 4:8, :].rearrange("p (a b) t -> p a b t", a=2)
                    V.tensor_tensor(og, og, aux[:], ALU.mult).then_inc(S("og_silu"), 1)

            flat = tsum[:].rearrange("p a b t -> p (a b t)")
            product = flat.rearrange("p (n t) -> p n t", t=P)

            def level_mask(lv):
                wait("gla_scores", lv + 1)
                if lv == NL + 1:
                    V.tensor_scalar(A_next[:].rearrange("p (b h) t -> p b h t", b=2),
                                    A_ps.rearrange("p (b h) t -> p b h t", b=2)[:, :, 0:2, :],
                                    1 / 8, None, ALU.mult).then_inc(S("gla_masked"), 1)
                    return
                m = spread(lmask[:, lv, :], 2 * G_HEADS)
                if lv == 0:
                    V.tensor_tensor(A_same[:], A_ps, m, ALU.mult).then_inc(S("gla_masked"), 1)
                    return
                wait("gla_masked", 2 * lv - 1)
                V.tensor_tensor(product, A_ps, m, ALU.mult).then_inc(S("gla_masked"), 1)
                wait("gla_masked", 2 * lv)
                V.tensor_tensor(A_same[:], A_same[:], product, ALU.add).then_inc(S("gla_masked"), 1)

            def behind_mixing(stage):
                def post(c, known):
                    lv = LEVEL_OF.get((stage, c))
                    if lv is not None:
                        level_mask(lv)
                return post

            def gla_variance(c, known):
                if c == KT - 1:
                    wait("gla_stat", 1)
                    wait("gla_masked", 2 * NL + 2)
                    for i in range(2):
                        V.tensor_scalar(tsum[:, i, :, :], span_banks[i][:], 1.0 / P, RMS_EPS, ALU.mult,
                                        ALU.add).then_inc(S("gla_var"), 1)

            linear("incols", dest=lambda a: inT[:, 2 * a:2 * a + 2, :], post=behind_incols, straight=True)
            linear("inrows", dest=lambda a: inV[:].rearrange("p r (c n) -> p r c n", n=T)[:, :, a, :],
                   post=behind_mixing("inrows"), straight=True)
            gate_chunk = linear("ingates", dest=lambda a: gates[:, a, :, :], before=gla_variance,
                                post=behind_mixing("ingates"), steps=True)
            for c in range(KT - 1):
                gate_chunk(c, c)
            auxf = aux[:].rearrange("p a b t -> p (a b t)")
            of = o_gla[:].rearrange("p a t -> p (a t)")

            def gla_newton():
                wait("gla_var", 2)
                wait("gla_root", 2)
                newton("gla_rstd", 0, flat, auxf, inT[:, 0:4, :].rearrange("p a t -> p (a t)"))

            def gla_gate():
                wait("gla_kept", 1)
                V.tensor_tensor(of, of, auxf, ALU.mult).then_inc(S("gla_norm"), 1)
                wait("gla_norm", 1)
                V.scalar_tensor_tensor(out=of, in0=of, scalar=col("gla"), in1=inT[:, 4:8, :].rearrange("p a t -> p (a t)"),
                                       op0=ALU.mult, op1=ALU.mult).then_inc(S("gla_o"), 1)

            def gla_lo():
                wait("gla_hi", 1)
                V.tensor_tensor(hA[:, 0:4, T:2 * T], o_gla[:], hA[:, 0:4, 0:T].bitcast(F32), ALU.subtract).then_inc(S("gla_lo"), 1)

            attention("moba", float(P) ** -0.5, prob2, in_hl(hA, 4),
                      leads=[None, lambda: gate_chunk(KT - 1, KT - 1)], between={0: gla_newton, 1: gla_gate, 2: gla_lo})
            lo = lo_of("branch", hM, False)

            def merge(c, known):
                par = (STAGE["branch"].acc_base + known) % 2
                t = tsum[:, par, :, :]
                wait("acc_summed", c + (STAGE["branch"].acc_base + 1))
                wait("gate_ready", c + 1)
                V.tensor_tensor(t, t, gates[:, c, :, :], ALU.mult).then_inc(S("branch_p"), 1)
                wait("branch_p", c + 1)
                V.tensor_tensor(t[:, 0, :], t[:, 0, :], t[:, 1, :], ALU.add).then_inc(S("branch_r"), 1)

            linear("branch", early=lambda c, known: lo(c - 1, known - 1) if known >= 1 else None, post=merge,
                   flush=lambda: lo(KT - 1, KT - 1))
            add_to_x("out", modulated(5))
            norm("ffb", x, [(hA, modulated(7))], shift=6 * SEGMENT)
            gated_feed_forward("gu2", "dn2", modulated(8))
            norm_in_place("final2", "final_ready")

        @block.gpsimd
        def _(pool):
            G = nc.gpsimd

            def wait(sem, value):
                pool.wait_ge(S(sem), value)

            HALF_STEPS = 4

            def ada_load(m, half):
                pool.dma_start(ada_w[:, half, :, :], dram["ada"][m, half]).then_inc(ada_loaded[half], 16)

            def ada_tile(m, known, last):
                for half in range(2):
                    pool.wait_ge(ada_loaded[half], m * 16 + 16)
                    w = ada_w[:, half, :, :]
                    n = m * (2 * HALF_STEPS) + HALF_STEPS * half
                    G.tensor_tensor(w, w, cact[:].unsqueeze(2).to_broadcast([P, KT, HALF]), ALU.mult).then_inc(S("ada_step"), 1)
                    wait("ada_step", n + 1)
                    G.tensor_tensor(w[:, 0:4, :], w[:, 0:4, :], w[:, 4:8, :], ALU.add).then_inc(S("ada_step"), 1)
                    wait("ada_step", n + 2)
                    G.tensor_tensor(w[:, 0:2, :], w[:, 0:2, :], w[:, 2:4, :], ALU.add).then_inc(S("ada_step"), 1)
                    wait("ada_step", n + 3)
                    G.tensor_tensor(ada_acc[:, known % SEGMENT, half * HALF:(half + 1) * HALF], w[:, 0, :], w[:, 1, :],
                                    ALU.add).then_inc(S("ada_step"), 1)
                    if not last:
                        wait("ada_step", n + 4)
                        ada_load(m + 1, half)

            def ada_segment(seg, known, last=False):
                if known:
                    wait("ada_used", seg)
                for k in range(SEGMENT):
                    ada_tile(seg * SEGMENT + k, k, last and k == SEGMENT - 1)

            ada_load(0, 0)
            ada_load(0, 1)
            wait("cols_loaded", 16)
            wait("consts_loaded", 16 * 5)
            n = 0
            for kt in G_TILES:
                wait("u_ready", kt + 1)
                for tap in range(TAPS):
                    w = taps[:, tap, kt:kt + 1]
                    u = upad[:, kt, tap:tap + T]
                    if tap == 0:
                        G.tensor_scalar(conv[:, kt, :], u, w, col("dw_b", kt), ALU.mult, ALU.add).then_inc(S("conv_pool_step"), 1)
                        n += 1
                        continue
                    wait("conv_pool_step", n)
                    G.tensor_scalar(pool_tmp[:], u, w, 0.0, ALU.mult, ALU.add).then_inc(S("conv_pool_step"), 1)
                    wait("conv_pool_step", n + 1)
                    G.tensor_tensor(conv[:, kt, :], conv[:, kt, :], pool_tmp[:], ALU.add).then_inc(S("conv_pool_step"), 1)
                    n += 2
            wait("cond_sig", 1)
            G.tensor_tensor(cact[:], cact[:], col("cond", 0, KT), ALU.mult).then_inc(S("cond_silu"), 1)
            wait("cond_silu", 1)
            ada_segment(0, 0)
            with pool.Fori(1, N_MOD - 1) as seg:
                ada_segment(seg, 1)
            ada_segment(N_MOD - 1, N_MOD - 1, True)
            for i in range(NL + 1):
                wait("gla_exp", i + 1)
                if i:
                    wait("gla_scores", i)
                G.tensor_tensor(qe[:], inT[:, 0:2, :], decay[:], ALU.mult).then_inc(S("gla_qk"), 1)
                G.tensor_tensor(ke[:], inT[:, 2:4, :], decay[:], ALU.mult).then_inc(S("gla_qk"), 1)


def bucket_of(dist):
    exact, far = BUCKETS // 2, 128
    if dist < exact:
        return dist
    return min(BUCKETS - 1, exact + int(np.log(dist / exact) / np.log(far / exact) * (BUCKETS - exact)))


def constants():
    i = np.arange(P)
    before = (i[:, None] <= i[None, :]).astype(np.float32)
    tri = np.zeros((P, TT, T), np.float32)
    tri[:, 0, :P], tri[:, 0, P:], tri[:, 1, P:] = before, 1, before
    spans = np.zeros((P, NL + 2, P), np.float32)
    lmask = np.zeros((P, NL + 1, P), np.float32)
    t, j = i[:, None], i[None, :]
    for lv, s in enumerate(LEVELS):
        mid = j // (2 * s) * (2 * s) + s - 1
        spans[:, lv, :] = ((t > j) & (t <= mid)) | ((t > mid) & (t <= j))
        lmask[:, lv, :] = (t // (2 * s) == j // (2 * s)) & (t % (2 * s) < s) & (j % (2 * s) >= s)
    spans[:, NL, :] = t > j
    spans[:, NL + 1, :] = t <= j
    lmask[:, NL, :] = t == j
    onehot = np.zeros((BUCKETS + 1, SKEW), np.float32)
    for c in range(SKEW):
        if c < T:
            onehot[bucket_of(T - 1 - c), c] = 1
        else:
            onehot[BUCKETS, c] = MASKED
    mask = np.full((P, 2 * P), MASKED, np.float32)
    mask[:, :P][i[:, None] >= i[None, :]] = 0
    return {
        "ones": np.ones((P, P), np.float32), "ident": np.eye(P, dtype=np.float32), "mask": mask,
        "tri": -8 * tri, "spans": spans / 16, "lmask": lmask / 8, "onehot": onehot,
    }


def tiles(w, k_tiles, columns):
    w3 = w.reshape(-1, P, w.shape[1])
    return np.stack([w3[kt][:, :, cs].transpose(1, 0, 2).reshape(P, -1) for kt, cs in zip(k_tiles, columns)])


def by_columns(w, width=256):
    n = w.shape[1] // width
    return tiles(w, [slice(None)] * n, [slice(c * width, (c + 1) * width) for c in range(n)])


def paired(w, step, n):
    return tiles(w, [slice(None)] * n, [np.r_[c * P:(c + 1) * P, (step + c) * P:(step + c + 1) * P] for c in range(n)])


def layout(a):
    def rows(v):
        return v.reshape(-1, P).T

    out = {}
    out["xT"] = a["x"][0].T.reshape(KT, P, T).transpose(1, 0, 2)
    out["memT"] = a["mem"][0].T.reshape(KT, P, T).transpose(1, 0, 2)
    vectors = {
        "mix0": a["norm_mix_g"][0], "mix1": a["norm_mix_g"][1], "memq0": a["norm_mem_g"][0],
        "memq1": a["norm_mem_g"][1], "src0": a["norm_memsrc_g"][0], "src1": a["norm_memsrc_g"][1],
        "ff0": a["norm_ff_g"][0], "ff1": a["norm_ff_g"][1], "pw1_b": a["conv_pw1_b"][0],
        "dw_b": a["conv_dw_b"][0], "ln_g": a["conv_ln_g"][0], "ln_b": a["conv_ln_b"][0],
        "pw2_b": a["conv_pw2_b"][0], "kv": a["kv_norm_g"], "final1": a["final_norm_g"],
        "ffa": a["norm_ff1_2"][0], "mixn": a["norm_mix_2"][0], "ffb": a["norm_ff2_2"][0],
        "final2": a["norm_final_2"], "gla": a["gla_norm_2"][0], "ada_b": a["b_ada_2"][0], "cond": a["c_2"][0],
    }
    spread_rows = {"fgate": a["fgate_b"], "rms_eps": np.float32([RMS_EPS]), "ln_eps": np.float32([LN_EPS])}
    packed = [rows(vectors[name]) if name in vectors else np.broadcast_to(spread_rows[name], (P, n))
              for name, n in COLUMNS]
    out["cols"] = np.concatenate(packed, axis=1)
    out["taps"] = a["conv_dw_w"][0].reshape(TAPS, KT, P).transpose(2, 0, 1)
    out["relT"] = np.concatenate([a["rel_bias_2"].T, np.ones((1, G_HEADS), np.float32)])
    out["wlr"] = np.concatenate([a["w_gla_lr_2"][0], a["b_gla_lr_2"][0][None]])
    out["ada"] = a["w_ada_2"][0].reshape(KT, P, N_MOD * KT, 2, HALF).transpose(2, 3, 1, 0, 4)

    out["pw1"] = paired(a["conv_pw1_w"][0], KT, KT)
    out["pw2"] = by_columns(a["conv_pw2_w"][0])
    for layer in range(2):
        for s in "qkvo":
            out[f"mem{s}{layer}"] = by_columns(a[f"mem_w{s}"][layer])
        out[f"up{layer}"] = by_columns(a["ff_w1"][layer])
        out[f"down{layer}"] = tiles(a["ff_w2"][layer], [slice(q * KT, (q + 1) * KT) for _ in range(4) for q in range(4)],
                                    [slice(c * 256, (c + 1) * 256) for c in range(4) for _ in range(4)])
    kvf = a["kvf_w"]
    out["foxk"], out["foxv"], out["foxf"] = by_columns(kvf[:, :D]), by_columns(kvf[:, D:2 * D]), by_columns(kvf[:, 2 * D:], HEADS)
    out["foxq"], out["foxo"] = by_columns(a["fox_wq"][0]), by_columns(a["fox_wo"][0])
    for i in (1, 2):
        gu = np.concatenate([a[f"w_ff{i}_gate_2"][0], a[f"w_ff{i}_up_2"][0]], axis=1)
        out[f"gu{i}"] = paired(gu, KF2, KF2)
        out[f"dn{i}"] = tiles(a[f"w_ff{i}_down_2"][0], [slice(11 * (q % 2), 11 * (q % 2) + 11) for _ in range(4) for q in range(4)],
                              [slice(m * P, (m + 1) * P) for c in range(4) for m in (2 * c, 2 * c, 2 * c + 1, 2 * c + 1)])
    w = a["w_in_2"][0]
    sizes = [256, 256, 512, 16, 512, 512, 512, 512, D, D]
    gq, gk, gv, glr, gog, mq, mk, mv, ga, gb = np.split(w, np.cumsum(sizes)[:-1], axis=1)
    out["incols"] = by_columns(np.concatenate([gq, gk, gog, mq, mk], axis=1))
    out["inrows"] = by_columns(np.concatenate([gv, mv], axis=1))
    out["inlr"] = by_columns(glr, 16)
    out["ingates"] = paired(np.concatenate([ga, gb], axis=1), KT, KT)
    out["branch"] = by_columns(np.concatenate([a["w_br_gla_2"][0], a["w_br_moba_2"][0]]), P)
    out["out"] = by_columns(a["w_out_2"][0])
    out.update(constants())
    return out


def kernel(**inputs):
    import concourse.bacc as bacc
    import ml_dtypes
    from concourse.bass_utils import run_bass_kernel_spmd

    nc = bacc.Bacc("TRN2", target_bir_lowering=False, num_devices=1)
    arrays = {k: np.ascontiguousarray(v) for k, v in layout({k: np.asarray(v) for k, v in inputs.items()}).items()}
    arrays["mask"] = arrays["mask"].astype(ml_dtypes.bfloat16)
    dram = {}
    for name, v in arrays.items():
        dram[name] = nc.dram_tensor(f"in_{name}", v.shape, mybir.dt.from_np(v.dtype), kind="ExternalInput").ap()
    out = nc.dram_tensor("out_xT", (P, KT, T), F32, kind="ExternalOutput").ap()
    program(nc, dram, out)
    r = run_bass_kernel_spmd(nc, [{f"in_{k}": v for k, v in arrays.items()}], core_ids=[0])
    got = np.asarray(r.results[0]["out_xT"])
    return np.ascontiguousarray(got.transpose(1, 0, 2).reshape(D, T).T)[None]
```
